# Optimizing a Trainium2 kernel written in Bass

```python
import jax, jax.numpy as jnp
from jax import lax
import numpy as np

D_MODEL = 2048
BATCH = 1
SEQ = 256
DEPTH = 2

CTX_LEN = 256
GRID_W = 64
EPS = 1e-6

HEAD_DIM = 128
ATTN_W = 3 * D_MODEL // 4
N_Q_HEADS = ATTN_W // HEAD_DIM
N_KV_HEADS = 4
Q_GROUP = N_Q_HEADS // N_KV_HEADS
KV_W = N_KV_HEADS * HEAD_DIM
ROPE_THETA = 10000.0
Q_BLOCK = 128

POOL_WINDOWS = (2, 4, 8, 16)
POOL_W = D_MODEL // 4
POOL_GROUP = POOL_W // len(POOL_WINDOWS)

EVEN_IN = ATTN_W + 2 * KV_W + POOL_W
EVEN_MIX = ATTN_W + POOL_W

FFT_W = D_MODEL // 2
N_FFT_GROUPS = 4
FFT_GROUP = FFT_W // N_FFT_GROUPS

CONV_W = D_MODEL // 2
CONV_WIDTH = 3

ODD_IN = FFT_W + 3 * CONV_W
ODD_MIX = FFT_W + CONV_W

D_FF = -(-8 * D_MODEL // (3 * 256)) * 256
N_EVEN = (DEPTH + 1) // 2
N_ODD = DEPTH // 2

kernel_name = 'hybrid_attn_pool_fourier_conv_dit'

def rmsnorm(x, g):
    xf = x.astype(jnp.float32)
    y = xf * lax.rsqrt(jnp.mean(xf * xf, axis=-1, keepdims=True) + EPS)
    return (y * g.astype(jnp.float32)).astype(x.dtype)

def adaln(cvec, w, bias):
    return jnp.split(jax.nn.silu(cvec) @ w + bias, 6, axis=-1)

def modulate(h, shift, scale):
    return h * (1 + scale) + shift

def rope_tables(n):
    n_rows = n // GRID_W
    row = jnp.repeat(jnp.arange(n_rows, dtype=jnp.float32), GRID_W)
    col = jnp.tile(jnp.arange(GRID_W, dtype=jnp.float32), n_rows)
    quarter = HEAD_DIM // 4
    freqs = ROPE_THETA ** (-jnp.arange(quarter, dtype=jnp.float32) / quarter)
    ang = jnp.stack([row[:, None] * freqs, col[:, None] * freqs], axis=1)
    return jnp.cos(ang), jnp.sin(ang)

def apply_rope(x, cos, sin):
    b, n, h, d = x.shape
    xr = x.reshape(b, n, h, 2, 2, d // 4)
    cs = cos.astype(x.dtype)[None, :, None]
    sn = sin.astype(x.dtype)[None, :, None]
    x1, x2 = xr[..., 0, :], xr[..., 1, :]
    out = jnp.stack([x1 * cs - x2 * sn, x1 * sn + x2 * cs], axis=-2)
    return out.reshape(b, n, h, d)

def block_attention(q, k, v):
    b, nq = q.shape[:2]
    nb = nq // Q_BLOCK
    qb = q.reshape(b, nb, Q_BLOCK, N_KV_HEADS, Q_GROUP, HEAD_DIM).transpose(1, 0, 2, 3, 4, 5)
    scale = HEAD_DIM ** -0.5

    def one_block(qblk):
        s = jnp.einsum('bqhgd,bkhd->bhgqk', qblk, k).astype(jnp.float32) * scale
        p = jax.nn.softmax(s, axis=-1).astype(v.dtype)
        return jnp.einsum('bhgqk,bkhd->bqhgd', p, v)

    o = lax.map(one_block, qb)
    return o.transpose(1, 0, 2, 3, 4, 5).reshape(b, nq, ATTN_W)

def pool_mixer(u, w_pool, pool_scale):
    b, n, _ = u.shape
    uf = u.astype(jnp.float32)
    cs = jnp.concatenate([jnp.zeros((b, 1, POOL_W), jnp.float32), jnp.cumsum(uf, axis=1)], axis=1)
    t = jnp.arange(n)
    outs = []
    for g, w in enumerate(POOL_WINDOWS):
        sl = slice(g * POOL_GROUP, (g + 1) * POOL_GROUP)
        lo = jnp.clip(t - w // 2, 0, n)
        hi = jnp.clip(t - w // 2 + w, 0, n)
        mean = (cs[:, hi, sl] - cs[:, lo, sl]) / (hi - lo).astype(jnp.float32)[None, :, None]
        outs.append(mean - uf[..., sl])
    pooled = jnp.stack(outs, axis=2).astype(u.dtype)
    y = jnp.einsum('bngc,gcd->bngd', pooled, w_pool).reshape(b, n, POOL_W)
    return y * pool_scale

def attn_pool_mixer(h, hc, w_in, q_g, k_g, w_pool, pool_scale, cos, sin, ctx_full):
    b, n, _ = h.shape
    q, k, v, u = jnp.split(h @ w_in, [ATTN_W, ATTN_W + KV_W, ATTN_W + 2 * KV_W], axis=-1)
    q = apply_rope(rmsnorm(q.reshape(b, n, N_Q_HEADS, HEAD_DIM), q_g), cos, sin)
    k = apply_rope(rmsnorm(k.reshape(b, n, N_KV_HEADS, HEAD_DIM), k_g), cos, sin)
    v = v.reshape(b, n, N_KV_HEADS, HEAD_DIM)
    lc = hc.shape[1]
    if ctx_full:
        qc, kc, vc, uc = jnp.split(hc @ w_in, [ATTN_W, ATTN_W + KV_W, ATTN_W + 2 * KV_W], axis=-1)
    else:
        kc, vc = jnp.split(hc @ w_in[:, ATTN_W:ATTN_W + 2 * KV_W], 2, axis=-1)
    kc = rmsnorm(kc.reshape(b, lc, N_KV_HEADS, HEAD_DIM), k_g)
    vc = vc.reshape(b, lc, N_KV_HEADS, HEAD_DIM)
    k_all = jnp.concatenate([kc, k], axis=1)
    v_all = jnp.concatenate([vc, v], axis=1)
    out = jnp.concatenate([block_attention(q, k_all, v_all), pool_mixer(u, w_pool, pool_scale)], axis=-1)
    out_c = None
    if ctx_full:
        qc = rmsnorm(qc.reshape(b, lc, N_Q_HEADS, HEAD_DIM), q_g)
        out_c = jnp.concatenate([block_attention(qc, kc, vc), pool_mixer(uc, w_pool, pool_scale)], axis=-1)
    return out, out_c

def fourier_mixer(f):
    b, n, _ = f.shape
    fg = f.reshape(b, n, N_FFT_GROUPS, FFT_GROUP).astype(jnp.float32)
    y = jnp.fft.fft2(fg, axes=(1, 3), norm='ortho').real
    return y.reshape(b, n, FFT_W).astype(f.dtype)

def short_conv_mixer(bg, cg, xin, conv_w):
    n = xin.shape[1]
    pad = CONV_WIDTH // 2
    u = jnp.pad(cg * xin, ((0, 0), (pad, CONV_WIDTH - 1 - pad), (0, 0)))
    y = sum(u[:, j:j + n] * conv_w[j] for j in range(CONV_WIDTH))
    return bg * y

def fourier_conv_mixer(h, w_in, conv_w):
    f, bg, cg, xin = jnp.split(h @ w_in, [FFT_W, FFT_W + CONV_W, FFT_W + 2 * CONV_W], axis=-1)
    return jnp.concatenate([fourier_mixer(f), short_conv_mixer(bg, cg, xin, conv_w)], axis=-1)

def swiglu(h, wg, wu, wd):
    return (jax.nn.silu(h @ wg) * (h @ wu)) @ wd

def setup_inputs(seed: int = 0) -> dict:
    key = jax.random.key(seed)
    ks = jax.random.split(key, 24)
    nrm = jax.random.normal
    f32 = jnp.float32
    return {
        'x': nrm(ks[0], (BATCH, SEQ, D_MODEL), f32),
        'c': nrm(ks[1], (BATCH, D_MODEL), f32),
        'ctx': nrm(ks[2], (BATCH, CTX_LEN, D_MODEL), f32),
        'c_ctx': nrm(ks[3], (D_MODEL,), f32),
        'norm_g': 1.0 + 0.02 * nrm(ks[4], (DEPTH, 2, D_MODEL), f32),
        'w_mod': nrm(ks[5], (DEPTH, D_MODEL, 6 * D_MODEL), f32) * (0.5 * D_MODEL ** -0.5),
        'b_mod': 0.02 * nrm(ks[6], (DEPTH, 6 * D_MODEL), f32),
        'w_in_even': nrm(ks[7], (N_EVEN, D_MODEL, EVEN_IN), f32) * D_MODEL ** -0.5,
        'w_out_even': nrm(ks[8], (N_EVEN, EVEN_MIX, D_MODEL), f32) * EVEN_MIX ** -0.5,
        'q_norm_g': 1.0 + 0.02 * nrm(ks[9], (N_EVEN, HEAD_DIM), f32),
        'k_norm_g': 1.0 + 0.02 * nrm(ks[10], (N_EVEN, HEAD_DIM), f32),
        'w_pool': nrm(ks[11], (N_EVEN, len(POOL_WINDOWS), POOL_GROUP, POOL_GROUP), f32) * POOL_GROUP ** -0.5,
        'pool_scale': 1.0 + 0.02 * nrm(ks[12], (N_EVEN, POOL_W), f32),
        'w_in_odd': nrm(ks[13], (N_ODD, D_MODEL, ODD_IN), f32) * D_MODEL ** -0.5,
        'w_out_odd': nrm(ks[14], (N_ODD, ODD_MIX, D_MODEL), f32) * ODD_MIX ** -0.5,
        'conv_w': nrm(ks[15], (N_ODD, CONV_WIDTH, CONV_W), f32) * CONV_WIDTH ** -0.5,
        'w_ffn_gate': nrm(ks[16], (DEPTH, D_MODEL, D_FF), f32) * D_MODEL ** -0.5,
        'w_ffn_up': nrm(ks[17], (DEPTH, D_MODEL, D_FF), f32) * D_MODEL ** -0.5,
        'w_ffn_down': nrm(ks[18], (DEPTH, D_FF, D_MODEL), f32) * D_FF ** -0.5,
        'final_g': 1.0 + 0.02 * nrm(ks[19], (D_MODEL,), f32),
    }

def reference(x, c, ctx, c_ctx, norm_g, w_mod, b_mod, w_in_even, w_out_even, q_norm_g, k_norm_g,
              w_pool, pool_scale, w_in_odd, w_out_odd, conv_w, w_ffn_gate, w_ffn_up, w_ffn_down,
              final_g):
    n = x.shape[1]
    cos, sin = rope_tables(n)
    xc = ctx
    for i in range(DEPTH):
        is_even = i % 2 == 0
        update_ctx = any(j % 2 == 0 for j in range(i + 1, DEPTH))
        sh1, sc1, g1, sh2, sc2, g2 = [m[:, None, :] for m in adaln(c, w_mod[i], b_mod[i])]
        h = modulate(rmsnorm(x, norm_g[i, 0]), sh1, sc1)
        if is_even or update_ctx:
            csh1, csc1, cg1, csh2, csc2, cg2 = adaln(c_ctx, w_mod[i], b_mod[i])
            hc = modulate(rmsnorm(xc, norm_g[i, 0]), csh1, csc1)
        if is_even:
            e = i // 2
            mix, mix_c = attn_pool_mixer(h, hc, w_in_even[e], q_norm_g[e], k_norm_g[e], w_pool[e],
                                         pool_scale[e], cos, sin, update_ctx)
            w_out = w_out_even[e]
        else:
            o = i // 2
            mix = fourier_conv_mixer(h, w_in_odd[o], conv_w[o])
            mix_c = fourier_conv_mixer(hc, w_in_odd[o], conv_w[o]) if update_ctx else None
            w_out = w_out_odd[o]
        x = x + g1 * (mix @ w_out)
        x = x + g2 * swiglu(modulate(rmsnorm(x, norm_g[i, 1]), sh2, sc2),
                            w_ffn_gate[i], w_ffn_up[i], w_ffn_down[i])
        if update_ctx:
            xc = xc + cg1 * (mix_c @ w_out)
            xc = xc + cg2 * swiglu(modulate(rmsnorm(xc, norm_g[i, 1]), csh2, csc2),
                                   w_ffn_gate[i], w_ffn_up[i], w_ffn_down[i])
    return rmsnorm(x, final_g)


_drawn_inputs = setup_inputs


def setup_inputs(seed=0):
    import zlib

    import numpy as np

    out = dict(_drawn_inputs(seed))
    spreads = {}
    factors = {'ctx': 3.8,
     'norm_g': 4.27,
     'q_norm_g': 8.0,
     'k_norm_g': 8.0,
     'pool_scale': 8.0,
     'final_g': 2.908}
    for name, (base, spread) in spreads.items():
        noise = np.random.default_rng([zlib.crc32(name.encode()), seed]).standard_normal(out[name].shape)
        drawn = base * np.exp(spread * noise) if base else spread * noise
        out[name] = __import__('jax').numpy.asarray(drawn.astype(out[name].dtype))
    for name, factor in factors.items():
        out[name] = (out[name] * factor).astype(out[name].dtype)
    return out
```

```python
from contextlib import ExitStack
from collections import namedtuple

import numpy as np

import concourse.bass as bass
from concourse import mybir

P = 128
D = 2048
KT = D // P
T = 256
NT = T // P
NC = 512
ND = D // NC
DFF = 5632
SLAB_K = 2
RING = 4
N_HEADS, N_KV, HD = 12, 4, 128
SCALE = float(HD) ** -0.5
EPS = 1e-6
SPLITS = (4, 4, 3)
START_CHUNKS = 8
MOD_CHUNKS = 6 * D // NC
PRE = 3

Chunk = namedtuple("Chunk", "kind w0 slot0 round0 n g pair use mods idx extra")


class Plan:

    def __init__(self):
        self.w = self.g = self.q = 0
        self.uses = [0, 0]

    def pair_use(self, pair):
        self.uses[pair] += 1
        return self.uses[pair] - 1

    def chunk(self, kind, idx, pair, n=8, mods=0, extra=None, both=False):
        c = Chunk(kind, self.w, self.w % RING, self.w // RING, n, self.g, pair, self.uses[pair],
                  tuple(range(self.q, self.q + mods)), idx, extra)
        self.w += n
        self.g += 1
        self.q += mods
        self.uses[pair] += 1
        if both:
            self.uses[1 - pair] += 1
        return c


def moved(c, i, w, g, use, q, idx):
    return c._replace(w0=c.w0 + i * w, round0=c.round0 + i * (w // RING), g=c.g + i * g,
                      use=c.use + i * use, mods=tuple(m + i * q for m in c.mods), idx=c.idx + i * idx)


def make_plan():
    p = Plan()
    plan = {}
    plan["even_in"] = [p.chunk("k", 0, 0, mods=2, both=True), p.chunk("v", 0, 0, mods=2, both=True),
                       p.chunk("q", 0, 0, mods=2), p.chunk("q", 1, 1, mods=1),
                       p.chunk("q", 2, 0, mods=1), p.chunk("u", 0, 1, mods=1)]
    plan["pool_use"] = (p.pair_use(0), p.uses[1])
    plan["even_out"] = [p.chunk("res", n, n % 2, mods=1, extra="stats gate") for n in range(ND)]
    h = 0
    for layer in range(2):
        splits = []
        for sp, nch in enumerate(SPLITS):
            mods = 1 if layer == 0 or sp == 0 else 0
            gu = []
            for i in range(nch):
                gu.append((p.chunk("gate", i, 0, mods=mods), p.chunk("up", i, 1, extra=h)))
                h += 1
            ex = ("gate" if sp == 0 else "") + (" stats" if sp == len(SPLITS) - 1 else "")
            down = [p.chunk("res", n, n % 2, n=2 * nch, extra=ex) for n in range(ND)]
            splits.append((gu, down))
        plan[f"ffn{layer}"] = splits
        if layer == 0:
            odd = [("f", 0), ("f", 1), ("cg", 0), ("xin", 0), ("bg", 0), ("cg", 1), ("xin", 1), ("bg", 1)]
            plan["odd_in"] = [p.chunk(k, i, n % 2, mods=1) for n, (k, i) in enumerate(odd)]
            plan["odd_out"] = [p.chunk("res", n, n % 2, mods=1, extra="stats gate") for n in range(ND)]
    assert p.q == 2 * MOD_CHUNKS - START_CHUNKS, p.q
    return plan, p.w


def build(nc, x_d, c_d, ctx_d, c_ctx_d, norm_g_d, w_mod_d, b_mod_d, w_in_e_d, w_out_e_d, q_g_d, k_g_d,
          w_pool_d, pool_scale_d, w_in_o_d, w_out_o_d, conv_w_d, w_gate_d, w_up_d, w_down_d, final_g_d,
          rope_cos_d, rope_sin_d, pool_mat_d, dft_d, out_d):
    f32, f32r, i32 = mybir.dt.float32, mybir.dt.float32r, mybir.dt.int32
    ALU, ACT, AX = mybir.AluOpType, mybir.ActivationFunctionType, mybir.AxisListType
    plan, n_slabs = make_plan()

    def slabs(w):
        return w.rearrange("(s j p) (n c) -> n s p j c", p=P, j=SLAB_K, c=NC)

    wv_in_e, wv_out_e = slabs(w_in_e_d[0]), slabs(w_out_e_d[0])
    wv_in_o, wv_out_o = slabs(w_in_o_d[0]), slabs(w_out_o_d[0])
    wv_gate = [slabs(w_gate_d[l]) for l in range(2)]
    wv_up = [slabs(w_up_d[l]) for l in range(2)]
    wv_down = [slabs(w_down_d[l]) for l in range(2)]
    wv_mod = [slabs(w_mod_d[l]) for l in range(2)]
    even_col = {"q": 0, "k": 3, "v": 4, "u": 5}
    odd_col = {"f": 0, "bg": 2, "cg": 4, "xin": 6}

    with ExitStack() as stack:
        def sb(name, shape, dt=f32):
            return stack.enter_context(nc.sbuf_tensor(name, shape, dt))

        def sem(name):
            return stack.enter_context(nc.semaphore(name))

        x_tok = sb("x_tok", [P, NT, D])
        h_hi, h_lo = sb("h_hi", [P, KT, T], f32r), sb("h_lo", [P, KT, T], f32r)
        m_hi, m_lo = sb("m_hi", [P, KT, T], f32r), sb("m_lo", [P, KT, T], f32r)
        raw = sb("raw", [P, RING, SLAB_K, NC])
        w_hi, w_lo = sb("w_hi", [P, RING, SLAB_K, NC], f32r), sb("w_lo", [P, RING, SLAB_K, NC], f32r)
        mod_raw = sb("mod_raw", [P, RING, SLAB_K, NC])
        acc = sb("acc", [P, 2, NC])
        gate_bc = sb("gate_bc", [P, D])
        scratch = sb("scratch", [P, 6144])
        tables = sb("tables", [P, 2560])
        junk = sb("junk", [P, NC])
        ident, ones = sb("ident", [P, P]), sb("ones", [P, 1])
        diag = sb("diag", [P, NT, P])
        rows = sb("rows", [P, 3, P])
        colsA = sb("colsA", [P, P])
        bias_cols = sb("bias_cols", [P, 2 * MOD_CHUNKS, 4])
        mod_cols = sb("mod_cols", [P, 2 * MOD_CHUNKS, 4])
        ctx_cols = sb("ctx_cols", [P, START_CHUNKS, 4])
        silu_c = sb("silu_c", [P, KT, 2])
        s_col = sb("s_col", [P, KT])
        sumsq = sb("sumsq", [P, NT, ND])
        msq = sb("msq", [P, NT])
        rms = sb("rms", [P, NT])
        head_sq = sb("head_sq", [P, 4, 4])
        head_ms = sb("head_ms", [P, NT, 4])
        head_r = sb("head_r", [P, NT, 4])
        guess, newton = sb("guess", [P, 8], mybir.dt.int32), sb("newton", [P, 8])
        neg_max = sb("neg_max", [P, 2])
        row_max = sb("row_max", [P, 2])
        p_sum = sb("p_sum", [P, 2])
        p_inv = sb("p_inv", [P, 2])

        ctx_tok = scratch[:, 0:4096].rearrange("p (t n) -> p t n", t=NT)
        hf = scratch[:, 4096:5120].rearrange("p (b j t) -> p b j t", b=2, j=2)
        kt_sb = x_tok[:, 0, :].rearrange("p (h k) -> p h k", h=N_KV)
        v_sb = x_tok[:, 1, :].rearrange("p (k n) -> p k n", k=4)
        qt = scratch[:, 0:2048].rearrange("p (c h t) -> p c h t", c=2, h=4)
        k_tmp = scratch[:, 0:2048].rearrange("p (i n) -> p i n", i=4)
        q_tmp = scratch[:, 2048:3072].rearrange("p (t n) -> p t n", t=NT)
        rope_a, rope_b = scratch[:, 3072:3584], scratch[:, 3584:4096]
        probs = scratch[:, 4096:5120].rearrange("p (b k) -> p b k", b=2)
        probs_t = scratch[:, 5120:6144].rearrange("p (b k t) -> p b k t", b=2, k=4)
        u_sb = q_tmp
        pooled = scratch[:, 3072:4096].rearrange("p (g t) -> p g t", g=4)
        fold = gate_bc[:, 0:1024].rearrange("p (a t d) -> p a t d", a=4, t=NT)
        rope_raw = gate_bc[:, 1024:1536].rearrange("p (a t d) -> p a t d", a=2, t=NT)
        head_g = gate_bc[:, 1536:1792].rearrange("p (a d) -> p a d", a=2)
        pool_mat = tables[:, 0:2048].rearrange("p (g k t) -> p g k t", g=4, k=NT)
        w_pool = tables[:, 2048:2560].rearrange("p (g d) -> p g d", g=4)
        dft_cs = tables[:, 0:1024].rearrange("p (k n) -> p k n", k=2)
        dft_ns = tables[:, 1024:1536].rearrange("p (k n) -> p k n", k=2)
        silu_g = scratch[:, 0:1024].rearrange("p (t n) -> p t n", t=NT)
        hid_tok = scratch[:, 1024:2048].rearrange("p (t n) -> p t n", t=NT)
        res_tmp = scratch[:, 2048:3072].rearrange("p (t n) -> p t n", t=NT)
        final_g = scratch[:, 4096:6144]
        f_sb = scratch[:, 0:2048].rearrange("p (t n) -> p t n", t=NT)
        y_conv = scratch[:, 0:1024].rearrange("p (c t) -> p c t", c=4)
        odd_tmp = scratch[:, 3072:4096].rearrange("p (t n) -> p t n", t=NT)
        dft1 = scratch[:, 5120:6144].rearrange("p (q n) -> p q n", q=2)

        c_cols = colsA[:, 0:32]
        norm_cols = colsA[:, 32:96]
        conv_cols = colsA[:, 96:120]
        pscale_cols = colsA[:, 120:124]

        def mod_vec(layer, v):
            n = layer * MOD_CHUNKS + v * ND
            return mod_cols[:, n:n + ND, :].rearrange("p n j -> p (n j)")

        bank = [stack.enter_context(nc.psum_tensor(f"bank{i}", [P, NC], f32)) for i in range(8)]
        B_COL, B_A, B_B, B_C = 4, 5, 6, 7

        raw_full = [sem(f"raw_full{i}") for i in range(RING)]
        hi_done, lo_done, slab_free = sem("hi_done"), sem("lo_done"), sem("slab_free")
        mod_full = [sem(f"mod_full{i}") for i in range(RING)]
        mod_step = sem("mod_step")
        mod_mm, mod_col_done = sem("mod_mm"), sem("mod_col_done")
        start_free, row_copied, row_mm, start_col = (
            sem("start_free"), sem("row_copied"), sem("row_mm"), sem("start_col"))
        pair_freed = [sem("pair0_freed"), sem("pair1_freed")]
        rows_in, x_in, rope_in, tab_in, wpool_in, x_again, fin_in, out_done = (
            sem("rows_in"), sem("x_in"), sem("rope_in"), sem("tab_in"), sem("wpool_in"),
            sem("x_again"), sem("fin_in"), sem("out_done"))
        ident_ready, cols_t, cols_ready, silu_ready = (
            sem("ident_ready"), sem("cols_t"), sem("cols_ready"), sem("silu_ready"))
        sq_done, diag_ready, norm_t, norm_hf, norm_hi, h_ready = (
            sem("sq_done"), sem("diag_ready"), sem("norm_t"), sem("norm_hf"), sem("norm_hi"), sem("h_ready"))
        v_self = sem("v_self")
        head_sums, rope_done = sem("head_sums"), sem("rope_done")
        kt_t, kt_in, qt_t, qt_in = sem("kt_t"), sem("kt_in"), sem("qt_t"), sem("qt_in")
        scores_done, max_done, exp_done, probs_done = (
            sem("scores_done"), sem("max_done"), sem("exp_done"), sem("probs_done"))
        pt_t, pt_in, pv_done, mix_hi, mix_lo = (
            sem("pt_t"), sem("pt_in"), sem("pv_done"), sem("mix_hi"), sem("mix_lo"))
        pool_mm = sem("pool_mm")
        gb_mm, gb_in = sem("gb_mm"), sem("gb_in")
        res_step = sem("res_step")
        hid_t, hid_hi, hid_lo = sem("hid_t"), sem("hid_hi"), sem("hid_lo")
        dft_a, dft_a_in, dft_y, u_conv_t, conv_done, bg_t, mixed = (
            sem("dft_a"), sem("dft_a_in"), sem("dft_y"), sem("u_conv_t"), sem("conv_done"), sem("bg_t"),
            sem("mixed"))
        x_final = sem("x_final")

        block = stack.enter_context(nc.Block())

        order = plan["even_out"] + [c for _, d in plan["ffn0"] for c in d] + plan["odd_out"] \
            + [c for _, d in plan["ffn1"] for c in d]
        res_no = {c.g: n + 1 for n, c in enumerate(order)}

        EVEN_MIX = 24 + 4
        DFT_MIX = 4
        HID_CREDIT = 2

        def loop_chunks(gu, i):
            (gate, up), was = gu[1], gu[0][1]
            return (moved(gate, i, 16, 2, 1, 1, 1),
                    moved(up, i, 16, 2, 1, 0, 1)._replace(extra=up.extra + i),
                    moved(was, i, 16, 2, 1, 0, 1)._replace(extra=was.extra + i))

        def acc_slot(c):
            return 0 if c.kind == "gate" else c.mods[-1] % 2

        @block.sync
        def _(sp):
            sp.dma_start(x_tok[:, :, :], x_d[0].rearrange("(t p) n -> p t n", p=P)).then_inc(x_in, 16)
            sp.dma_start(ctx_tok, ctx_d[0].rearrange("(t p) n -> p t n", p=P)).then_inc(x_in, 16)

            def load(c, view, col, row0=0):
                for s in range(c.n):
                    if not isinstance(c.w0, int) or c.w0 + s >= RING:
                        sp.wait_ge(lo_done, c.w0 + (s - RING + 1))
                    slot = (c.slot0 + s) % RING
                    sp.dma_start(raw[:, slot, :, :], view[col, row0 + s]).then_inc(raw_full[slot], 16)

            def ffn(layer):
                first = 0
                for gu, down in plan[f"ffn{layer}"]:
                    with sp.Fori(0, len(gu)) as i:
                        for c, view in zip(gu[0], (wv_gate, wv_up)):
                            load(moved(c, i, 16, 2, 1, 0, 1), view[layer], first + i)
                    for c in down:
                        load(c, wv_down[layer], c.idx, 2 * first)
                    first += len(gu)

            for c in plan["even_in"]:
                load(c, wv_in_e, even_col[c.kind] + c.idx)
            for c in plan["even_out"]:
                load(c, wv_out_e, c.idx)
                if c.idx == 0:
                    sp.wait_ge(pv_done, 24)
                    sp.dma_start(x_tok[:, :, :], x_d[0].rearrange("(t p) n -> p t n", p=P)) \
                      .then_inc(x_again, 16)
            ffn(0)
            for c in plan["odd_in"]:
                load(c, wv_in_o, odd_col[c.kind] + c.idx)
            for c in plan["odd_out"]:
                load(c, wv_out_o, c.idx)
            ffn(1)
            for n in range(ND):
                sp.wait_ge(x_final, n + 1)
                sp.dma_start(out_d[0].rearrange("(t p) n -> p t n", p=P)[:, :, n * NC:(n + 1) * NC],
                             x_tok[:, :, n * NC:(n + 1) * NC]).then_inc(out_done, 16)
            sp.wait_ge(out_done, 16 * ND)

        @block.gpsimd
        def _(pool):
            def load_mod(view, n, s, slot):
                pool.dma_start(mod_raw[:, slot, :, :], view[n, s]).then_inc(mod_full[slot], 16)

            for s in range(RING):
                load_mod(wv_mod[0], 0, s, s)
            pool.memset(ident[:, :], 0.0).then_inc(ident_ready, 1)
            pool.wait_ge(ident_ready, 1)
            pool.affine_select(out=ident[:, :], in_=ident[:, :], compare_op=ALU.not_equal, fill=1.0,
                               base=0, pattern=[[-1, P]], channel_multiplier=1).then_inc(ident_ready, 1)
            with pool.Fori(0, ND - 1) as i:
                for s in range(16):
                    pool.wait_ge(start_free, i * 16 + s + 1)
                    n, t = [(i, s + 4), (i + 4, s - 4), (i + 1, s - 12)][(s >= 4) + (s >= 12)]
                    load_mod(wv_mod[0], n, t, s % RING)
            for s in range(16):
                pool.wait_ge(start_free, (ND - 1) * 16 + s + 1)
                n, t = [(ND - 1, s + 4), (START_CHUNKS - 1, s - 4), (START_CHUNKS, s - 12)][(s >= 4) + (s >= 12)]
                load_mod(wv_mod[0], n, t, s % RING)

            def stream(layer, n0, count, q0):
                with pool.Fori(0, count) as i:
                    for s in range(8):
                        pool.wait_ge(mod_step, (i + q0) * 16 + 2 * (s - RING + 1))
                        load_mod(wv_mod[layer], i + n0, s, s % RING)

            n_rest = MOD_CHUNKS - START_CHUNKS
            for s in range(RING, 8):
                pool.wait_ge(mod_step, 2 * (s - RING + 1))
                load_mod(wv_mod[0], START_CHUNKS, s, s % RING)
            stream(0, START_CHUNKS + 1, n_rest - 1, 1)
            stream(1, 0, MOD_CHUNKS, n_rest)

        @block.tensor
        def _(pe):
            drained = {}

            def take(b, reader, value):
                if b in drained:
                    pe.wait_ge(*drained[b])
                drained[b] = (reader, value)

            pe.wait_ge(ident_ready, 2)
            pe.wait_ge(rows_in, 16 * 7)
            pe.wait_ge(cols_ready, 3)
            for a in range(3):
                op = pe.transpose(bank[B_A][:, a * P:(a + 1) * P], rows[:, a, :], ident[:, :])
            op.then_inc(cols_t, 1)
            pe.wait_ge(silu_ready, 2)
            with pe.Fori(0, ND) as i:
                def matvec(b, half):
                    if half == 0:
                        pe.wait_ge(row_copied, 2 * i + b + 1)
                    for s in range(4 * half, 4 * half + 4):
                        pe.wait_ge(mod_full[s % RING], (i * 4 + (2 * b + s // RING + 1)) * 16)
                        for j in range(SLAB_K):
                            k = SLAB_K * s + j
                            op = pe.matmul(bank[b][0:2, :], silu_c[:, k, :], mod_raw[:, s % RING, j, :],
                                           start=(k == 0), stop=(k == KT - 1))
                        op.then_inc(start_free, 1)

                def row_to_cols(b):
                    pe.wait_ge(row_copied, 2 * i + b + 3)
                    pe.wait_ge(start_col, 2 * i + b + 1)
                    for j in range(4):
                        op = pe.matmul(bank[B_COL][:, 2 * j:2 * j + 2], acc[0:2, b, j * P:(j + 1) * P],
                                       ident[0:2, 0:2], start=True, stop=True)
                    op.then_inc(row_mm, 1)

                matvec(0, 0)
                matvec(0, 1)
                matvec(1, 0)
                row_to_cols(0)
                matvec(1, 1)
                row_to_cols(1)
            drained[B_COL] = (start_col, 2 * ND + 1)
            drained[B_A] = (cols_ready, 4)

            def norm_group(nz, x_in_tok, grp):
                b = B_A + grp % 2
                if grp == 0:
                    pe.wait_ge(diag_ready, NT * (nz + 1))
                take(b, norm_hf, 8 * nz + grp + 1)
                for j in range(2):
                    for t in range(NT):
                        ft = 2 * grp + j
                        op = pe.matmul(bank[b][:, j * T + t * P:j * T + (t + 1) * P],
                                       x_in_tok[:, t, ft * P:(ft + 1) * P], diag[:, t, :],
                                       start=True, stop=True)
                op.then_inc(norm_t, 1)

            def mod_columns(q, slot):
                take(B_COL, mod_col_done, q + 1)
                pe.wait_ge(mod_step, (q + 1) * 16)
                for j in range(4):
                    op = pe.matmul(bank[B_COL][:, j:j + 1], acc[:, slot, j * P:(j + 1) * P], ones[:, :],
                                   start=True, stop=True)
                op.then_inc(mod_mm, 1)

            def gemm(c, hi, lo, side, ready=None, both=None):
                groups = [(hi, lo, c.pair)]
                if both:
                    groups.append((*both, 1 - c.pair))
                for _, _, pair in groups:
                    if not isinstance(c.use, int) or c.use > 0:
                        pe.wait_ge(pair_freed[pair], c.use)
                for s in range(c.n):
                    if ready and s in ready:
                        for w in ready[s]:
                            pe.wait_ge(*w)
                    pe.wait_ge(lo_done, c.w0 + s + 1)
                    slot = (c.slot0 + s) % RING
                    for j in range(SLAB_K):
                        k = SLAB_K * s + j
                        for a_hi, a_lo, pair in groups:
                            for t in range(NT):
                                ps = bank[2 * pair + t][:, :]
                                ah, al = a_hi[:, k, t * P:(t + 1) * P], a_lo[:, k, t * P:(t + 1) * P]
                                last = s == c.n - 1 and j == SLAB_K - 1
                                pe.matmul(ps, ah, w_hi[:, slot, j, :], start=(k == 0), stop=False)
                                pe.matmul(ps, ah, w_lo[:, slot, j, :], start=False, stop=False)
                                op = pe.matmul(ps, al, w_hi[:, slot, j, :], start=False, stop=last)
                    op.then_inc(slab_free, 1)
                    side(s)

            def mods_at(c, prev, s):
                if s == 0 and prev is not None and prev.mods:
                    mod_columns(prev.mods[-1], acc_slot(prev))
                if s == 4 and c is not None and len(c.mods) == 2:
                    mod_columns(c.mods[0], c.mods[0] % 2)

            def gate_columns(layer, v, n, value):
                take(B_C, gb_in, value)
                g = mod_vec(layer, v)
                if n == 0:
                    pe.wait_ge(mod_col_done, layer * MOD_CHUNKS + (v + 1) * ND - START_CHUNKS)
                for j in range(4):
                    ft = 4 * n + j
                    op = pe.matmul(bank[B_C][:, j * P:(j + 1) * P], g[:, ft:ft + 1].broadcast_to([P, P]),
                                   ident[:, :], start=True, stop=True)
                op.then_inc(gb_mm, 1)

            def transposes(bk, src, count, sem_):
                for j in range(count):
                    op = pe.transpose(bank[bk][:, j * P:(j + 1) * P], src(j), ident[:, :])
                op.then_inc(sem_, 1)

            for grp in range(8):
                norm_group(0, x_tok, grp)
            for grp in range(8):
                norm_group(1, ctx_tok, grp)

            def unit(i):
                if 0 <= i - 3 < 24:
                    u = i - 3
                    pe.wait_ge(pt_in, u + 1)
                    take(B_C, mix_lo, u + 1)
                    kv = (4 * (u // 8) + u % 4) // 3
                    for k in range(4):
                        op = pe.matmul(bank[B_C][:, 0:P], v_sb[:, k, kv * P:(kv + 1) * P],
                                       probs_t[:, u % 2, k, :], start=(k == 0), stop=(k == 3))
                    op.then_inc(pv_done, 1)
                if 0 <= i - 2 < 24:
                    u = i - 2
                    pe.wait_ge(probs_done, u + 1)
                    take(B_B, pt_in, u + 1)
                    transposes(B_B, lambda j: probs[:, u % 2, j * P:(j + 1) * P], 4, pt_t)
                if 0 <= i < 24:
                    c, t, h = i // 8, (i // 4) % 2, i % 4
                    if i == 0:
                        pe.wait_ge(kt_in, 4)
                    pe.wait_ge(qt_in, 2 * c + t + 1)
                    take(B_A, exp_done, i + 1)
                    pe.matmul(bank[B_A][:, :], qt[:, c % 2, h, t * P:(t + 1) * P],
                              kt_sb[:, (4 * c + h) // 3, :], start=True, stop=True).then_inc(scores_done, 1)

            def q_turn(c, t):
                pe.wait_ge(rope_done, 4 + 2 * c + t + 1)
                take(B_COL, qt_in, 2 * c + t + 1)
                transposes(B_COL, lambda j: q_tmp[:, t, j * P:(j + 1) * P], 4, qt_t)

            prev = None
            for n, c in enumerate(plan["even_in"]):
                def side(s, c=c, n=n, prev=prev):
                    mods_at(c, prev, s)
                    if n == 2 and s < 4:
                        pe.wait_ge(rope_done, s + 1)
                        take(B_B, kt_in, s + 1)
                        transposes(B_B, lambda j: k_tmp[:, s, j * P:(j + 1) * P], 4, kt_t)
                    if n >= 3 and s in (5, 7):
                        q_turn(n - 3, (s - 5) // 2)
                    if n >= 4:
                        unit(8 * (n - 4) + s)
                ready = {s: [(h_ready, s + 1), (h_ready, 8 + s + 1)] for s in range(8)} if n == 0 else None
                gemm(c, h_hi, h_lo, side, ready, both=(m_hi, m_lo) if n < 2 else None)
                prev = c
            pool_use = plan["pool_use"]
            for i in range(16, 28):
                mods_at(None, prev, i - 16)
                if i == 24:
                    pe.wait_ge(pair_freed[prev.pair], prev.use + 1)
                    pe.wait_ge(tab_in, 16)
                    pe.wait_ge(pair_freed[0], pool_use[0])
                    for g in range(4):
                        for k in range(NT):
                            op = pe.matmul(bank[g // 2][:, (g % 2) * T:(g % 2 + 1) * T],
                                           u_sb[:, k, g * P:(g + 1) * P], pool_mat[:, g, k, :],
                                           start=(k == 0), stop=(k == NT - 1))
                    op.then_inc(pool_mm, 1)
                unit(i)
            pe.wait_ge(pair_freed[0], pool_use[0] + 1)
            pe.wait_ge(wpool_in, 16)
            pe.wait_ge(pair_freed[1], pool_use[1])
            for g in range(4):
                op = pe.matmul(bank[2 + g // 2][:, (g % 2) * T:(g % 2 + 1) * T], w_pool[:, g, :],
                               pooled[:, g, :], start=True, stop=True)
            op.then_inc(pool_mm, 1)

            gates_made = 0

            def res_side(c, prev, layer, v, s):
                nonlocal gates_made
                mods_at(c, prev, s)
                if "gate" in c.extra and s == 4:
                    gate_columns(layer, v, c.idx, gates_made + 1)
                    gates_made += 1

            prev = None
            for c in plan["even_out"]:
                gemm(c, m_hi, m_lo, lambda s: res_side(c, prev, 0, 2, s),
                     {0: [(mix_lo, EVEN_MIX)]} if c.idx == 0 else None)
                prev = c
            mods_at(None, prev, 0)

            def hid_turn(up):
                h = up.extra
                pe.wait_ge(pair_freed[1], up.use + 1)
                for t in range(NT):
                    take(B_A + t, hid_lo, HID_CREDIT + 2 * h + t + 1)
                    transposes(B_A + t, lambda j: hid_tok[:, t, j * P:(j + 1) * P], 4, hid_t)

            def ffn(layer, nz):
                for sp_n, (gu, down) in enumerate(plan[f"ffn{layer}"]):
                    def gate_up(gate, up, was, ready=None):
                        gemm(gate, h_hi, h_lo, lambda s: hid_turn(was) if was and s == 1 else None, ready)
                        gemm(up, h_hi, h_lo, lambda s: mods_at(None, gate, s))

                    normed = {s: [(h_ready, 8 * nz + s + 1)] for s in range(8)} if sp_n == 0 else None
                    gate_up(*gu[0], None, normed)
                    with pe.Fori(0, len(gu) - 1) as i:
                        gate, up, was = loop_chunks(gu, i)
                        for t in range(NT):
                            drained[B_A + t] = (hid_lo, HID_CREDIT + 2 * was.extra + t - 1)
                        if gate.mods:
                            drained[B_COL] = (mod_col_done, gate.mods[0])
                        gate_up(gate, up, was)
                    gate, up = gu[-1]
                    h = up.extra
                    for t in range(NT):
                        drained[B_A + t] = (hid_lo, HID_CREDIT + 2 * h + t - 1)
                    if gate.mods:
                        drained[B_COL] = (mod_col_done, gate.mods[0] + 1)
                    for c in down:
                        def side(s):
                            if c.idx == 0 and s == 1:
                                hid_turn(up)
                            res_side(c, None, layer, 5, s)
                        ready = {0: [(hid_lo, HID_CREDIT + 2 * h)],
                                 2 * (len(gu) - 1): [(hid_lo, HID_CREDIT + 2 * h + 2)]} \
                            if c.idx == 0 else None
                        gemm(c, m_hi, m_lo, side, ready)

            for grp in range(8):
                norm_group(2, x_tok, grp)
            ffn(0, 2)
            for grp in range(8):
                norm_group(3, x_tok, grp)

            def dft_side(i):
                g, r = divmod(i, 4)
                if g >= 4:
                    return
                if r == 0:
                    f = plan["odd_in"][g // 2]
                    pe.wait_ge(pair_freed[f.pair], f.use + 1)
                    if g == 0:
                        pe.wait_ge(tab_in, 48)
                    for q in range(2):
                        take(B_A + q, dft_a_in, 2 * g + q + 1)
                        for k in range(NT):
                            ch = g * 256 + q * P
                            op = pe.matmul(bank[B_A + q][:, :], f_sb[:, k, ch:ch + P], dft_cs[:, k, :],
                                           start=(k == 0), stop=(k == NT - 1))
                        op.then_inc(dft_a, 1)
                if r == 2:
                    pe.wait_ge(dft_a_in, 2 * g + 2)
                    take(B_C, mix_lo, EVEN_MIX + g + 1)
                    for o in range(2):
                        for q in range(2):
                            pe.matmul(bank[B_C][:, o * T:(o + 1) * T], dft_cs[:, q, o * P:(o + 1) * P],
                                      dft1[:, q, 0:T], start=(q == 0), stop=False)
                            op = pe.matmul(bank[B_C][:, o * T:(o + 1) * T], dft_ns[:, q, o * P:(o + 1) * P],
                                           dft1[:, q, T:2 * T], start=False, stop=(q == 1))
                    op.then_inc(dft_y, 1)

            def conv_turn(src, t_sem, reader, value):
                pe.wait_ge(pair_freed[src.pair], src.use + 1)
                for b in range(2):
                    take(B_A + b, reader, value(b))
                    for j in range(2):
                        for t in range(NT):
                            ct = 2 * b + j
                            op = pe.transpose(bank[B_A + b][:, j * T + t * P:j * T + (t + 1) * P],
                                              odd_tmp[:, t, ct * P:(ct + 1) * P], ident[:, :])
                    op.then_inc(t_sem, 1)

            prev = None
            for n, c in enumerate(plan["odd_in"]):
                def side(s, c=c, n=n, prev=prev):
                    mods_at(c, prev, s)
                    if n >= 2:
                        dft_side(8 * (n - 2) + s)
                    if c.kind == "bg" and s == 2:
                        conv_turn(prev, u_conv_t, conv_done, lambda b: 4 * c.idx + 2 * b + 2)
                    if c.kind == "cg" and c.idx == 1 and s == 1:
                        conv_turn(prev, bg_t, mixed, lambda b: b + 1)
                gemm(c, h_hi, h_lo, side,
                     {s: [(h_ready, 24 + s + 1)] for s in range(8)} if n == 0 else None)
                prev = c
            for c in plan["odd_out"]:
                def side(s, c=c, prev=prev):
                    if c.idx == 0 and s == 1:
                        conv_turn(prev, bg_t, mixed, lambda b: 2 + b + 1)
                    res_side(c, prev, 1, 2, s)
                gemm(c, m_hi, m_lo, side,
                     {0: [(mix_lo, EVEN_MIX + DFT_MIX + 4)], 6: [(mix_lo, EVEN_MIX + DFT_MIX + 8)]}
                     if c.idx == 0 else None)
                prev = c
            mods_at(None, prev, 0)
            for grp in range(8):
                norm_group(4, x_tok, grp)
            ffn(1, 4)

        @block.scalar
        def _(act):
            act.wait_ge(cols_ready, 3)
            row_parts = [(c_d.rearrange("b (k p) -> (b k) p", p=P), 0, 0, 16),
                         (c_ctx_d.rearrange("(k p) -> k p", p=P), 0, 16, 16),
                         (norm_g_d.rearrange("l s (k p) -> (l s k) p", p=P), 0, 32, 64),
                         (conv_w_d.rearrange("o j (k p) -> (o j k) p", p=P), 0, 96, 24),
                         (pool_scale_d.rearrange("o (k p) -> (o k) p", p=P), 0, 120, 4),
                         (b_mod_d[0].rearrange("(k p) -> k p", p=P), 1, 0, 96),
                         (b_mod_d[1].rearrange("(k p) -> k p", p=P), 2, 0, 96)]
            for src, a, r, n in row_parts:
                act.dma_start(rows[r:r + n, a, :], src).then_inc(rows_in, 16)
            act.dma_start(head_g[:, 0, :], q_g_d[0:1, :].broadcast_to([P, HD])).then_inc(rope_in, 16)
            act.dma_start(head_g[:, 1, :], k_g_d[0:1, :].broadcast_to([P, HD])).then_inc(rope_in, 16)
            act.dma_start(rope_raw[:, 0, :, :], rope_cos_d.rearrange("(t p) d -> p t d", p=P)) \
               .then_inc(rope_in, 16)
            act.dma_start(rope_raw[:, 1, :, :], rope_sin_d.rearrange("(t p) d -> p t d", p=P)) \
               .then_inc(rope_in, 16)
            act.dma_start(pool_mat, pool_mat_d.rearrange("g (k p) t -> p g k t", p=P)).then_inc(tab_in, 16)
            act.dma_start(w_pool, w_pool_d[0].rearrange("g c d -> c g d")).then_inc(wpool_in, 16)
            act.wait_ge(cols_ready, 4)
            for v in range(2):
                act.activation(silu_c[:, :, v], c_cols[:, 16 * v:16 * v + 16], ACT.Silu) \
                   .then_inc(silu_ready, 1)

            def hi(c, s):
                slot = (c.slot0 + s) % RING
                if not isinstance(c.w0, int) or c.w0 + s >= RING:
                    act.wait_ge(slab_free, c.w0 + (s - RING + 1))
                act.wait_ge(raw_full[slot], (c.round0 + (c.slot0 + s) // RING + 1) * 16)
                act.activation(w_hi[:, slot, :, :], raw[:, slot, :, :], ACT.Copy).then_inc(hi_done, 1)

            squared = summed = 0

            def square(src, t, n):
                nonlocal squared
                if squared:
                    act.wait_ge(sq_done, squared)
                squared += 1
                act.activation(junk[:, :], src[:, t, n * NC:(n + 1) * NC], ACT.Square,
                               accum_out=sumsq[:, t, n:n + 1]).then_inc(sq_done, 1)

            act.wait_ge(x_in, 32)
            for t in range(NT):
                for n in range(ND):
                    square(x_tok, t, n)
            for s in range(RING):
                hi(plan["even_in"][0], s)
            with act.Fori(0, ND) as i:
                for b in range(2):
                    act.wait_ge(start_free, (2 * i + b + 1) * 8)
                    act.wait_ge(row_mm, 2 * i + b + 1)
                    act.activation(acc[0:2, b, :], bank[b][0:2, :], ACT.Copy).then_inc(row_copied, 1)
            act.wait_ge(diag_ready, NT)
            for t in range(NT):
                for n in range(ND):
                    square(ctx_tok, t, n)

            def chunk(c, at, start=0):
                for s in range(start, c.n):
                    hi(c, s)
                    at(s)

            def prefill(c, lo_=0, hi_=PRE):
                for s in range(lo_, hi_):
                    hi(c, s)

            def norm(nz, dst):
                for grp in range(8):
                    act.wait_ge(norm_hf, 8 * nz + grp + 1)
                    act.activation(dst[:, 2 * grp:2 * grp + 2, :], hf[:, grp % 2, :, :], ACT.Copy) \
                       .then_inc(norm_hi, 1)

            def head_sum(src, i):
                nonlocal summed
                if summed:
                    act.wait_ge(head_sums, summed)
                summed += 1
                for h in range(4):
                    op = act.activation(junk[:, h * P:(h + 1) * P], src[:, h * P:(h + 1) * P], ACT.Square,
                                        accum_out=head_sq[:, i, h:h + 1])
                op.then_inc(head_sums, 1)

            def unit(i):
                if 0 <= i - 4 < 24:
                    u = i - 4
                    act.wait_ge(max_done, u + 1)
                    if u >= 2:
                        act.wait_ge(pt_t, u - 1)
                    act.activation(probs[:, u % 2, :], bank[B_A][:, :], ACT.Exp, scale=SCALE,
                                   bias=neg_max[:, u % 2:u % 2 + 1],
                                   accum_out=p_sum[:, u % 2:u % 2 + 1]).then_inc(exp_done, 1)
                if 0 <= i - 6 < 24:
                    u = i - 6
                    act.wait_ge(pt_t, u + 1)
                    if u >= 2:
                        act.wait_ge(pv_done, u - 1)
                    act.activation(probs_t[:, u % 2, :, :],
                                   bank[B_B][:, :].rearrange("p (k t) -> p k t", k=4), ACT.Copy) \
                       .then_inc(pt_in, 1)
                if 0 <= i - 7 < 24:
                    u = i - 7
                    act.wait_ge(pv_done, u + 1)
                    h, t = 4 * (u // 8) + u % 4, (u // 4) % 2
                    act.activation(m_hi[:, h, t * P:(t + 1) * P], bank[B_C][:, 0:P], ACT.Copy) \
                       .then_inc(mix_hi, 1)

            def even_at(n, prev, s):
                if n == 1:
                    if s == 3:
                        act.wait_ge(slab_free, prev.w0 + prev.n)
                        for t in range(NT):
                            op = act.activation(k_tmp[:, t, :], bank[t][:, :], ACT.Copy)
                        op.then_inc(pair_freed[0], 1)
                    if s in (4, 6):
                        act.wait_ge(pair_freed[(s - 4) // 2], 1)
                        for i in (s - 4, s - 3):
                            head_sum(k_tmp[:, i, :], i)
                if n == 2:
                    if s == 3:
                        act.wait_ge(slab_free, prev.w0 + prev.n)
                        for t in range(NT):
                            op = act.activation(v_sb[:, 2 + t, :], bank[t][:, :], ACT.Copy)
                        op.then_inc(pair_freed[0], 1)
                    if 4 <= s:
                        i = s - 4
                        act.wait_ge(kt_t, i + 1)
                        at = 2 * P + i * P if i < 2 else (i - 2) * P
                        act.activation(kt_sb[:, :, at:at + P],
                                       bank[B_B][:, :].rearrange("p (h k) -> p h k", h=4), ACT.Copy) \
                           .then_inc(kt_in, 1)
                if n >= 3 and s == 3:
                    c = n - 3
                    act.wait_ge(slab_free, prev.w0 + prev.n)
                    if c > 0:
                        act.wait_ge(qt_t, 2 * c)
                    for t in range(NT):
                        op = act.activation(q_tmp[:, t, :], bank[2 * prev.pair + t][:, :], ACT.Copy)
                    op.then_inc(pair_freed[prev.pair], 1)
                    act.wait_ge(pair_freed[prev.pair], prev.use + 1)
                    for t in range(NT):
                        head_sum(q_tmp[:, t, :], t)
                if n >= 4 and s in (1, 3):
                    c, t = n - 4, (s - 1) // 2
                    act.wait_ge(qt_t, 2 * c + t + 1)
                    act.activation(qt[:, c % 2, :, t * P:(t + 1) * P],
                                   bank[B_COL][:, :].rearrange("p (h k) -> p h k", h=4), ACT.Copy) \
                       .then_inc(qt_in, 1)
                if n >= 4:
                    unit(8 * (n - 4) + s)

            even_in, even_out = plan["even_in"], plan["even_out"]
            norm(0, h_hi)
            norm(1, m_hi)
            prev = None
            for n, c in enumerate(even_in):
                chunk(c, lambda s: even_at(n, prev, s), RING if n == 0 else 0)
                prev = c
            for i in range(16, 32):
                if i < 16 + RING:
                    hi(even_out[0], i - 16)
                if i in (17, 19):
                    c, t = 2, (i - 17) // 2
                    act.wait_ge(qt_t, 2 * c + t + 1)
                    act.activation(qt[:, 0, :, t * P:(t + 1) * P],
                                   bank[B_COL][:, :].rearrange("p (h k) -> p h k", h=4), ACT.Copy) \
                       .then_inc(qt_in, 1)
                if i == 19:
                    act.wait_ge(slab_free, prev.w0 + prev.n)
                    for t in range(NT):
                        op = act.activation(u_sb[:, t, :], bank[2 * prev.pair + t][:, :], ACT.Copy)
                    op.then_inc(pair_freed[prev.pair], 1)
                unit(i)
                if i == 28:
                    act.wait_ge(pool_mm, 1)
                    for b in range(2):
                        op = act.activation(pooled[:, 2 * b:2 * b + 2, :],
                                            bank[b][:, :].rearrange("p (g t) -> p g t", g=2), ACT.Copy)
                    op.then_inc(pair_freed[0], 1)
            act.wait_ge(pool_mm, 2)
            for g in range(4):
                act.activation(m_hi[:, N_HEADS + g, :], bank[2 + g // 2][:, (g % 2) * T:(g % 2 + 1) * T],
                               ACT.Copy, scale=pscale_cols[:, g:g + 1]).then_inc(mix_hi, 1)

            gates_made = 0

            def gate_copy(n):
                nonlocal gates_made
                gates_made += 1
                act.wait_ge(gb_mm, gates_made)
                act.activation(gate_bc[:, n * NC:(n + 1) * NC], bank[B_C][:, :], ACT.Copy) \
                   .then_inc(gb_in, 1)

            def res_at(prev, s):
                if prev is None:
                    return
                if s == 0 and "gate" in prev.extra:
                    gate_copy(prev.idx)
                if s == 4 and "stats" in prev.extra:
                    act.wait_ge(res_step, res_no[prev.g])
                    for t in range(NT):
                        square(x_tok, t, prev.idx)

            def res_phase(chunks, first_at, start):
                prev = None
                for c in chunks:
                    chunk(c, (lambda s: res_at(prev, s)) if prev else first_at, start if prev is None else 0)
                    prev = c
                if "gate" in prev.extra:
                    gate_copy(prev.idx)
                return prev._replace(extra=prev.extra.replace("gate", ""))

            def last_squares(prev, nxt):
                if nxt is not None:
                    prefill(nxt)
                res_at(prev, 4)
                if nxt is not None:
                    prefill(nxt, PRE, RING)

            prev = res_phase(even_out, lambda s: None, RING)

            def hid_copy(h, i):
                for t in range(NT):
                    act.wait_ge(hid_t, 2 * h + t + 1)
                    dst = m_hi[:, :, t * P:(t + 1) * P].rearrange("p (c k) q -> p c k q", k=4)
                    act.activation(dst[:, i, :, :], bank[B_A + t][:, :].rearrange("p (k q) -> p k q", k=4),
                                   ACT.Copy).then_inc(hid_hi, 1)

            def ffn(layer):
                prev, start = None, RING
                for gu, down in plan[f"ffn{layer}"]:
                    def gate_up(gate, up, was, start=0):
                        def gate_at(s):
                            if was is not None and was.kind == "res":
                                res_at(was, s)
                            elif was is not None and s == 5:
                                hid_copy(was.extra, was.idx)

                        def up_at(s):
                            if s == 3:
                                act.wait_ge(slab_free, gate.w0 + gate.n)
                                act.wait_ge(pair_freed[1], up.use)
                                for t in range(NT):
                                    op = act.activation(silu_g[:, t, :], bank[t][:, :], ACT.Silu)
                                op.then_inc(pair_freed[0], 1)

                        chunk(gate, gate_at, start)
                        chunk(up, up_at)

                    gate_up(*gu[0], prev, start)
                    start = 0
                    with act.Fori(0, len(gu) - 1) as i:
                        gate_up(*loop_chunks(gu, i))
                    up = gu[-1][1]
                    prev = res_phase(down, lambda s: hid_copy(up.extra, up.idx) if s == 5 else None, 0)
                return prev

            last_squares(prev, plan["ffn0"][0][0][0][0])
            norm(2, h_hi)
            act.dma_start(dft_cs, dft_d[:, 0:512].rearrange("(k p) n -> p k n", p=P)).then_inc(tab_in, 16)
            act.dma_start(dft_ns, dft_d[:, 512:768].rearrange("(k p) n -> p k n", p=P)).then_inc(tab_in, 16)
            prev = ffn(0)
            odd_in, odd_out = plan["odd_in"], plan["odd_out"]
            last_squares(prev, odd_in[0])
            norm(3, h_hi)

            def odd_at(n, prev, s):
                i = 8 * (n - 2) + s
                if i >= 4 and i % 4 == 0 and i // 4 - 1 < 4:
                    g = i // 4 - 1
                    act.wait_ge(dft_a, 2 * g + 1)
                    if g > 0:
                        act.wait_ge(dft_y, g)
                    act.activation(dft1[:, 0, :], bank[B_A][:, :], ACT.Copy).then_inc(dft_a_in, 1)
                if i >= 6 and (i - 6) % 4 == 0 and (i - 6) // 4 < 4:
                    g = (i - 6) // 4
                    act.wait_ge(dft_y, g + 1)
                    act.activation(m_hi[:, 2 * g:2 * g + 2, :],
                                   bank[B_C][:, :].rearrange("p (o t) -> p o t", o=2), ACT.Copy) \
                       .then_inc(mix_hi, 1)
                if prev is not None and s == 3:
                    half = prev.idx
                    banks = [bank[2 * prev.pair + t][:, :] for t in range(NT)]
                    if prev.kind in ("f", "cg", "bg"):
                        act.wait_ge(slab_free, prev.w0 + prev.n)
                        if prev.kind == "cg" and half == 1:
                            act.wait_ge(bg_t, 2)
                        if prev.kind == "bg":
                            act.wait_ge(u_conv_t, 2 * half + 2)
                        for t in range(NT):
                            dst = f_sb[:, t, half * NC:(half + 1) * NC] if prev.kind == "f" else odd_tmp[:, t, :]
                            op = act.activation(dst, banks[t], ACT.Copy)
                        op.then_inc(pair_freed[prev.pair], 1)
                if prev is not None and prev.kind == "bg" and s == 6:
                    mixed_hi(prev.idx)

            def mixed_hi(half):
                for b in range(2):
                    act.wait_ge(mixed, 2 * half + b + 1)
                    for j in range(2):
                        ct = 2 * b + j
                        act.activation(m_hi[:, 8 + 4 * half + ct, :], y_conv[:, ct, :], ACT.Copy) \
                           .then_inc(mix_hi, 1)

            prev = None
            for n, c in enumerate(odd_in):
                chunk(c, lambda s: odd_at(n, prev, s), RING if n == 0 else 0)
                prev = c
            prev = res_phase(odd_out, lambda s: odd_at(8, odd_in[-1], s), 0)
            last_squares(prev, plan["ffn1"][0][0][0][0])
            norm(4, h_hi)
            act.wait_ge(h_ready, 40)
            act.dma_start(final_g, final_g_d.rearrange("(a n) -> a n", a=1).broadcast_to([P, D])) \
               .then_inc(fin_in, 16)
            prev = ffn(1)
            last_squares(prev, None)

        @block.vector
        def _(dve):
            steps = 0

            def own(op):
                nonlocal steps
                op.then_inc(v_self, 1)
                steps += 1

            def own_wait():
                dve.wait_ge(v_self, steps)

            def lo(c, s):
                slot = (c.slot0 + s) % RING
                dve.wait_ge(hi_done, c.w0 + s + 1)
                dve.tensor_tensor(w_lo[:, slot, :, :], raw[:, slot, :, :], w_hi[:, slot, :, :].bitcast(f32),
                                  ALU.subtract).then_inc(lo_done, 1)

            dve.memset(ones[:, :], 1.0)
            for a in range(3):
                dve.memset(rows[:, a, :], 0.0).then_inc(cols_ready, 1)
            dve.memset(junk[:, 0:1], 0.0).then_inc(row_copied, 2)
            dve.memset(junk[:, 1:2], 0.0).then_inc(row_mm, 2)
            dve.memset(junk[:, 2:3], 0.0).then_inc(start_col, 1)
            dve.memset(junk[:, 3:4], 0.0).then_inc(hid_lo, HID_CREDIT)
            dve.wait_ge(cols_t, 1)
            dve.tensor_copy(colsA[:, :], bank[B_A][:, 0:P])
            for l in range(2):
                op = dve.tensor_copy(bias_cols[:, l * MOD_CHUNKS:(l + 1) * MOD_CHUNKS, :].rearrange(
                    "p n j -> p (n j)"), bank[B_A][:, (1 + l) * P:(1 + l) * P + 96])
            op.then_inc(cols_ready, 1)

            dve.wait_ge(rope_in, 64)

            def halves(ap):
                return ap.rearrange("p (b h q) -> p b h q", b=2, h=2)

            for a in range(2):
                g = head_g[:, a, :]
                for t in range(NT):
                    dve.tensor_tensor(fold[:, 2 * a, t, :], rope_raw[:, 0, t, :], g, ALU.mult)
                    for h in range(2):
                        op = dve.tensor_tensor(halves(fold[:, 2 * a + 1, t, :])[:, :, h, :],
                                               halves(rope_raw[:, 1, t, :])[:, :, h, :],
                                               halves(g)[:, :, 1 - h, :], ALU.mult)
            own(op)

            def rsqrt(y, x, n):
                own(dve.tensor_scalar(guess[:, 0:n], x.bitcast(i32), 1, None, ALU.logical_shift_right))
                own_wait()
                own(dve.tensor_scalar(y.bitcast(i32), guess[:, 0:n], -1.0, float(0x5F3759DF), ALU.mult,
                                      ALU.add))
                own_wait()
                for _ in range(3):
                    own(dve.tensor_tensor(newton[:, 0:n], y, y, ALU.mult))
                    own_wait()
                    own(dve.scalar_tensor_tensor(out=newton[:, 0:n], in0=newton[:, 0:n], scalar=-0.5, in1=x,
                                                 op0=ALU.mult, op1=ALU.mult))
                    own_wait()
                    own(dve.scalar_tensor_tensor(out=y, in0=newton[:, 0:n], scalar=1.5, in1=y,
                                                 op0=ALU.add, op1=ALU.mult))
                    own_wait()

            def rms_diag(nz, sq_count, norm_w, scale_cols):
                dve.wait_ge(sq_done, sq_count)
                own(dve.tensor_reduce(msq[:, :], sumsq[:, :, :], AX.X, ALU.add))
                own_wait()
                own(dve.tensor_scalar(msq[:, :], msq[:, :], 1.0 / D, EPS, ALU.mult, ALU.add))
                own_wait()
                rsqrt(rms[:, :], msq[:, :], NT)
                if nz is None:
                    return
                if nz > 0:
                    dve.wait_ge(norm_t, 8 * nz)
                for t in range(NT):
                    dve.tensor_scalar(diag[:, t, :], ident[:, :], rms[:, t:t + 1], None, ALU.mult) \
                       .then_inc(diag_ready, 1)
                own(dve.scalar_tensor_tensor(out=s_col[:, :], in0=scale_cols, scalar=1.0, in1=norm_w,
                                             op0=ALU.add, op1=ALU.mult))
                own_wait()

            def norm(nz, shift, dst_lo):
                def lo(grp):
                    dve.wait_ge(norm_hi, 8 * nz + grp + 1)
                    hi_ = (h_hi if dst_lo is h_lo else m_hi)[:, 2 * grp:2 * grp + 2, :].bitcast(f32)
                    dve.tensor_tensor(dst_lo[:, 2 * grp:2 * grp + 2, :], hf[:, grp % 2, :, :], hi_,
                                      ALU.subtract).then_inc(h_ready, 1)
                for grp in range(8):
                    if grp >= 2 or nz > 0:
                        dve.wait_ge(h_ready, 8 * nz + max(grp - 1, 0))
                    dve.wait_ge(norm_t, 8 * nz + grp + 1)
                    for j in range(2):
                        ft = 2 * grp + j
                        op = dve.tensor_scalar(hf[:, grp % 2, j, :], bank[B_A + grp % 2][:, j * T:(j + 1) * T],
                                               s_col[:, ft:ft + 1], shift[:, ft:ft + 1], ALU.mult, ALU.add)
                    op.then_inc(norm_hf, 1)
                    if grp > 0:
                        lo(grp - 1)
                lo(7)

            for s in range(RING):
                lo(plan["even_in"][0], s)
            with dve.Fori(0, ND) as i:
                for b in range(2):
                    dve.wait_ge(row_mm, 2 * i + b + 3)
                    both = bank[B_COL][:, 0:8].rearrange("p (j v) -> p j v", v=2)
                    n = i + 4 * b
                    dve.tensor_tensor(mod_cols[:, n, :], both[:, :, 0], bias_cols[:, n, :], ALU.add)
                    dve.tensor_tensor(ctx_cols[:, n, :], both[:, :, 1], bias_cols[:, n, :], ALU.add) \
                       .then_inc(start_col, 1)
            dve.wait_ge(start_col, 2 * ND + 1)

            def norm_w(layer, sub):
                o = (2 * layer + sub) * KT
                return norm_cols[:, o:o + KT]

            def mod_slab(q, sl, slot, strict):
                dve.wait_ge(mod_full[sl % RING], (q * 2 + (2 * START_CHUNKS + sl // RING + 1)) * 16)
                if sl == 0:
                    if strict:
                        dve.wait_ge(mod_mm, q)
                    elif q >= 2:
                        dve.wait_ge(mod_mm, q - 1)
                    else:
                        dve.wait_ge(row_mm, 2 * ND + 2)
                for j in range(SLAB_K):
                    k = SLAB_K * sl + j
                    w = mod_raw[:, sl % RING, j, :]
                    if k == 0:
                        dve.tensor_scalar(acc[:, slot, :], w, silu_c[:, 0, 0:1], None, ALU.mult) \
                           .then_inc(mod_step, 1)
                    else:
                        dve.wait_ge(mod_step, q * 16 + k)
                        dve.scalar_tensor_tensor(out=acc[:, slot, :], in0=w, scalar=silu_c[:, k, 0:1],
                                                 in1=acc[:, slot, :], op0=ALU.mult, op1=ALU.add) \
                           .then_inc(mod_step, 1)

            def chunk(c, at, start=0):
                total, done = 8 * len(c.mods), 0
                strict = c.kind == "gate" or c is plan["odd_in"][0]
                for s in range(start, c.n):
                    lo(c, s)
                    until = total * (s - start + 1) // (c.n - start)
                    for m in range(done, until):
                        q = c.mods[m // 8]
                        mod_slab(q, m % 8, 0 if c.kind == "gate" else q % 2, strict)
                    done = until
                    at(s)

            def prefill(c, first=0, end=PRE):
                for s in range(first, end):
                    lo(c, s)

            def mod_out(q):
                dve.wait_ge(mod_mm, q + 1)
                dve.tensor_tensor(mod_cols[:, q + START_CHUNKS, :], bank[B_COL][:, 0:4],
                                  bias_cols[:, q + START_CHUNKS, :], ALU.add).then_inc(mod_col_done, 1)

            def mods_at(c, prev, s):
                if s == 4 and prev is not None and prev.mods:
                    mod_out(prev.mods[-1])
                if s == 7 and c is not None and len(c.mods) == 2:
                    mod_out(c.mods[0])

            even_in, even_out = plan["even_in"], plan["even_out"]
            rms_diag(0, 8, norm_w(0, 0), mod_vec(0, 1))
            norm(0, mod_vec(0, 0), h_lo)
            ctx_scale = ctx_cols[:, ND:2 * ND, :].rearrange("p n j -> p (n j)")
            ctx_shift = ctx_cols[:, 0:ND, :].rearrange("p n j -> p (n j)")
            rms_diag(1, 16, norm_w(0, 0), ctx_scale)
            norm(1, ctx_shift, m_lo)

            def heads(ap):
                return ap.rearrange("p (h d) -> p h d", h=4)

            def head_rms(i):
                own(dve.tensor_scalar(head_ms[:, :, :], head_sq[:, i:i + 2, :], 1.0 / HD, EPS, ALU.mult,
                                      ALU.add))
                own_wait()
                rsqrt(head_r[:, :, :].rearrange("p t h -> p (t h)"),
                      head_ms[:, :, :].rearrange("p t h -> p (t h)"), 2 * 4)

            def head_norm(src, t):
                own(dve.tensor_tensor(heads(src), heads(src),
                                      head_r[:, t, :].unsqueeze(2).broadcast_to([P, 4, HD]), ALU.mult))
                own_wait()

            roped = 0

            def rope(src, t, a):
                nonlocal roped
                if roped:
                    dve.wait_ge(rope_done, roped)
                roped += 1
                cos = fold[:, 2 * a, t, :].unsqueeze(1).broadcast_to([P, 4, HD])
                own(dve.tensor_tensor(heads(rope_a), heads(src), cos, ALU.mult))
                quarters = "p (h b s q) -> p h b s q"
                sv = src.rearrange(quarters, h=4, b=2, s=2)
                bv = rope_b.rearrange(quarters, h=4, b=2, s=2)
                for s in range(2):
                    sin = halves(fold[:, 2 * a + 1, t, :])[:, :, s, :].unsqueeze(1).broadcast_to([P, 4, 2, 32])
                    own(dve.tensor_tensor(bv[:, :, :, s, :], sv[:, :, :, 1 - s, :], sin, ALU.mult))
                own_wait()
                return dve.tensor_tensor(src, rope_a, rope_b, ALU.add)

            def unit(i):
                if 0 <= i - 4 < 24:
                    u = i - 4
                    b = u % 2
                    dve.wait_ge(scores_done, u + 1)
                    own(dve.tensor_reduce(row_max[:, b:b + 1], bank[B_A][:, :], AX.X, ALU.max))
                    own_wait()
                    dve.tensor_scalar(neg_max[:, b:b + 1], row_max[:, b:b + 1], -SCALE, None, ALU.mult) \
                       .then_inc(max_done, 1)
                if 0 <= i - 7 < 24:
                    u = i - 7
                    dve.wait_ge(mix_hi, u + 1)
                    h, t = 4 * (u // 8) + u % 4, (u // 4) % 2
                    dve.tensor_tensor(m_lo[:, h, t * P:(t + 1) * P], bank[B_C][:, 0:P],
                                      m_hi[:, h, t * P:(t + 1) * P].bitcast(f32), ALU.subtract) \
                       .then_inc(mix_lo, 1)
                if 0 <= i - 4 < 24:
                    dve.wait_ge(exp_done, (i - 4) + 1)
                    b = (i - 4) % 2
                    own(dve.reciprocal(p_inv[:, b:b + 1], p_sum[:, b:b + 1]))
                    own_wait()
                    dve.tensor_scalar(probs[:, b, :], probs[:, b, :], p_inv[:, b:b + 1], None, ALU.mult) \
                       .then_inc(probs_done, 1)

            def even_at(n, prev, s):
                nonlocal roped
                mods_at(plan["even_in"][n], prev, s)
                if n == 1:
                    if s == 3:
                        dve.wait_ge(slab_free, prev.w0 + prev.n)
                        dve.tensor_copy(k_tmp[:, 2, :], bank[2][:, :])
                        dve.tensor_copy(k_tmp[:, 3, :], bank[3][:, :]).then_inc(pair_freed[1], 1)
                    if s >= 4:
                        i = s - 4
                        if i % 2 == 0:
                            dve.wait_ge(head_sums, i + 2)
                            head_rms(i)
                        head_norm(k_tmp[:, i, :], i % 2)
                        if i < NT:
                            rope(k_tmp[:, i, :], i, 1).then_inc(rope_done, 1)
                        else:
                            g = head_g[:, 1, :].unsqueeze(1).broadcast_to([P, 4, HD])
                            dve.tensor_tensor(heads(k_tmp[:, i, :]), heads(k_tmp[:, i, :]), g, ALU.mult) \
                               .then_inc(rope_done, 1)
                            roped = i + 1
                if n == 2 and s == 3:
                    dve.wait_ge(slab_free, prev.w0 + prev.n)
                    dve.tensor_copy(v_sb[:, 0, :], bank[2][:, :])
                    dve.tensor_copy(v_sb[:, 1, :], bank[3][:, :]).then_inc(pair_freed[1], 1)
                if n >= 3 and s in (4, 6):
                    c, t = n - 3, (s - 4) // 2
                    if t == 0:
                        dve.wait_ge(head_sums, 4 + 2 * c + 2)
                        head_rms(0)
                    head_norm(q_tmp[:, t, :], t)
                    rope(q_tmp[:, t, :], t, 0).then_inc(rope_done, 1)
                if n >= 4:
                    unit(8 * (n - 4) + s)

            prev = None
            for n, c in enumerate(even_in):
                chunk(c, lambda s: even_at(n, prev, s), RING if n == 0 else 0)
                prev = c
            for i in range(16, 32):
                if i < 16 + RING:
                    lo(even_out[0], i - 16)
                mods_at(None, prev, i - 16)
                unit(i)
            for g in range(4):
                dve.wait_ge(mix_hi, 24 + 2 * (g // 2) + 2)
                dve.scalar_tensor_tensor(out=m_lo[:, N_HEADS + g, :],
                                         in0=bank[2 + g // 2][:, (g % 2) * T:(g % 2 + 1) * T],
                                         scalar=pscale_cols[:, g:g + 1],
                                         in1=m_hi[:, N_HEADS + g, :].bitcast(f32),
                                         op0=ALU.mult, op1=ALU.subtract).then_inc(mix_lo, 1)
            gates_used = 0

            def residual(prev):
                nonlocal gates_used
                if res_no[prev.g] > 1:
                    dve.wait_ge(res_step, res_no[prev.g] - 1)
                cols = slice(prev.idx * NC, (prev.idx + 1) * NC)
                dve.wait_ge(slab_free, prev.w0 + prev.n)
                if "gate" in prev.extra:
                    gates_used += 1
                    dve.wait_ge(gb_in, gates_used)
                for t in range(NT):
                    op = dve.tensor_tensor(res_tmp[:, t, :], bank[2 * prev.pair + t][:, :], gate_bc[:, cols],
                                           ALU.mult)
                op.then_inc(pair_freed[prev.pair], 1)
                dve.wait_ge(pair_freed[prev.pair], prev.use + 1)
                for t in range(NT):
                    op = dve.tensor_tensor(x_tok[:, t, cols], x_tok[:, t, cols], res_tmp[:, t, :], ALU.add)
                op.then_inc(res_step, 1)

            def res_phase(chunks, first_at, start):
                prev = None
                for c in chunks:
                    def at(s, prev=prev):
                        if prev is None:
                            first_at(s)
                        else:
                            mods_at(c, prev, s)
                            if s == 3:
                                residual(prev)
                    chunk(c, at, start if prev is None else 0)
                    prev = c
                return prev

            def last_residual(prev, nxt):
                if nxt is not None:
                    prefill(nxt)
                residual(prev)
                if nxt is not None:
                    prefill(nxt, PRE, RING)
                mods_at(None, prev, 4)

            prev = res_phase(even_out, lambda s: dve.wait_ge(x_again, 16) if s == 7 else None, RING)
            last_residual(prev, plan["ffn0"][0][0][0][0])
            rms_diag(2, 24, norm_w(0, 1), mod_vec(0, 4))
            norm(2, mod_vec(0, 3), h_lo)

            def hid_lo_half(h, i):
                for t in range(NT):
                    dve.wait_ge(hid_hi, 2 * h + t + 1)
                    rng = (slice(None), slice(None), slice(t * P, (t + 1) * P))
                    hi_ = m_hi[rng].rearrange("p (c k) q -> p c k q", k=4)[:, i, :, :].bitcast(f32)
                    lo_ = m_lo[rng].rearrange("p (c k) q -> p c k q", k=4)[:, i, :, :]
                    dve.tensor_tensor(lo_, bank[B_A + t][:, :].rearrange("p (k q) -> p k q", k=4), hi_,
                                      ALU.subtract).then_inc(hid_lo, 1)

            def ffn(layer):
                prev, start = None, RING
                for gu, down in plan[f"ffn{layer}"]:
                    def hidden(prev, gate_use, s):
                        if s == 3:
                            dve.wait_ge(slab_free, prev.w0 + prev.n)
                            dve.wait_ge(pair_freed[0], gate_use + 1)
                            for t in range(NT):
                                op = dve.tensor_tensor(hid_tok[:, t, :], silu_g[:, t, :],
                                                       bank[2 + t][:, :], ALU.mult)
                            op.then_inc(pair_freed[1], 1)
                        if s == 5:
                            hid_lo_half(prev.extra, prev.idx)

                    def gate_up(gate, up, was, start=0):
                        def gate_at(s):
                            if was is None:
                                return
                            if was.kind == "up":
                                hidden(was, gate.use - 1, s)
                            elif s == 3:
                                residual(was)
                        chunk(gate, gate_at, start)
                        chunk(up, lambda s: mods_at(None, gate, s))

                    gate_up(gu[0][0], gu[0][1], prev, start)
                    start = 0
                    with dve.Fori(0, len(gu) - 1) as i:
                        gate_up(*loop_chunks(gu, i))
                    last_gate, last_up = gu[-1]
                    prev = res_phase(down, lambda s: hidden(last_up, last_gate.use, s), 0)
                return prev

            prev = ffn(0)
            last_residual(prev, plan["odd_in"][0])
            rms_diag(3, 32, norm_w(1, 0), mod_vec(1, 1))
            norm(3, mod_vec(1, 0), h_lo)

            def odd_at(n, prev, s):
                mods_at(plan["odd_in"][n] if n < 8 else None, prev, s)
                i = 8 * (n - 2) + s
                if i >= 4 and i % 4 == 0 and i // 4 - 1 < 4:
                    g = i // 4 - 1
                    dve.wait_ge(dft_a, 2 * g + 2)
                    if g > 0:
                        dve.wait_ge(dft_y, g)
                    dve.wait_ge(dft_a_in, 2 * g + 1)
                    dve.tensor_copy(dft1[:, 1, :], bank[B_B][:, :]).then_inc(dft_a_in, 1)
                if i >= 6 and (i - 6) % 4 == 0 and (i - 6) // 4 < 4:
                    g = (i - 6) // 4
                    dve.wait_ge(mix_hi, EVEN_MIX + g + 1)
                    dve.tensor_tensor(m_lo[:, 2 * g:2 * g + 2, :],
                                      bank[B_C][:, :].rearrange("p (o t) -> p o t", o=2),
                                      m_hi[:, 2 * g:2 * g + 2, :].bitcast(f32), ALU.subtract) \
                       .then_inc(mix_lo, 1)
                if prev is None:
                    return
                half = prev.idx
                if prev.kind == "xin" and s == 3:
                    dve.wait_ge(slab_free, prev.w0 + prev.n)
                    cg = plan["odd_in"][n - 2]
                    dve.wait_ge(pair_freed[cg.pair], cg.use + 1)
                    for t in range(NT):
                        op = dve.tensor_tensor(odd_tmp[:, t, :], odd_tmp[:, t, :],
                                               bank[2 * prev.pair + t][:, :], ALU.mult)
                    op.then_inc(pair_freed[prev.pair], 1)
                if n < 8 and plan["odd_in"][n].kind == "bg" and s == 6:
                    conv(plan["odd_in"][n].idx)
                if prev.kind == "bg" and s == 5:
                    for b in range(2):
                        dve.wait_ge(bg_t, 2 * half + b + 1)
                        op = dve.tensor_tensor(y_conv[:, 2 * b:2 * b + 2, :], y_conv[:, 2 * b:2 * b + 2, :],
                                               bank[B_A + b][:, :].rearrange("p (j t) -> p j t", j=2),
                                               ALU.mult)
                        op.then_inc(mixed, 1)
                if prev.kind == "bg" and s == 6:
                    for ct in range(4):
                        dve.wait_ge(mix_hi, EVEN_MIX + DFT_MIX + 4 * half + ct + 1)
                        m = 8 + 4 * half + ct
                        dve.tensor_tensor(m_lo[:, m, :], y_conv[:, ct, :], m_hi[:, m, :].bitcast(f32),
                                          ALU.subtract).then_inc(mix_lo, 1)

            def conv(half):
                for ct in range(4):
                    if ct % 2 == 0:
                        dve.wait_ge(u_conv_t, 2 * half + ct // 2 + 1)
                    u = bank[B_A + ct // 2][:, (ct % 2) * T:(ct % 2 + 1) * T]
                    y = y_conv[:, ct, :]
                    k = 4 * half + ct
                    w = [conv_cols[:, 8 * j + k:8 * j + k + 1] for j in range(3)]
                    own(dve.tensor_scalar(y, u, w[1], None, ALU.mult))
                    own_wait()
                    own(dve.scalar_tensor_tensor(out=y[:, 1:T], in0=u[:, 0:T - 1], scalar=w[0],
                                                 in1=y[:, 1:T], op0=ALU.mult, op1=ALU.add))
                    own_wait()
                    dve.scalar_tensor_tensor(out=y[:, 0:T - 1], in0=u[:, 1:T], scalar=w[2],
                                             in1=y[:, 0:T - 1], op0=ALU.mult, op1=ALU.add) \
                       .then_inc(conv_done, 1)
                dve.wait_ge(conv_done, 4 * half + 4)

            prev = None
            for n, c in enumerate(plan["odd_in"]):
                chunk(c, lambda s: odd_at(n, prev, s), RING if n == 0 else 0)
                prev = c
            prev = res_phase(plan["odd_out"], lambda s: odd_at(8, plan["odd_in"][-1], s), 0)
            last_residual(prev, plan["ffn1"][0][0][0][0])
            rms_diag(4, 40, norm_w(1, 1), mod_vec(1, 4))
            norm(4, mod_vec(1, 3), h_lo)
            prev = ffn(1)
            last_residual(prev, None)
            rms_diag(None, 48, None, None)
            dve.wait_ge(fin_in, 16)
            for n in range(ND):
                for t in range(NT):
                    cols = slice(n * NC, (n + 1) * NC)
                    op = dve.scalar_tensor_tensor(out=x_tok[:, t, cols], in0=x_tok[:, t, cols],
                                                  scalar=rms[:, t:t + 1], in1=final_g[:, cols],
                                                  op0=ALU.mult, op1=ALU.mult)
                op.then_inc(x_final, 1)


def tables():
    f = np.float32
    quarter = HD // 4
    grid_w = 64
    freqs = f(10000.0) ** (-np.arange(quarter, dtype=f) / f(quarter))
    pos = np.arange(T)
    ang = np.stack([(pos // grid_w).astype(f)[:, None] * freqs, (pos % grid_w).astype(f)[:, None] * freqs], 1)
    cos, sin = np.cos(ang).astype(f), np.sin(ang).astype(f)
    rope_cos = np.stack([cos, cos], 2).reshape(T, HD)
    rope_sin = np.stack([-sin, sin], 2).reshape(T, HD)
    pool = np.zeros((4, T, T), f)
    for g, w in enumerate((2, 4, 8, 16)):
        for t in range(T):
            lo, hi = max(t - w // 2, 0), min(t - w // 2 + w, T)
            pool[g, lo:hi, t] = f(1) / f(hi - lo)
            pool[g, t, t] -= f(1)
    a = 2 * np.pi * ((np.arange(T)[:, None] * np.arange(T)[None, :]) % T) / T
    c, s = np.cos(a) / 16, np.sin(a) / 16
    dft = np.concatenate([c, s, -s], 1).astype(f)
    return {"rope_cos": rope_cos, "rope_sin": rope_sin, "pool_mat": pool, "dft": dft}


_INS = ["x", "c", "ctx", "c_ctx", "norm_g", "w_mod", "b_mod", "w_in_even", "w_out_even", "q_norm_g",
        "k_norm_g", "w_pool", "pool_scale", "w_in_odd", "w_out_odd", "conv_w", "w_ffn_gate", "w_ffn_up",
        "w_ffn_down", "final_g"]


def kernel(**inputs):
    import concourse.bacc as bacc
    from concourse.bass_utils import run_bass_kernel_spmd

    nc = bacc.Bacc("TRN2", target_bir_lowering=False, num_devices=1)
    given = {n: np.ascontiguousarray(inputs[n]) for n in _INS}
    given.update(tables())
    arrays, args = {}, []
    for name, a in given.items():
        arrays[f"in_{name}"] = a
        args.append(nc.dram_tensor(f"in_{name}", a.shape, mybir.dt.from_np(a.dtype), kind="ExternalInput").ap())
    args.append(nc.dram_tensor("out_0", (1, T, D), mybir.dt.float32, kind="ExternalOutput").ap())
    build(nc, *args)
    r = run_bass_kernel_spmd(nc, [arrays], core_ids=[0])
    return r.results[0]["out_0"]
```

```python
from contextlib import ExitStack
from collections import namedtuple

import numpy as np

import concourse.bass as bass
from concourse import mybir

P = 128
D = 2048
KT = D // P
T = 256
NT = T // P
NC = 512
ND = D // NC
DFF = 5632
SLAB_K = 2
RING = 4
N_HEADS, N_KV, HD = 12, 4, 128
SCALE = float(HD) ** -0.5
EPS = 1e-6
SPLITS = (4, 4, 3)
START_CHUNKS = 8
MOD_CHUNKS = 6 * D // NC
PRE = 3

Chunk = namedtuple("Chunk", "kind w0 slot0 round0 n g pair use mods idx extra")


class Plan:

    def __init__(self):
        self.w = self.g = self.q = 0
        self.uses = [0, 0]

    def pair_use(self, pair):
        self.uses[pair] += 1
        return self.uses[pair] - 1

    def chunk(self, kind, idx, pair, n=8, mods=0, extra=None, both=False):
        c = Chunk(kind, self.w, self.w % RING, self.w // RING, n, self.g, pair, self.uses[pair],
                  tuple(range(self.q, self.q + mods)), idx, extra)
        self.w += n
        self.g += 1
        self.q += mods
        self.uses[pair] += 1
        if both:
            self.uses[1 - pair] += 1
        return c


def moved(c, i, w, g, use, q, idx):
    return c._replace(w0=c.w0 + i * w, round0=c.round0 + i * (w // RING), g=c.g + i * g,
                      use=c.use + i * use, mods=tuple(m + i * q for m in c.mods), idx=c.idx + i * idx)


def make_plan():
    p = Plan()
    plan = {}
    plan["even_in"] = [p.chunk("k", 0, 0, both=True), p.chunk("v", 0, 0, mods=2, both=True),
                       p.chunk("q", 0, 0, mods=2), p.chunk("q", 1, 1, mods=1),
                       p.chunk("q", 2, 0, mods=1), p.chunk("u", 0, 1, mods=1)]
    plan["pool_use"] = (p.pair_use(0), p.uses[1])
    plan["rest_mods"] = (p.q, p.q + 1)
    p.q += 2
    plan["even_out"] = [p.chunk("res", n, n % 2, mods=1, extra="stats gate") for n in range(ND)]
    h = 0
    for layer in range(2):
        splits = []
        for sp, nch in enumerate(SPLITS):
            mods = 1 if layer == 0 or sp == 0 else 0
            gu = []
            for i in range(nch):
                gu.append((p.chunk("gate", i, 0, mods=mods), p.chunk("up", i, 1, extra=h)))
                h += 1
            ex = ("gate" if sp == 0 else "") + (" stats" if sp == len(SPLITS) - 1 else "")
            down = [p.chunk("res", n, n % 2, n=2 * nch, extra=ex) for n in range(ND)]
            splits.append((gu, down))
        plan[f"ffn{layer}"] = splits
        if layer == 0:
            odd = [("f", 0), ("f", 1), ("cg", 0), ("xin", 0), ("bg", 0), ("cg", 1), ("xin", 1), ("bg", 1)]
            plan["odd_in"] = [p.chunk(k, i, n % 2, mods=1) for n, (k, i) in enumerate(odd)]
            plan["odd_out"] = [p.chunk("res", n, n % 2, mods=1, extra="stats gate") for n in range(ND)]
    assert p.q == 2 * MOD_CHUNKS - START_CHUNKS, p.q
    return plan, p.w


def build(nc, x_d, c_d, ctx_d, c_ctx_d, norm_g_d, w_mod_d, b_mod_d, w_in_e_d, w_out_e_d, q_g_d, k_g_d,
          w_pool_d, pool_scale_d, w_in_o_d, w_out_o_d, conv_w_d, w_gate_d, w_up_d, w_down_d, final_g_d,
          rope_cos_d, rope_sin_d, pool_mat_d, dft_d, out_d):
    f32, f32r, i32 = mybir.dt.float32, mybir.dt.float32r, mybir.dt.int32
    ALU, ACT, AX = mybir.AluOpType, mybir.ActivationFunctionType, mybir.AxisListType
    plan, n_slabs = make_plan()

    def slabs(w):
        return w.rearrange("(s j p) (n c) -> n s p j c", p=P, j=SLAB_K, c=NC)

    wv_in_e, wv_out_e = slabs(w_in_e_d[0]), slabs(w_out_e_d[0])
    wv_in_o, wv_out_o = slabs(w_in_o_d[0]), slabs(w_out_o_d[0])
    wv_gate = [slabs(w_gate_d[l]) for l in range(2)]
    wv_up = [slabs(w_up_d[l]) for l in range(2)]
    wv_down = [slabs(w_down_d[l]) for l in range(2)]
    wv_mod = [slabs(w_mod_d[l]) for l in range(2)]
    even_col = {"q": 0, "k": 3, "v": 4, "u": 5}
    odd_col = {"f": 0, "bg": 2, "cg": 4, "xin": 6}

    with ExitStack() as stack:
        def sb(name, shape, dt=f32):
            return stack.enter_context(nc.sbuf_tensor(name, shape, dt))

        def sem(name):
            return stack.enter_context(nc.semaphore(name))

        x_tok = sb("x_tok", [P, NT, D])
        h_hi, h_lo = sb("h_hi", [P, KT, T], f32r), sb("h_lo", [P, KT, T], f32r)
        m_hi, m_lo = sb("m_hi", [P, KT, T], f32r), sb("m_lo", [P, KT, T], f32r)
        raw = sb("raw", [P, RING, SLAB_K, NC])
        w_hi, w_lo = sb("w_hi", [P, RING, SLAB_K, NC], f32r), sb("w_lo", [P, RING, SLAB_K, NC], f32r)
        mod_raw = sb("mod_raw", [P, RING, SLAB_K, NC])
        acc = sb("acc", [P, 2, NC])
        gate_bc = sb("gate_bc", [P, D])
        scratch = sb("scratch", [P, 6144])
        tables = sb("tables", [P, 2560])
        junk = sb("junk", [P, NC])
        ident, ones = sb("ident", [P, P]), sb("ones", [P, 1])
        rows = sb("rows", [P, 4, P])
        colsA = sb("colsA", [P, P])
        bias_cols = sb("bias_cols", [P, 2 * MOD_CHUNKS, 4])
        mod_cols = sb("mod_cols", [P, 2 * MOD_CHUNKS, 4])
        ctx_cols = sb("ctx_cols", [P, START_CHUNKS, 4])
        silu_c = sb("silu_c", [P, KT, 2])
        s_col = sb("s_col", [P, 2, KT])
        sumsq = sb("sumsq", [P, 2, NT, ND])
        msq = sb("msq", [P, 2, NT])
        rms = sb("rms", [P, 2, NT])
        head_sq = sb("head_sq", [P, 4, 4])
        head_ms = sb("head_ms", [P, NT, 4])
        head_r = sb("head_r", [P, NT, 4])
        junk2 = sb("junk2", [P, NT])
        guess, newton = sb("guess", [P, 8], mybir.dt.int32), sb("newton", [P, 8])
        neg_max = sb("neg_max", [P, 2])
        row_max = sb("row_max", [P, 2])
        p_sum = sb("p_sum", [P, 2])
        p_inv = sb("p_inv", [P, 2])

        ctx_tok = scratch[:, 0:4096].rearrange("p (t n) -> p t n", t=NT)
        hf = scratch[:, 4096:5120].rearrange("p (b j t) -> p b j t", b=2, j=2)
        x_norm = scratch[:, 5120:6144].rearrange("p (b t n) -> p b t n", b=2, t=NT)
        kt_sb = x_tok[:, 0, :].rearrange("p (h k) -> p h k", h=N_KV)
        v_sb = x_tok[:, 1, :].rearrange("p (k n) -> p k n", k=4)
        qt = scratch[:, 0:2048].rearrange("p (c h t) -> p c h t", c=2, h=4)
        k_tmp = scratch[:, 0:2048].rearrange("p (i n) -> p i n", i=4)
        q_tmp = scratch[:, 2048:3072].rearrange("p (t n) -> p t n", t=NT)
        rope_a, rope_b = scratch[:, 3072:3584], scratch[:, 3584:4096]
        probs = scratch[:, 4096:5120].rearrange("p (b k) -> p b k", b=2)
        probs_t = scratch[:, 5120:6144].rearrange("p (b k t) -> p b k t", b=2, k=4)
        u_sb = q_tmp
        pooled = scratch[:, 3072:4096].rearrange("p (g t) -> p g t", g=4)
        fold = gate_bc[:, 0:1024].rearrange("p (a t d) -> p a t d", a=4, t=NT)
        rope_raw = gate_bc[:, 1024:1536].rearrange("p (a t d) -> p a t d", a=2, t=NT)
        head_g = gate_bc[:, 1536:1792].rearrange("p (a d) -> p a d", a=2)
        pool_mat = tables[:, 0:2048].rearrange("p (g k t) -> p g k t", g=4, k=NT)
        w_pool = tables[:, 2048:2560].rearrange("p (g d) -> p g d", g=4)
        dft_cs = tables[:, 0:1024].rearrange("p (k n) -> p k n", k=2)
        dft_ns = tables[:, 1024:1536].rearrange("p (k n) -> p k n", k=2)
        silu_g = scratch[:, 0:1024].rearrange("p (t n) -> p t n", t=NT)
        hid_tok = scratch[:, 1024:2048].rearrange("p (t n) -> p t n", t=NT)
        res_tmp = scratch[:, 2048:3072].rearrange("p (t n) -> p t n", t=NT)
        final_g = scratch[:, 4096:6144]
        f_sb = scratch[:, 0:2048].rearrange("p (t n) -> p t n", t=NT)
        y_conv = scratch[:, 0:1024].rearrange("p (c t) -> p c t", c=4)
        odd_tmp = scratch[:, 3072:4096].rearrange("p (t n) -> p t n", t=NT)
        dft1 = scratch[:, 5120:6144].rearrange("p (q n) -> p q n", q=2)

        start_raw = [mod_raw[:, s, :, :] for s in range(RING)] + \
            [v[:, i * 1024:(i + 1) * 1024].rearrange("p (j n) -> p j n", j=SLAB_K)
             for v in (gate_bc, tables) for i in range(2)]

        norm_cols = colsA[:, 0:64]
        conv_cols = colsA[:, 64:88]
        pscale_cols = colsA[:, 88:92]

        def mod_vec(layer, v):
            n = layer * MOD_CHUNKS + v * ND
            return mod_cols[:, n:n + ND, :].rearrange("p n j -> p (n j)")

        bank = [stack.enter_context(nc.psum_tensor(f"bank{i}", [P, NC], f32)) for i in range(8)]
        B_COL, B_A, B_B, B_C = 4, 5, 6, 7

        raw_full = [sem(f"raw_full{i}") for i in range(RING)]
        hi_done, lo_done, slab_free = sem("hi_done"), sem("lo_done"), sem("slab_free")
        mod_full = [sem(f"mod_full{i}") for i in range(RING)]
        start_full = mod_full + [sem(f"start_full{i}") for i in range(RING, 8)]
        mod_step = sem("mod_step")
        mod_mm, mod_col_done = sem("mod_mm"), sem("mod_col_done")
        start_free, row_copied, row_mm, start_col = (
            sem("start_free"), sem("row_copied"), sem("row_mm"), sem("start_col"))
        pair_freed = [sem("pair0_freed"), sem("pair1_freed")]
        rows_in, x_in, rope_in, tab_in, wpool_in, x_again, fin_in, out_done = (
            sem("rows_in"), sem("x_in"), sem("rope_in"), sem("tab_in"), sem("wpool_in"),
            sem("x_again"), sem("fin_in"), sem("out_done"))
        c_in, c_t = sem("c_in"), sem("c_t")
        ident_ready, cols_t, cols_ready, silu_ready = (
            sem("ident_ready"), sem("cols_t"), sem("cols_ready"), sem("silu_ready"))
        sq_done, rms_ready, norm_x, norm_t, norm_hf, norm_hi, h_ready = (
            sem("sq_done"), sem("rms_ready"), sem("norm_x"), sem("norm_t"), sem("norm_hf"), sem("norm_hi"),
            sem("h_ready"))
        v_self = sem("v_self")
        head_sums, rope_done = sem("head_sums"), sem("rope_done")
        kt_t, kt_in, qt_t, qt_in = sem("kt_t"), sem("kt_in"), sem("qt_t"), sem("qt_in")
        scores_done, max_done, exp_done, probs_done = (
            sem("scores_done"), sem("max_done"), sem("exp_done"), sem("probs_done"))
        pt_t, pt_in, pv_done, mix_hi, mix_lo = (
            sem("pt_t"), sem("pt_in"), sem("pv_done"), sem("mix_hi"), sem("mix_lo"))
        pool_mm = sem("pool_mm")
        gb_mm, gb_in = sem("gb_mm"), sem("gb_in")
        res_step = sem("res_step")
        hid_t, hid_hi, hid_lo = sem("hid_t"), sem("hid_hi"), sem("hid_lo")
        dft_a, dft_a_in, dft_y, u_conv_t, conv_done, bg_t, mixed = (
            sem("dft_a"), sem("dft_a_in"), sem("dft_y"), sem("u_conv_t"), sem("conv_done"), sem("bg_t"),
            sem("mixed"))
        x_final = sem("x_final")

        block = stack.enter_context(nc.Block())

        order = plan["even_out"] + [c for _, d in plan["ffn0"] for c in d] + plan["odd_out"] \
            + [c for _, d in plan["ffn1"] for c in d]
        res_no = {c.g: n + 1 for n, c in enumerate(order)}

        EVEN_MIX = 24 + 4
        DFT_MIX = 4
        HID_CREDIT = 2

        def loop_chunks(gu, i):
            (gate, up), was = gu[1], gu[0][1]
            return (moved(gate, i, 16, 2, 1, 1, 1),
                    moved(up, i, 16, 2, 1, 0, 1)._replace(extra=up.extra + i),
                    moved(was, i, 16, 2, 1, 0, 1)._replace(extra=was.extra + i))

        def norm_groups(k):
            if k == 0:
                return [(n, n // 2, n % 2) for n in range(16)]
            return [(16 + 8 * (k - 1) + g, g, 0) for g in range(8)]

        def norm_first(k):
            return norm_groups(k)[:2]

        def start_groups(i):
            return norm_groups(0)[4 * i:4 * i + 4]

        def norm_side(k, s):
            return norm_groups(k)[2 + 2 * s:4 + 2 * s]

        def norm_source(which):
            return (x_tok, ctx_tok)[which]

        def start_col_chunk(m):
            return m // 2 + ND * (m % 2)

        def acc_slot(c):
            return 0 if c.kind == "gate" else c.mods[-1] % 2

        @block.sync
        def _(sp):
            sp.wait_ge(cols_ready, 4)
            for src, r in ((c_d.rearrange("b (k p) -> (b k) p", p=P), 0),
                           (c_ctx_d.rearrange("(k p) -> k p", p=P), 16)):
                sp.dma_start(rows[r:r + 16, 3, :], src).then_inc(c_in, 16)
            for src, a, r, n in ((norm_g_d.rearrange("l s (k p) -> (l s k) p", p=P), 0, 0, 64),
                                 (conv_w_d.rearrange("o j (k p) -> (o j k) p", p=P), 0, 64, 24),
                                 (pool_scale_d.rearrange("o (k p) -> (o k) p", p=P), 0, 88, 4),
                                 (b_mod_d[0].rearrange("(k p) -> k p", p=P), 1, 0, 96),
                                 (b_mod_d[1].rearrange("(k p) -> k p", p=P), 2, 0, 96)):
                sp.dma_start(rows[r:r + n, a, :], src).then_inc(rows_in, 16)
            def load(c, view, col, row0=0):
                for s in range(c.n):
                    load_slab(c, s, view[col, row0 + s])

            def load_slab(c, s, src):
                if not isinstance(c.w0, int) or c.w0 + s >= RING:
                    sp.wait_ge(lo_done, c.w0 + (s - RING + 1))
                slot = (c.slot0 + s) % RING
                sp.dma_start(raw[:, slot, :, :], src).then_inc(raw_full[slot], 16)

            keys = plan["even_in"][0]
            for m in range(START_CHUNKS):
                for s in range(RING, 8):
                    if m > 0:
                        sp.wait_ge(start_free, 8 * (m - 1) + s + 1)
                    sp.dma_start(start_raw[s], wv_mod[0][start_col_chunk(m), s]).then_inc(start_full[s], 16)
                if m == 0:
                    sp.dma_start(x_tok[:, :, :], x_d[0].rearrange("(t p) n -> p t n", p=P)).then_inc(x_in, 16)
                    sp.dma_start(ctx_tok, ctx_d[0].rearrange("(t p) n -> p t n", p=P)).then_inc(x_in, 16)
                else:
                    load_slab(keys, m - 1, wv_in_e[even_col["k"], m - 1])
            load_slab(keys, 7, wv_in_e[even_col["k"], 7])

            def ffn(layer):
                first = 0
                for gu, down in plan[f"ffn{layer}"]:
                    with sp.Fori(0, len(gu)) as i:
                        for c, view in zip(gu[0], (wv_gate, wv_up)):
                            load(moved(c, i, 16, 2, 1, 0, 1), view[layer], first + i)
                    for c in down:
                        load(c, wv_down[layer], c.idx, 2 * first)
                    first += len(gu)

            for c in plan["even_in"][1:]:
                load(c, wv_in_e, even_col[c.kind] + c.idx)
            for c in plan["even_out"]:
                load(c, wv_out_e, c.idx)
                if c.idx == 0:
                    sp.wait_ge(pv_done, 24)
                    sp.dma_start(x_tok[:, :, :], x_d[0].rearrange("(t p) n -> p t n", p=P)) \
                      .then_inc(x_again, 16)
            ffn(0)
            for c in plan["odd_in"]:
                load(c, wv_in_o, odd_col[c.kind] + c.idx)
            for c in plan["odd_out"]:
                load(c, wv_out_o, c.idx)
            ffn(1)
            for n in range(ND):
                sp.wait_ge(x_final, n + 1)
                sp.dma_start(out_d[0].rearrange("(t p) n -> p t n", p=P)[:, :, n * NC:(n + 1) * NC],
                             x_tok[:, :, n * NC:(n + 1) * NC]).then_inc(out_done, 16)
            sp.wait_ge(out_done, 16 * ND)

        @block.gpsimd
        def _(pool):
            def load_mod(view, n, s, slot):
                pool.dma_start(mod_raw[:, slot, :, :], view[n, s]).then_inc(mod_full[slot], 16)

            pool.memset(ident[:, :], 0.0).then_inc(ident_ready, 1)
            pool.wait_ge(ident_ready, 1)
            pool.affine_select(out=ident[:, :], in_=ident[:, :], compare_op=ALU.not_equal, fill=1.0,
                               base=0, pattern=[[-1, P]], channel_multiplier=1).then_inc(ident_ready, 1)
            for s in range(RING):
                load_mod(wv_mod[0], 0, s, s)
            with pool.Fori(0, ND - 1) as i:
                for b, n in ((0, i + ND), (1, i + 1)):
                    for s in range(RING):
                        pool.wait_ge(start_free, i * 16 + (8 * b + s + 1))
                        load_mod(wv_mod[0], n, s, s)
            for b, n in ((0, START_CHUNKS - 1), (1, START_CHUNKS)):
                for s in range(RING):
                    pool.wait_ge(start_free, (ND - 1) * 16 + 8 * b + s + 1)
                    load_mod(wv_mod[0], n, s, s)

            def stream(layer, n0, count, q0):
                with pool.Fori(0, count) as i:
                    for s in range(8):
                        pool.wait_ge(mod_step, (i + q0) * 16 + 2 * (s - RING + 1))
                        load_mod(wv_mod[layer], i + n0, s, s % RING)

            n_rest = MOD_CHUNKS - START_CHUNKS
            for s in range(RING, 8):
                pool.wait_ge(mod_step, 2 * (s - RING + 1))
                load_mod(wv_mod[0], START_CHUNKS, s, s % RING)
            stream(0, START_CHUNKS + 1, n_rest - 1, 1)
            stream(1, 0, MOD_CHUNKS, n_rest)

        @block.tensor
        def _(pe):
            drained = {}

            def take(b, reader, value):
                if b in drained:
                    pe.wait_ge(*drained[b])
                drained[b] = (reader, value)

            pe.wait_ge(ident_ready, 2)
            pe.wait_ge(cols_ready, 4)
            pe.wait_ge(c_in, 32)
            pe.transpose(bank[B_B][:, 0:P], rows[:, 3, :], ident[:, :]).then_inc(c_t, 1)
            pe.wait_ge(rows_in, 16 * 5)
            for a in range(3):
                op = pe.transpose(bank[B_A][:, a * P:(a + 1) * P], rows[:, a, :], ident[:, :])
            op.then_inc(cols_t, 1)
            pe.wait_ge(silu_ready, 2)
            def matvec(m):
                if m > 0:
                    pe.wait_ge(row_copied, m)
                for s in range(8):
                    pe.wait_ge(start_full[s], (m + 1) * 16)
                    for j in range(SLAB_K):
                        k = SLAB_K * s + j
                        op = pe.matmul(bank[B_C][0:2, :], silu_c[:, k, :], start_raw[s][:, j, :],
                                       start=(k == 0), stop=(k == KT - 1))
                    op.then_inc(start_free, 1)

            def row_to_cols(m):
                pe.wait_ge(row_copied, m + 1)
                if m > 0:
                    pe.wait_ge(start_col, m)
                for j in range(4):
                    op = pe.matmul(bank[B_COL][:, 2 * j:2 * j + 2], acc[0:2, m % 2, j * P:(j + 1) * P],
                                   ident[0:2, 0:2], start=True, stop=True)
                op.then_inc(row_mm, 1)

            def norm_turn(groups):
                for n, _, _ in groups:
                    b = B_A + n % 2
                    pe.wait_ge(norm_x, n + 1)
                    take(b, norm_hf, n + 1)
                    for j in range(2):
                        for t in range(NT):
                            op = pe.transpose(bank[b][:, j * T + t * P:j * T + (t + 1) * P],
                                              x_norm[:, n % 2, t, j * P:(j + 1) * P], ident[:, :])
                    op.then_inc(norm_t, 1)

            def h_waits(k):
                base = norm_groups(k)[0][0]
                return {s: [(h_ready, base + s + 1)] for s in range(8)}

            def mod_columns(q, slot):
                take(B_COL, mod_col_done, q + 1)
                pe.wait_ge(mod_step, (q + 1) * 16)
                for j in range(4):
                    op = pe.matmul(bank[B_COL][:, j:j + 1], acc[:, slot, j * P:(j + 1) * P], ones[:, :],
                                   start=True, stop=True)
                op.then_inc(mod_mm, 1)

            def gemm_slab(c, s, groups):
                pe.wait_ge(lo_done, c.w0 + s + 1)
                slot = (c.slot0 + s) % RING
                for j in range(SLAB_K):
                    k = SLAB_K * s + j
                    for a_hi, a_lo, pair in groups:
                        for t in range(NT):
                            ps = bank[2 * pair + t][:, :]
                            ah, al = a_hi[:, k, t * P:(t + 1) * P], a_lo[:, k, t * P:(t + 1) * P]
                            last = s == c.n - 1 and j == SLAB_K - 1
                            pe.matmul(ps, ah, w_hi[:, slot, j, :], start=(k == 0), stop=False)
                            pe.matmul(ps, ah, w_lo[:, slot, j, :], start=False, stop=False)
                            op = pe.matmul(ps, al, w_hi[:, slot, j, :], start=False, stop=last)
                op.then_inc(slab_free, 1)

            def gemm(c, hi, lo, side, ready=None, both=None):
                groups = [(hi, lo, c.pair)]
                if both:
                    groups.append((*both, 1 - c.pair))
                for _, _, pair in groups:
                    if not isinstance(c.use, int) or c.use > 0:
                        pe.wait_ge(pair_freed[pair], c.use)
                for s in range(c.n):
                    if ready and s in ready:
                        for w in ready[s]:
                            pe.wait_ge(*w)
                    gemm_slab(c, s, groups)
                    side(s)

            def mods_at(c, prev, s):
                if s == 0 and prev is not None and prev.mods:
                    mod_columns(prev.mods[-1], acc_slot(prev))
                if s == 4 and c is not None and len(c.mods) == 2:
                    mod_columns(c.mods[0], c.mods[0] % 2)

            def gate_columns(layer, v, n, value):
                take(B_C, gb_in, value)
                g = mod_vec(layer, v)
                if n == 0:
                    pe.wait_ge(mod_col_done, layer * MOD_CHUNKS + (v + 1) * ND - START_CHUNKS)
                for j in range(4):
                    ft = 4 * n + j
                    op = pe.matmul(bank[B_C][:, j * P:(j + 1) * P], g[:, ft:ft + 1].broadcast_to([P, P]),
                                   ident[:, :], start=True, stop=True)
                op.then_inc(gb_mm, 1)

            def transposes(bk, src, count, sem_):
                for j in range(count):
                    op = pe.transpose(bank[bk][:, j * P:(j + 1) * P], src(j), ident[:, :])
                op.then_inc(sem_, 1)

            def key_slab(s):
                pe.wait_ge(h_ready, 2 * s + 2)
                gemm_slab(plan["even_in"][0], s, [(h_hi, h_lo, 0), (m_hi, m_lo, 1)])

            drained[B_A] = (cols_ready, 5)
            for i in range(ND):
                matvec(2 * i)
                if i > 0:
                    key_slab(2 * i - 2)
                row_to_cols(2 * i)
                matvec(2 * i + 1)
                if i > 0:
                    key_slab(2 * i - 1)
                row_to_cols(2 * i + 1)
                norm_turn(start_groups(i))
            drained[B_COL] = (start_col, START_CHUNKS)
            drained[B_C] = (row_copied, START_CHUNKS)
            for s in range(6, 8):
                key_slab(s)

            def unit(i):
                if 0 <= i - 3 < 24:
                    u = i - 3
                    pe.wait_ge(pt_in, u + 1)
                    take(B_C, mix_lo, u + 1)
                    kv = (4 * (u // 8) + u % 4) // 3
                    for k in range(4):
                        op = pe.matmul(bank[B_C][:, 0:P], v_sb[:, k, kv * P:(kv + 1) * P],
                                       probs_t[:, u % 2, k, :], start=(k == 0), stop=(k == 3))
                    op.then_inc(pv_done, 1)
                if 0 <= i - 2 < 24:
                    u = i - 2
                    pe.wait_ge(probs_done, u + 1)
                    take(B_B, pt_in, u + 1)
                    transposes(B_B, lambda j: probs[:, u % 2, j * P:(j + 1) * P], 4, pt_t)
                if 0 <= i < 24:
                    c, t, h = i // 8, (i // 4) % 2, i % 4
                    if i == 0:
                        pe.wait_ge(kt_in, 4)
                    pe.wait_ge(qt_in, 2 * c + t + 1)
                    take(B_A, exp_done, i + 1)
                    pe.matmul(bank[B_A][:, :], qt[:, c % 2, h, t * P:(t + 1) * P],
                              kt_sb[:, (4 * c + h) // 3, :], start=True, stop=True).then_inc(scores_done, 1)

            def q_turn(c, t):
                pe.wait_ge(rope_done, 4 + 2 * c + t + 1)
                take(B_COL, qt_in, 2 * c + t + 1)
                transposes(B_COL, lambda j: q_tmp[:, t, j * P:(j + 1) * P], 4, qt_t)

            prev = plan["even_in"][0]
            for n, c in enumerate(plan["even_in"][1:], 1):
                def side(s, c=c, n=n, prev=prev):
                    mods_at(c, prev, s)
                    if n == 2 and s < 4:
                        pe.wait_ge(rope_done, s + 1)
                        take(B_B, kt_in, s + 1)
                        transposes(B_B, lambda j: k_tmp[:, s, j * P:(j + 1) * P], 4, kt_t)
                    if n >= 3 and s in (5, 7):
                        q_turn(n - 3, (s - 5) // 2)
                    if n >= 4:
                        unit(8 * (n - 4) + s)
                gemm(c, h_hi, h_lo, side, both=(m_hi, m_lo) if n < 2 else None)
                prev = c
            pool_use, rest = plan["pool_use"], plan["rest_mods"]
            for i in range(16, 28):
                mods_at(None, prev, i - 16)
                if i == 24:
                    pe.wait_ge(pair_freed[prev.pair], prev.use + 1)
                    pe.wait_ge(tab_in, 16)
                    pe.wait_ge(pair_freed[0], pool_use[0])
                    for g in range(4):
                        for k in range(NT):
                            op = pe.matmul(bank[g // 2][:, (g % 2) * T:(g % 2 + 1) * T],
                                           u_sb[:, k, g * P:(g + 1) * P], pool_mat[:, g, k, :],
                                           start=(k == 0), stop=(k == NT - 1))
                    op.then_inc(pool_mm, 1)
                    mod_columns(rest[0], rest[0] % 2)
                unit(i)
            pe.wait_ge(pair_freed[0], pool_use[0] + 1)
            pe.wait_ge(wpool_in, 16)
            pe.wait_ge(pair_freed[1], pool_use[1])
            for g in range(4):
                op = pe.matmul(bank[2 + g // 2][:, (g % 2) * T:(g % 2 + 1) * T], w_pool[:, g, :],
                               pooled[:, g, :], start=True, stop=True)
            op.then_inc(pool_mm, 1)

            gates_made = 0

            def res_side(c, prev, layer, v, s):
                nonlocal gates_made
                mods_at(c, prev, s)
                if "gate" in c.extra and s == 4:
                    gate_columns(layer, v, c.idx, gates_made + 1)
                    gates_made += 1

            prev = plan["even_out"][0]._replace(mods=rest[1:])
            for c in plan["even_out"]:
                gemm(c, m_hi, m_lo, lambda s: res_side(c, prev, 0, 2, s),
                     {0: [(mix_lo, EVEN_MIX)]} if c.idx == 0 else None)
                prev = c
            mods_at(None, prev, 0)

            def hid_turn(up):
                h = up.extra
                pe.wait_ge(pair_freed[1], up.use + 1)
                for t in range(NT):
                    take(B_A + t, hid_lo, HID_CREDIT + 2 * h + t + 1)
                    transposes(B_A + t, lambda j: hid_tok[:, t, j * P:(j + 1) * P], 4, hid_t)

            def ffn(layer, k):
                norm_turn(norm_first(k))
                for sp_n, (gu, down) in enumerate(plan[f"ffn{layer}"]):
                    def gate_up(gate, up, was, norm=None):
                        def side(s):
                            if norm:
                                norm_turn(norm_side(norm, s))
                            if was and s == 1:
                                hid_turn(was)
                        gemm(gate, h_hi, h_lo, side, h_waits(norm) if norm else None)
                        gemm(up, h_hi, h_lo, lambda s: mods_at(None, gate, s))

                    gate_up(*gu[0], None, k if sp_n == 0 else None)
                    with pe.Fori(0, len(gu) - 1) as i:
                        gate, up, was = loop_chunks(gu, i)
                        for t in range(NT):
                            drained[B_A + t] = (hid_lo, HID_CREDIT + 2 * was.extra + t - 1)
                        if gate.mods:
                            drained[B_COL] = (mod_col_done, gate.mods[0])
                        gate_up(gate, up, was)
                    gate, up = gu[-1]
                    h = up.extra
                    for t in range(NT):
                        drained[B_A + t] = (hid_lo, HID_CREDIT + 2 * h + t - 1)
                    if gate.mods:
                        drained[B_COL] = (mod_col_done, gate.mods[0] + 1)
                    for c in down:
                        def side(s):
                            if c.idx == 0 and s == 1:
                                hid_turn(up)
                            res_side(c, None, layer, 5, s)
                        ready = {0: [(hid_lo, HID_CREDIT + 2 * h)],
                                 2 * (len(gu) - 1): [(hid_lo, HID_CREDIT + 2 * h + 2)]} \
                            if c.idx == 0 else None
                        gemm(c, m_hi, m_lo, side, ready)

            ffn(0, 1)

            def dft_side(i):
                g, r = divmod(i, 4)
                if g >= 4:
                    return
                if r == 0:
                    f = plan["odd_in"][g // 2]
                    pe.wait_ge(pair_freed[f.pair], f.use + 1)
                    if g == 0:
                        pe.wait_ge(tab_in, 48)
                    for q in range(2):
                        take(B_A + q, dft_a_in, 2 * g + q + 1)
                        for k in range(NT):
                            ch = g * 256 + q * P
                            op = pe.matmul(bank[B_A + q][:, :], f_sb[:, k, ch:ch + P], dft_cs[:, k, :],
                                           start=(k == 0), stop=(k == NT - 1))
                        op.then_inc(dft_a, 1)
                if r == 2:
                    pe.wait_ge(dft_a_in, 2 * g + 2)
                    take(B_C, mix_lo, EVEN_MIX + g + 1)
                    for o in range(2):
                        for q in range(2):
                            pe.matmul(bank[B_C][:, o * T:(o + 1) * T], dft_cs[:, q, o * P:(o + 1) * P],
                                      dft1[:, q, 0:T], start=(q == 0), stop=False)
                            op = pe.matmul(bank[B_C][:, o * T:(o + 1) * T], dft_ns[:, q, o * P:(o + 1) * P],
                                           dft1[:, q, T:2 * T], start=False, stop=(q == 1))
                    op.then_inc(dft_y, 1)

            def conv_turn(src, t_sem, reader, value):
                pe.wait_ge(pair_freed[src.pair], src.use + 1)
                for b in range(2):
                    take(B_A + b, reader, value(b))
                    for j in range(2):
                        for t in range(NT):
                            ct = 2 * b + j
                            op = pe.transpose(bank[B_A + b][:, j * T + t * P:j * T + (t + 1) * P],
                                              odd_tmp[:, t, ct * P:(ct + 1) * P], ident[:, :])
                    op.then_inc(t_sem, 1)

            norm_turn(norm_first(2))
            prev = None
            for n, c in enumerate(plan["odd_in"]):
                def side(s, c=c, n=n, prev=prev):
                    if n == 0:
                        norm_turn(norm_side(2, s))
                    mods_at(c, prev, s)
                    if n >= 2:
                        dft_side(8 * (n - 2) + s)
                    if c.kind == "bg" and s == 2:
                        conv_turn(prev, u_conv_t, conv_done, lambda b: 4 * c.idx + 2 * b + 2)
                    if c.kind == "cg" and c.idx == 1 and s == 1:
                        conv_turn(prev, bg_t, mixed, lambda b: b + 1)
                gemm(c, h_hi, h_lo, side, h_waits(2) if n == 0 else None)
                prev = c
            for c in plan["odd_out"]:
                def side(s, c=c, prev=prev):
                    if c.idx == 0 and s == 1:
                        conv_turn(prev, bg_t, mixed, lambda b: 2 + b + 1)
                    res_side(c, prev, 1, 2, s)
                gemm(c, m_hi, m_lo, side,
                     {0: [(mix_lo, EVEN_MIX + DFT_MIX + 4)], 6: [(mix_lo, EVEN_MIX + DFT_MIX + 8)]}
                     if c.idx == 0 else None)
                prev = c
            mods_at(None, prev, 0)
            ffn(1, 3)

        @block.scalar
        def _(act):
            act.wait_ge(c_t, 1)
            for v in range(2):
                act.activation(silu_c[:, :, v], bank[B_B][:, 16 * v:16 * v + 16], ACT.Silu) \
                   .then_inc(silu_ready, 1)

            def hi(c, s):
                slot = (c.slot0 + s) % RING
                if not isinstance(c.w0, int) or c.w0 + s >= RING:
                    act.wait_ge(slab_free, c.w0 + (s - RING + 1))
                act.wait_ge(raw_full[slot], (c.round0 + (c.slot0 + s) // RING + 1) * 16)
                act.activation(w_hi[:, slot, :, :], raw[:, slot, :, :], ACT.Copy).then_inc(hi_done, 1)

            squared = summed = 0

            def square(which, t, n):
                nonlocal squared
                if squared:
                    act.wait_ge(sq_done, squared)
                squared += 1
                act.activation(junk[:, :], norm_source(which)[:, t, n * NC:(n + 1) * NC], ACT.Square,
                               accum_out=sumsq[:, which, t, n:n + 1]).then_inc(sq_done, 1)

            def chunk(c, at, start=0):
                for s in range(start, c.n):
                    hi(c, s)
                    at(s)

            def prefill(c, lo_=0, hi_=PRE):
                for s in range(lo_, hi_):
                    hi(c, s)

            def norm_scaled(k, n, g, which):
                act.wait_ge(rms_ready, which + 1 if k == 0 else k + 2)
                if n >= 2:
                    act.wait_ge(norm_t, n - 1)
                for t in range(NT):
                    op = act.activation(x_norm[:, n % 2, t, :], norm_source(which)[:, t, g * T:(g + 1) * T],
                                        ACT.Copy, scale=rms[:, which, t:t + 1])
                op.then_inc(norm_x, 1)

            def norm_his(k, groups):
                every = norm_groups(k)
                for n, g, which in groups:
                    act.wait_ge(norm_hf, n + 1)
                    act.activation((h_hi, m_hi)[which][:, 2 * g:2 * g + 2, :], hf[:, n % 2, :, :], ACT.Copy) \
                       .then_inc(norm_hi, 1)
                    ahead = n - every[0][0] + 2
                    if ahead < len(every):
                        norm_scaled(k, *every[ahead])

            def norm_start(k):
                for group in norm_groups(k)[:2]:
                    norm_scaled(k, *group)
                norm_his(k, norm_first(k))

            def head_sum(src, i):
                nonlocal summed
                if summed:
                    act.wait_ge(head_sums, summed)
                summed += 1
                for h in range(4):
                    op = act.activation(junk[:, h * P:(h + 1) * P], src[:, h * P:(h + 1) * P], ACT.Square,
                                        accum_out=head_sq[:, i, h:h + 1])
                op.then_inc(head_sums, 1)

            def unit(i):
                if 0 <= i - 4 < 24:
                    u = i - 4
                    act.wait_ge(max_done, u + 1)
                    if u >= 2:
                        act.wait_ge(pt_t, u - 1)
                    act.activation(probs[:, u % 2, :], bank[B_A][:, :], ACT.Exp, scale=SCALE,
                                   bias=neg_max[:, u % 2:u % 2 + 1],
                                   accum_out=p_sum[:, u % 2:u % 2 + 1]).then_inc(exp_done, 1)
                if 0 <= i - 6 < 24:
                    u = i - 6
                    act.wait_ge(pt_t, u + 1)
                    if u >= 2:
                        act.wait_ge(pv_done, u - 1)
                    act.activation(probs_t[:, u % 2, :, :],
                                   bank[B_B][:, :].rearrange("p (k t) -> p k t", k=4), ACT.Copy) \
                       .then_inc(pt_in, 1)
                if 0 <= i - 7 < 24:
                    u = i - 7
                    act.wait_ge(pv_done, u + 1)
                    h, t = 4 * (u // 8) + u % 4, (u // 4) % 2
                    act.activation(m_hi[:, h, t * P:(t + 1) * P], bank[B_C][:, 0:P], ACT.Copy) \
                       .then_inc(mix_hi, 1)

            def even_at(n, prev, s):
                if n == 1:
                    if s == 3:
                        act.wait_ge(slab_free, prev.w0 + prev.n)
                        for t in range(NT):
                            op = act.activation(k_tmp[:, t, :], bank[t][:, :], ACT.Copy)
                        op.then_inc(pair_freed[0], 1)
                    if s in (4, 6):
                        act.wait_ge(pair_freed[(s - 4) // 2], 1)
                        for i in (s - 4, s - 3):
                            head_sum(k_tmp[:, i, :], i)
                if n == 2:
                    if s == 3:
                        act.wait_ge(slab_free, prev.w0 + prev.n)
                        for t in range(NT):
                            op = act.activation(v_sb[:, 2 + t, :], bank[t][:, :], ACT.Copy)
                        op.then_inc(pair_freed[0], 1)
                    if 4 <= s:
                        i = s - 4
                        act.wait_ge(kt_t, i + 1)
                        at = 2 * P + i * P if i < 2 else (i - 2) * P
                        act.activation(kt_sb[:, :, at:at + P],
                                       bank[B_B][:, :].rearrange("p (h k) -> p h k", h=4), ACT.Copy) \
                           .then_inc(kt_in, 1)
                if n >= 3 and s == 3:
                    c = n - 3
                    act.wait_ge(slab_free, prev.w0 + prev.n)
                    if c > 0:
                        act.wait_ge(qt_t, 2 * c)
                    for t in range(NT):
                        op = act.activation(q_tmp[:, t, :], bank[2 * prev.pair + t][:, :], ACT.Copy)
                    op.then_inc(pair_freed[prev.pair], 1)
                    act.wait_ge(pair_freed[prev.pair], prev.use + 1)
                    for t in range(NT):
                        head_sum(q_tmp[:, t, :], t)
                if n >= 4 and s in (1, 3):
                    c, t = n - 4, (s - 1) // 2
                    act.wait_ge(qt_t, 2 * c + t + 1)
                    act.activation(qt[:, c % 2, :, t * P:(t + 1) * P],
                                   bank[B_COL][:, :].rearrange("p (h k) -> p h k", h=4), ACT.Copy) \
                       .then_inc(qt_in, 1)
                if n >= 4:
                    unit(8 * (n - 4) + s)

            even_in, even_out = plan["even_in"], plan["even_out"]

            def start_row(m):
                act.wait_ge(start_free, (m + 1) * 8)
                if m >= 2:
                    act.wait_ge(row_mm, m - 1)
                act.activation(acc[0:2, m % 2, :], bank[B_C][0:2, :], ACT.Copy).then_inc(row_copied, 1)

            for i in range(ND):
                start_row(2 * i)
                if i == 0:
                    for which in range(2):
                        act.wait_ge(x_in, 32)
                        for t in range(NT):
                            for n in range(ND):
                                square(which, t, n)
                else:
                    hi(even_in[0], 2 * i)
                start_row(2 * i + 1)
                if i == 0:
                    for s in range(2):
                        hi(even_in[0], s)
                    for group in norm_groups(0)[:2]:
                        norm_scaled(0, *group)
                else:
                    hi(even_in[0], 2 * i + 1)
                norm_his(0, start_groups(i))
            act.wait_ge(start_free, 8 * START_CHUNKS)
            act.dma_start(head_g[:, 0, :], q_g_d[0:1, :].broadcast_to([P, HD])).then_inc(rope_in, 16)
            act.dma_start(head_g[:, 1, :], k_g_d[0:1, :].broadcast_to([P, HD])).then_inc(rope_in, 16)
            act.dma_start(rope_raw[:, 0, :, :], rope_cos_d.rearrange("(t p) d -> p t d", p=P)) \
               .then_inc(rope_in, 16)
            act.dma_start(rope_raw[:, 1, :, :], rope_sin_d.rearrange("(t p) d -> p t d", p=P)) \
               .then_inc(rope_in, 16)
            act.dma_start(pool_mat, pool_mat_d.rearrange("g (k p) t -> p g k t", p=P)).then_inc(tab_in, 16)
            act.dma_start(w_pool, w_pool_d[0].rearrange("g c d -> c g d")).then_inc(wpool_in, 16)

            prev = even_in[0]
            for n, c in enumerate(even_in[1:], 1):
                chunk(c, lambda s: even_at(n, prev, s))
                prev = c
            for i in range(16, 32):
                if i < 16 + RING:
                    hi(even_out[0], i - 16)
                if i in (17, 19):
                    c, t = 2, (i - 17) // 2
                    act.wait_ge(qt_t, 2 * c + t + 1)
                    act.activation(qt[:, 0, :, t * P:(t + 1) * P],
                                   bank[B_COL][:, :].rearrange("p (h k) -> p h k", h=4), ACT.Copy) \
                       .then_inc(qt_in, 1)
                if i == 19:
                    act.wait_ge(slab_free, prev.w0 + prev.n)
                    for t in range(NT):
                        op = act.activation(u_sb[:, t, :], bank[2 * prev.pair + t][:, :], ACT.Copy)
                    op.then_inc(pair_freed[prev.pair], 1)
                unit(i)
                if i == 28:
                    act.wait_ge(pool_mm, 1)
                    for b in range(2):
                        op = act.activation(pooled[:, 2 * b:2 * b + 2, :],
                                            bank[b][:, :].rearrange("p (g t) -> p g t", g=2), ACT.Copy)
                    op.then_inc(pair_freed[0], 1)
            act.wait_ge(pool_mm, 2)
            for g in range(4):
                act.activation(m_hi[:, N_HEADS + g, :], bank[2 + g // 2][:, (g % 2) * T:(g % 2 + 1) * T],
                               ACT.Copy, scale=pscale_cols[:, g:g + 1]).then_inc(mix_hi, 1)

            gates_made = 0

            def gate_copy(n):
                nonlocal gates_made
                gates_made += 1
                act.wait_ge(gb_mm, gates_made)
                act.activation(gate_bc[:, n * NC:(n + 1) * NC], bank[B_C][:, :], ACT.Copy) \
                   .then_inc(gb_in, 1)

            def res_at(prev, s):
                if prev is None:
                    return
                if s == 0 and "gate" in prev.extra:
                    gate_copy(prev.idx)
                if s == 4 and "stats" in prev.extra:
                    act.wait_ge(res_step, res_no[prev.g])
                    for t in range(NT):
                        square(0, t, prev.idx)

            def res_phase(chunks, first_at, start):
                prev = None
                for c in chunks:
                    chunk(c, (lambda s: res_at(prev, s)) if prev else first_at, start if prev is None else 0)
                    prev = c
                if "gate" in prev.extra:
                    gate_copy(prev.idx)
                return prev._replace(extra=prev.extra.replace("gate", ""))

            def last_squares(prev, nxt):
                if nxt is not None:
                    prefill(nxt)
                res_at(prev, 4)
                if nxt is not None:
                    prefill(nxt, PRE, RING)

            prev = res_phase(even_out, lambda s: None, RING)

            def hid_copy(h, i):
                for t in range(NT):
                    act.wait_ge(hid_t, 2 * h + t + 1)
                    dst = m_hi[:, :, t * P:(t + 1) * P].rearrange("p (c k) q -> p c k q", k=4)
                    act.activation(dst[:, i, :, :], bank[B_A + t][:, :].rearrange("p (k q) -> p k q", k=4),
                                   ACT.Copy).then_inc(hid_hi, 1)

            def ffn(layer, k):
                norm_start(k)
                prev, start = None, RING
                for gu, down in plan[f"ffn{layer}"]:
                    def gate_up(gate, up, was, start=0):
                        def gate_at(s):
                            if start and s >= 4:
                                norm_his(k, norm_side(k, s - 4))
                            if was is not None and was.kind == "res":
                                res_at(was, s)
                            elif was is not None and s == 5:
                                hid_copy(was.extra, was.idx)

                        def up_at(s):
                            if s == 3:
                                act.wait_ge(slab_free, gate.w0 + gate.n)
                                act.wait_ge(pair_freed[1], up.use)
                                for t in range(NT):
                                    op = act.activation(silu_g[:, t, :], bank[t][:, :], ACT.Silu)
                                op.then_inc(pair_freed[0], 1)

                        chunk(gate, gate_at, start)
                        chunk(up, up_at)

                    gate_up(*gu[0], prev, start)
                    if start and layer == 1:
                        act.wait_ge(h_ready, norm_groups(3)[-1][0] + 1)
                        act.dma_start(final_g, final_g_d.rearrange("(a n) -> a n", a=1)
                                      .broadcast_to([P, D])).then_inc(fin_in, 16)
                    start = 0
                    with act.Fori(0, len(gu) - 1) as i:
                        gate_up(*loop_chunks(gu, i))
                    up = gu[-1][1]
                    prev = res_phase(down, lambda s: hid_copy(up.extra, up.idx) if s == 5 else None, 0)
                return prev

            last_squares(prev, plan["ffn0"][0][0][0][0])
            act.dma_start(dft_cs, dft_d[:, 0:512].rearrange("(k p) n -> p k n", p=P)).then_inc(tab_in, 16)
            act.dma_start(dft_ns, dft_d[:, 512:768].rearrange("(k p) n -> p k n", p=P)).then_inc(tab_in, 16)
            prev = ffn(0, 1)
            odd_in, odd_out = plan["odd_in"], plan["odd_out"]
            last_squares(prev, odd_in[0])
            norm_start(2)

            def odd_at(n, prev, s):
                if n == 0 and s >= 4:
                    norm_his(2, norm_side(2, s - 4))
                i = 8 * (n - 2) + s
                if i >= 4 and i % 4 == 0 and i // 4 - 1 < 4:
                    g = i // 4 - 1
                    act.wait_ge(dft_a, 2 * g + 1)
                    if g > 0:
                        act.wait_ge(dft_y, g)
                    act.activation(dft1[:, 0, :], bank[B_A][:, :], ACT.Copy).then_inc(dft_a_in, 1)
                if i >= 6 and (i - 6) % 4 == 0 and (i - 6) // 4 < 4:
                    g = (i - 6) // 4
                    act.wait_ge(dft_y, g + 1)
                    act.activation(m_hi[:, 2 * g:2 * g + 2, :],
                                   bank[B_C][:, :].rearrange("p (o t) -> p o t", o=2), ACT.Copy) \
                       .then_inc(mix_hi, 1)
                if prev is not None and s == 3:
                    half = prev.idx
                    banks = [bank[2 * prev.pair + t][:, :] for t in range(NT)]
                    if prev.kind in ("f", "cg", "bg"):
                        act.wait_ge(slab_free, prev.w0 + prev.n)
                        if prev.kind == "cg" and half == 1:
                            act.wait_ge(bg_t, 2)
                        if prev.kind == "bg":
                            act.wait_ge(u_conv_t, 2 * half + 2)
                        for t in range(NT):
                            dst = f_sb[:, t, half * NC:(half + 1) * NC] if prev.kind == "f" else odd_tmp[:, t, :]
                            op = act.activation(dst, banks[t], ACT.Copy)
                        op.then_inc(pair_freed[prev.pair], 1)
                if prev is not None and prev.kind == "bg" and s == 6:
                    mixed_hi(prev.idx)

            def mixed_hi(half):
                for b in range(2):
                    act.wait_ge(mixed, 2 * half + b + 1)
                    for j in range(2):
                        ct = 2 * b + j
                        act.activation(m_hi[:, 8 + 4 * half + ct, :], y_conv[:, ct, :], ACT.Copy) \
                           .then_inc(mix_hi, 1)

            prev = None
            for n, c in enumerate(odd_in):
                chunk(c, lambda s: odd_at(n, prev, s), RING if n == 0 else 0)
                prev = c
            prev = res_phase(odd_out, lambda s: odd_at(8, odd_in[-1], s), 0)
            last_squares(prev, plan["ffn1"][0][0][0][0])
            prev = ffn(1, 3)
            last_squares(prev, None)

        @block.vector
        def _(dve):
            steps = 0

            def own(op):
                nonlocal steps
                op.then_inc(v_self, 1)
                steps += 1

            def own_wait():
                dve.wait_ge(v_self, steps)

            def lo(c, s):
                slot = (c.slot0 + s) % RING
                dve.wait_ge(hi_done, c.w0 + s + 1)
                dve.tensor_tensor(w_lo[:, slot, :, :], raw[:, slot, :, :], w_hi[:, slot, :, :].bitcast(f32),
                                  ALU.subtract).then_inc(lo_done, 1)

            dve.memset(ones[:, :], 1.0).then_inc(hid_lo, HID_CREDIT)
            for a in (3, 0, 1, 2):
                dve.memset(rows[:, a, :], 0.0).then_inc(cols_ready, 1)
            dve.wait_ge(cols_t, 1)
            dve.tensor_copy(colsA[:, :], bank[B_A][:, 0:P])
            for l in range(2):
                op = dve.tensor_copy(bias_cols[:, l * MOD_CHUNKS:(l + 1) * MOD_CHUNKS, :].rearrange(
                    "p n j -> p (n j)"), bank[B_A][:, (1 + l) * P:(1 + l) * P + 96])
            op.then_inc(cols_ready, 1)

            def rsqrt(y, x, n):
                own(dve.tensor_scalar(guess[:, 0:n], x.bitcast(i32), 1, None, ALU.logical_shift_right))
                own_wait()
                own(dve.tensor_scalar(y.bitcast(i32), guess[:, 0:n], -1.0, float(0x5F3759DF), ALU.mult,
                                      ALU.add))
                own_wait()
                for _ in range(3):
                    own(dve.tensor_tensor(newton[:, 0:n], y, y, ALU.mult))
                    own_wait()
                    own(dve.scalar_tensor_tensor(out=newton[:, 0:n], in0=newton[:, 0:n], scalar=-0.5, in1=x,
                                                 op0=ALU.mult, op1=ALU.mult))
                    own_wait()
                    own(dve.scalar_tensor_tensor(out=y, in0=newton[:, 0:n], scalar=1.5, in1=y,
                                                 op0=ALU.add, op1=ALU.mult))
                    own_wait()

            def stream_rms(which, sq_count, count):
                dve.wait_ge(sq_done, sq_count)
                ms = msq[:, which, :]
                own(dve.tensor_reduce(ms, sumsq[:, which, :, :], AX.X, ALU.add))
                own_wait()
                own(dve.tensor_scalar(ms, ms, 1.0 / D, EPS, ALU.mult, ALU.add))
                own_wait()
                rsqrt(rms[:, which, :], ms, NT)
                dve.tensor_copy(junk2[:, :], rms[:, which, :]).then_inc(rms_ready, 1)

            def scale_col(which, norm_w, scale, tiles=slice(0, KT)):
                own(dve.scalar_tensor_tensor(out=s_col[:, which, tiles], in0=scale[:, tiles], scalar=1.0,
                                             in1=norm_w[:, tiles], op0=ALU.add, op1=ALU.mult))
                own_wait()

            def norm_step(groups, shifts):
                for pair in (groups[0:2], groups[2:4]):
                    for n, g, which in pair:
                        if n >= 2:
                            dve.wait_ge(h_ready, n - 1)
                        dve.wait_ge(norm_t, n + 1)
                        for j in range(2):
                            ft = 2 * g + j
                            op = dve.tensor_scalar(hf[:, n % 2, j, :], bank[B_A + n % 2][:, j * T:(j + 1) * T],
                                                   s_col[:, which, ft:ft + 1], shifts[which][:, ft:ft + 1],
                                                   ALU.mult, ALU.add)
                        op.then_inc(norm_hf, 1)
                    for n, g, which in pair:
                        dve.wait_ge(norm_hi, n + 1)
                        hi_, lo_ = ((h_hi, h_lo), (m_hi, m_lo))[which]
                        dve.tensor_tensor(lo_[:, 2 * g:2 * g + 2, :], hf[:, n % 2, :, :],
                                          hi_[:, 2 * g:2 * g + 2, :].bitcast(f32), ALU.subtract) \
                           .then_inc(h_ready, 1)

            def norm_w(layer, sub):
                o = (2 * layer + sub) * KT
                return norm_cols[:, o:o + KT]

            def mod_slab(q, sl, slot, strict):
                dve.wait_ge(mod_full[sl % RING], (q * 2 + (START_CHUNKS + sl // RING + 1)) * 16)
                if sl == 0:
                    if strict:
                        dve.wait_ge(mod_mm, q)
                    elif q >= 2:
                        dve.wait_ge(mod_mm, q - 1)
                    else:
                        dve.wait_ge(row_mm, START_CHUNKS)
                for j in range(SLAB_K):
                    k = SLAB_K * sl + j
                    w = mod_raw[:, sl % RING, j, :]
                    if k == 0:
                        dve.tensor_scalar(acc[:, slot, :], w, silu_c[:, 0, 0:1], None, ALU.mult) \
                           .then_inc(mod_step, 1)
                    else:
                        dve.wait_ge(mod_step, q * 16 + k)
                        dve.scalar_tensor_tensor(out=acc[:, slot, :], in0=w, scalar=silu_c[:, k, 0:1],
                                                 in1=acc[:, slot, :], op0=ALU.mult, op1=ALU.add) \
                           .then_inc(mod_step, 1)

            def chunk(c, at, start=0):
                total, done = 8 * len(c.mods), 0
                strict = c.kind == "gate" or c is plan["odd_in"][0]
                for s in range(start, c.n):
                    lo(c, s)
                    at(s)
                    until = total * (s - start + 1) // (c.n - start)
                    for m in range(done, until):
                        q = c.mods[m // 8]
                        mod_slab(q, m % 8, 0 if c.kind == "gate" else q % 2, strict)
                    done = until

            def prefill(c, first=0, end=PRE):
                for s in range(first, end):
                    lo(c, s)

            def mod_out(q):
                dve.wait_ge(mod_mm, q + 1)
                dve.tensor_tensor(mod_cols[:, q + START_CHUNKS, :], bank[B_COL][:, 0:4],
                                  bias_cols[:, q + START_CHUNKS, :], ALU.add).then_inc(mod_col_done, 1)

            def mods_at(c, prev, s):
                if s == 4 and prev is not None and prev.mods:
                    mod_out(prev.mods[-1])
                if s == 7 and c is not None and len(c.mods) == 2:
                    mod_out(c.mods[0])

            even_in, even_out = plan["even_in"], plan["even_out"]
            ctx_scale = ctx_cols[:, ND:2 * ND, :].rearrange("p n j -> p (n j)")
            ctx_shift = ctx_cols[:, 0:ND, :].rearrange("p n j -> p (n j)")
            start_shifts = (mod_vec(0, 0), ctx_shift)

            def start_cols(m):
                n = start_col_chunk(m)
                both = bank[B_COL][:, 0:8].rearrange("p (j v) -> p j v", v=2)
                dve.wait_ge(row_mm, m + 1)
                dve.tensor_tensor(mod_cols[:, n, :], both[:, :, 0], bias_cols[:, n, :], ALU.add)
                dve.tensor_tensor(ctx_cols[:, n, :], both[:, :, 1], bias_cols[:, n, :], ALU.add) \
                   .then_inc(start_col, 1)

            dve.wait_ge(cols_ready, 5)
            for i in range(ND):
                start_cols(2 * i)
                if i == 0:
                    for which in range(2):
                        stream_rms(which, 8 * (which + 1), which + 1)
                else:
                    lo(even_in[0], 2 * i)
                start_cols(2 * i + 1)
                dve.wait_ge(start_col, 2 * i + 2)
                for which, scale in ((0, mod_vec(0, 1)), (1, ctx_scale)):
                    scale_col(which, norm_w(0, 0), scale, slice(4 * i, 4 * i + 4))
                if i == 0:
                    lo(even_in[0], 0)
                lo(even_in[0], 2 * i + 1)
                norm_step(start_groups(i), start_shifts)

            def halves(ap):
                return ap.rearrange("p (b h q) -> p b h q", b=2, h=2)

            def heads(ap):
                return ap.rearrange("p (h d) -> p h d", h=4)

            def fold_tables():
                dve.wait_ge(rope_in, 64)
                for a in range(2):
                    g = head_g[:, a, :]
                    for t in range(NT):
                        dve.tensor_tensor(fold[:, 2 * a, t, :], rope_raw[:, 0, t, :], g, ALU.mult)
                        for h in range(2):
                            op = dve.tensor_tensor(halves(fold[:, 2 * a + 1, t, :])[:, :, h, :],
                                                   halves(rope_raw[:, 1, t, :])[:, :, h, :],
                                                   halves(g)[:, :, 1 - h, :], ALU.mult)
                own(op)

            def head_rms(i):
                own(dve.tensor_scalar(head_ms[:, :, :], head_sq[:, i:i + 2, :], 1.0 / HD, EPS, ALU.mult,
                                      ALU.add))
                own_wait()
                rsqrt(head_r[:, :, :].rearrange("p t h -> p (t h)"),
                      head_ms[:, :, :].rearrange("p t h -> p (t h)"), 2 * 4)

            def head_norm(src, t):
                own(dve.tensor_tensor(heads(src), heads(src),
                                      head_r[:, t, :].unsqueeze(2).broadcast_to([P, 4, HD]), ALU.mult))
                own_wait()

            roped = 0

            def rope(src, t, a):
                nonlocal roped
                if roped:
                    dve.wait_ge(rope_done, roped)
                roped += 1
                cos = fold[:, 2 * a, t, :].unsqueeze(1).broadcast_to([P, 4, HD])
                own(dve.tensor_tensor(heads(rope_a), heads(src), cos, ALU.mult))
                quarters = "p (h b s q) -> p h b s q"
                sv = src.rearrange(quarters, h=4, b=2, s=2)
                bv = rope_b.rearrange(quarters, h=4, b=2, s=2)
                for s in range(2):
                    sin = halves(fold[:, 2 * a + 1, t, :])[:, :, s, :].unsqueeze(1).broadcast_to([P, 4, 2, 32])
                    own(dve.tensor_tensor(bv[:, :, :, s, :], sv[:, :, :, 1 - s, :], sin, ALU.mult))
                own_wait()
                return dve.tensor_tensor(src, rope_a, rope_b, ALU.add)

            def unit(i):
                if 0 <= i - 4 < 24:
                    u = i - 4
                    b = u % 2
                    dve.wait_ge(scores_done, u + 1)
                    own(dve.tensor_reduce(row_max[:, b:b + 1], bank[B_A][:, :], AX.X, ALU.max))
                    own_wait()
                    dve.tensor_scalar(neg_max[:, b:b + 1], row_max[:, b:b + 1], -SCALE, None, ALU.mult) \
                       .then_inc(max_done, 1)
                if 0 <= i - 7 < 24:
                    u = i - 7
                    dve.wait_ge(mix_hi, u + 1)
                    h, t = 4 * (u // 8) + u % 4, (u // 4) % 2
                    dve.tensor_tensor(m_lo[:, h, t * P:(t + 1) * P], bank[B_C][:, 0:P],
                                      m_hi[:, h, t * P:(t + 1) * P].bitcast(f32), ALU.subtract) \
                       .then_inc(mix_lo, 1)
                if 0 <= i - 4 < 24:
                    dve.wait_ge(exp_done, (i - 4) + 1)
                    b = (i - 4) % 2
                    own(dve.reciprocal(p_inv[:, b:b + 1], p_sum[:, b:b + 1]))
                    own_wait()
                    dve.tensor_scalar(probs[:, b, :], probs[:, b, :], p_inv[:, b:b + 1], None, ALU.mult) \
                       .then_inc(probs_done, 1)

            def even_at(n, prev, s):
                nonlocal roped
                if n == 1 and s == 0:
                    fold_tables()
                mods_at(plan["even_in"][n], prev, s)
                if n == 1:
                    if s == 3:
                        dve.wait_ge(slab_free, prev.w0 + prev.n)
                        dve.tensor_copy(k_tmp[:, 2, :], bank[2][:, :])
                        dve.tensor_copy(k_tmp[:, 3, :], bank[3][:, :]).then_inc(pair_freed[1], 1)
                    if s >= 4:
                        i = s - 4
                        if i % 2 == 0:
                            dve.wait_ge(head_sums, i + 2)
                            head_rms(i)
                        head_norm(k_tmp[:, i, :], i % 2)
                        if i < NT:
                            rope(k_tmp[:, i, :], i, 1).then_inc(rope_done, 1)
                        else:
                            g = head_g[:, 1, :].unsqueeze(1).broadcast_to([P, 4, HD])
                            dve.tensor_tensor(heads(k_tmp[:, i, :]), heads(k_tmp[:, i, :]), g, ALU.mult) \
                               .then_inc(rope_done, 1)
                            roped = i + 1
                if n == 2 and s == 3:
                    dve.wait_ge(slab_free, prev.w0 + prev.n)
                    dve.tensor_copy(v_sb[:, 0, :], bank[2][:, :])
                    dve.tensor_copy(v_sb[:, 1, :], bank[3][:, :]).then_inc(pair_freed[1], 1)
                if n >= 3 and s in (4, 6):
                    c, t = n - 3, (s - 4) // 2
                    if t == 0:
                        dve.wait_ge(head_sums, 4 + 2 * c + 2)
                        head_rms(0)
                    head_norm(q_tmp[:, t, :], t)
                    rope(q_tmp[:, t, :], t, 0).then_inc(rope_done, 1)
                if n >= 4:
                    unit(8 * (n - 4) + s)

            prev = even_in[0]
            for n, c in enumerate(even_in[1:], 1):
                chunk(c, lambda s: even_at(n, prev, s))
                prev = c
            rest = plan["rest_mods"]
            for i in range(16, 32):
                if i < 16 + RING:
                    lo(even_out[0], i - 16)
                mods_at(None, prev, i - 16)
                unit(i)
                if i == 28:
                    mod_out(rest[0])
                mod_slab(rest[(i - 16) // 8], (i - 16) % 8, rest[(i - 16) // 8] % 2, False)
            for g in range(4):
                dve.wait_ge(mix_hi, 24 + 2 * (g // 2) + 2)
                dve.scalar_tensor_tensor(out=m_lo[:, N_HEADS + g, :],
                                         in0=bank[2 + g // 2][:, (g % 2) * T:(g % 2 + 1) * T],
                                         scalar=pscale_cols[:, g:g + 1],
                                         in1=m_hi[:, N_HEADS + g, :].bitcast(f32),
                                         op0=ALU.mult, op1=ALU.subtract).then_inc(mix_lo, 1)
            gates_used = 0

            def residual(prev):
                nonlocal gates_used
                if res_no[prev.g] > 1:
                    dve.wait_ge(res_step, res_no[prev.g] - 1)
                cols = slice(prev.idx * NC, (prev.idx + 1) * NC)
                dve.wait_ge(slab_free, prev.w0 + prev.n)
                if "gate" in prev.extra:
                    gates_used += 1
                    dve.wait_ge(gb_in, gates_used)
                for t in range(NT):
                    op = dve.tensor_tensor(res_tmp[:, t, :], bank[2 * prev.pair + t][:, :], gate_bc[:, cols],
                                           ALU.mult)
                op.then_inc(pair_freed[prev.pair], 1)
                dve.wait_ge(pair_freed[prev.pair], prev.use + 1)
                for t in range(NT):
                    op = dve.tensor_tensor(x_tok[:, t, cols], x_tok[:, t, cols], res_tmp[:, t, :], ALU.add)
                op.then_inc(res_step, 1)

            def res_phase(chunks, first_at, start):
                prev = None
                for c in chunks:
                    def at(s, prev=prev):
                        if prev is None:
                            first_at(s)
                        else:
                            mods_at(c, prev, s)
                            if s == 3:
                                residual(prev)
                    chunk(c, at, start if prev is None else 0)
                    prev = c
                return prev

            def last_residual(prev, nxt):
                if nxt is not None:
                    prefill(nxt)
                residual(prev)
                if nxt is not None:
                    prefill(nxt, PRE, RING)
                mods_at(None, prev, 4)

            def first_out(s):
                if s == 4:
                    mod_out(rest[1])
                if s == 7:
                    dve.wait_ge(x_again, 16)

            prev = res_phase(even_out, first_out, RING)
            last_residual(prev, plan["ffn0"][0][0][0][0])

            def hid_lo_half(h, i):
                for t in range(NT):
                    dve.wait_ge(hid_hi, 2 * h + t + 1)
                    rng = (slice(None), slice(None), slice(t * P, (t + 1) * P))
                    hi_ = m_hi[rng].rearrange("p (c k) q -> p c k q", k=4)[:, i, :, :].bitcast(f32)
                    lo_ = m_lo[rng].rearrange("p (c k) q -> p c k q", k=4)[:, i, :, :]
                    dve.tensor_tensor(lo_, bank[B_A + t][:, :].rearrange("p (k q) -> p k q", k=4), hi_,
                                      ALU.subtract).then_inc(hid_lo, 1)

            def ffn(layer, k):
                stream_rms(0, 16 + 8 * k, k + 2)
                scale_col(0, norm_w(layer, 1), mod_vec(layer, 4))
                shifts = (mod_vec(layer, 3),)
                norm_step(norm_first(k), shifts)
                prev, start = None, RING
                for gu, down in plan[f"ffn{layer}"]:
                    def hidden(prev, gate_use, s):
                        if s == 3:
                            dve.wait_ge(slab_free, prev.w0 + prev.n)
                            dve.wait_ge(pair_freed[0], gate_use + 1)
                            for t in range(NT):
                                op = dve.tensor_tensor(hid_tok[:, t, :], silu_g[:, t, :],
                                                       bank[2 + t][:, :], ALU.mult)
                            op.then_inc(pair_freed[1], 1)
                        if s == 5:
                            hid_lo_half(prev.extra, prev.idx)

                    def gate_up(gate, up, was, start=0):
                        def gate_at(s):
                            if start and s >= 4:
                                norm_step(norm_side(k, s - 4), shifts)
                            if was is None:
                                return
                            if was.kind == "up":
                                hidden(was, gate.use - 1, s)
                            elif s == 3:
                                residual(was)
                        chunk(gate, gate_at, start)
                        chunk(up, lambda s: mods_at(None, gate, s))

                    gate_up(gu[0][0], gu[0][1], prev, start)
                    start = 0
                    with dve.Fori(0, len(gu) - 1) as i:
                        gate_up(*loop_chunks(gu, i))
                    last_gate, last_up = gu[-1]
                    prev = res_phase(down, lambda s: hidden(last_up, last_gate.use, s), 0)
                return prev

            prev = ffn(0, 1)
            last_residual(prev, plan["odd_in"][0])
            stream_rms(0, 32, 4)
            scale_col(0, norm_w(1, 0), mod_vec(1, 1))
            norm_step(norm_first(2), (mod_vec(1, 0),))

            def odd_at(n, prev, s):
                mods_at(plan["odd_in"][n] if n < 8 else None, prev, s)
                if n == 0 and s >= 4:
                    norm_step(norm_side(2, s - 4), (mod_vec(1, 0),))
                i = 8 * (n - 2) + s
                if i >= 4 and i % 4 == 0 and i // 4 - 1 < 4:
                    g = i // 4 - 1
                    dve.wait_ge(dft_a, 2 * g + 2)
                    if g > 0:
                        dve.wait_ge(dft_y, g)
                    dve.wait_ge(dft_a_in, 2 * g + 1)
                    dve.tensor_copy(dft1[:, 1, :], bank[B_B][:, :]).then_inc(dft_a_in, 1)
                if i >= 6 and (i - 6) % 4 == 0 and (i - 6) // 4 < 4:
                    g = (i - 6) // 4
                    dve.wait_ge(mix_hi, EVEN_MIX + g + 1)
                    dve.tensor_tensor(m_lo[:, 2 * g:2 * g + 2, :],
                                      bank[B_C][:, :].rearrange("p (o t) -> p o t", o=2),
                                      m_hi[:, 2 * g:2 * g + 2, :].bitcast(f32), ALU.subtract) \
                       .then_inc(mix_lo, 1)
                if prev is None:
                    return
                half = prev.idx
                if prev.kind == "xin" and s == 3:
                    dve.wait_ge(slab_free, prev.w0 + prev.n)
                    cg = plan["odd_in"][n - 2]
                    dve.wait_ge(pair_freed[cg.pair], cg.use + 1)
                    for t in range(NT):
                        op = dve.tensor_tensor(odd_tmp[:, t, :], odd_tmp[:, t, :],
                                               bank[2 * prev.pair + t][:, :], ALU.mult)
                    op.then_inc(pair_freed[prev.pair], 1)
                if n < 8 and plan["odd_in"][n].kind == "bg" and s == 6:
                    conv(plan["odd_in"][n].idx)
                if prev.kind == "bg" and s == 5:
                    for b in range(2):
                        dve.wait_ge(bg_t, 2 * half + b + 1)
                        op = dve.tensor_tensor(y_conv[:, 2 * b:2 * b + 2, :], y_conv[:, 2 * b:2 * b + 2, :],
                                               bank[B_A + b][:, :].rearrange("p (j t) -> p j t", j=2),
                                               ALU.mult)
                        op.then_inc(mixed, 1)
                if prev.kind == "bg" and s == 6:
                    for ct in range(4):
                        dve.wait_ge(mix_hi, EVEN_MIX + DFT_MIX + 4 * half + ct + 1)
                        m = 8 + 4 * half + ct
                        dve.tensor_tensor(m_lo[:, m, :], y_conv[:, ct, :], m_hi[:, m, :].bitcast(f32),
                                          ALU.subtract).then_inc(mix_lo, 1)

            def conv(half):
                for ct in range(4):
                    if ct % 2 == 0:
                        dve.wait_ge(u_conv_t, 2 * half + ct // 2 + 1)
                    u = bank[B_A + ct // 2][:, (ct % 2) * T:(ct % 2 + 1) * T]
                    y = y_conv[:, ct, :]
                    k = 4 * half + ct
                    w = [conv_cols[:, 8 * j + k:8 * j + k + 1] for j in range(3)]
                    own(dve.tensor_scalar(y, u, w[1], None, ALU.mult))
                    own_wait()
                    own(dve.scalar_tensor_tensor(out=y[:, 1:T], in0=u[:, 0:T - 1], scalar=w[0],
                                                 in1=y[:, 1:T], op0=ALU.mult, op1=ALU.add))
                    own_wait()
                    dve.scalar_tensor_tensor(out=y[:, 0:T - 1], in0=u[:, 1:T], scalar=w[2],
                                             in1=y[:, 0:T - 1], op0=ALU.mult, op1=ALU.add) \
                       .then_inc(conv_done, 1)
                dve.wait_ge(conv_done, 4 * half + 4)

            prev = None
            for n, c in enumerate(plan["odd_in"]):
                chunk(c, lambda s: odd_at(n, prev, s), RING if n == 0 else 0)
                prev = c
            prev = res_phase(plan["odd_out"], lambda s: odd_at(8, plan["odd_in"][-1], s), 0)
            last_residual(prev, plan["ffn1"][0][0][0][0])
            prev = ffn(1, 3)
            last_residual(prev, None)
            stream_rms(0, 48, 6)
            dve.wait_ge(fin_in, 16)
            for n in range(ND):
                for t in range(NT):
                    cols = slice(n * NC, (n + 1) * NC)
                    op = dve.scalar_tensor_tensor(out=x_tok[:, t, cols], in0=x_tok[:, t, cols],
                                                  scalar=rms[:, 0, t:t + 1], in1=final_g[:, cols],
                                                  op0=ALU.mult, op1=ALU.mult)
                op.then_inc(x_final, 1)


def tables():
    f = np.float32
    quarter = HD // 4
    grid_w = 64
    freqs = f(10000.0) ** (-np.arange(quarter, dtype=f) / f(quarter))
    pos = np.arange(T)
    ang = np.stack([(pos // grid_w).astype(f)[:, None] * freqs, (pos % grid_w).astype(f)[:, None] * freqs], 1)
    cos, sin = np.cos(ang).astype(f), np.sin(ang).astype(f)
    rope_cos = np.stack([cos, cos], 2).reshape(T, HD)
    rope_sin = np.stack([-sin, sin], 2).reshape(T, HD)
    pool = np.zeros((4, T, T), f)
    for g, w in enumerate((2, 4, 8, 16)):
        for t in range(T):
            lo, hi = max(t - w // 2, 0), min(t - w // 2 + w, T)
            pool[g, lo:hi, t] = f(1) / f(hi - lo)
            pool[g, t, t] -= f(1)
    a = 2 * np.pi * ((np.arange(T)[:, None] * np.arange(T)[None, :]) % T) / T
    c, s = np.cos(a) / 16, np.sin(a) / 16
    dft = np.concatenate([c, s, -s], 1).astype(f)
    return {"rope_cos": rope_cos, "rope_sin": rope_sin, "pool_mat": pool, "dft": dft}


_INS = ["x", "c", "ctx", "c_ctx", "norm_g", "w_mod", "b_mod", "w_in_even", "w_out_even", "q_norm_g",
        "k_norm_g", "w_pool", "pool_scale", "w_in_odd", "w_out_odd", "conv_w", "w_ffn_gate", "w_ffn_up",
        "w_ffn_down", "final_g"]


def kernel(**inputs):
    import concourse.bacc as bacc
    from concourse.bass_utils import run_bass_kernel_spmd

    nc = bacc.Bacc("TRN2", target_bir_lowering=False, num_devices=1)
    given = {n: np.ascontiguousarray(inputs[n]) for n in _INS}
    given.update(tables())
    arrays, args = {}, []
    for name, a in given.items():
        arrays[f"in_{name}"] = a
        args.append(nc.dram_tensor(f"in_{name}", a.shape, mybir.dt.from_np(a.dtype), kind="ExternalInput").ap())
    args.append(nc.dram_tensor("out_0", (1, T, D), mybir.dt.float32, kind="ExternalOutput").ap())
    build(nc, *args)
    r = run_bass_kernel_spmd(nc, [arrays], core_ids=[0])
    return r.results[0]["out_0"]
```

```python
from contextlib import ExitStack
from collections import namedtuple

import numpy as np

import concourse.bass as bass
from concourse import mybir

P = 128
D = 2048
KT = D // P
T = 256
NT = T // P
NC = 512
ND = D // NC
SLAB_K = 2
RING = 4
N_HEADS, N_KV, HD = 12, 4, 128
SCALE = float(HD) ** -0.5
EPS = 1e-6
SPLITS = (4, 4, 3)
START_CHUNKS = 8
START_DVE = 4
START_PE = 8 - START_DVE
MOD_CHUNKS = 6 * D // NC

Chunk = namedtuple("Chunk", "kind w0 slot0 round0 n g pair use mods idx extra")


Group = namedtuple("Group", "n which f0 nf toks")
NORM_TURNS = {(1, 0): 2, (3, 0): 3, (1, 1): 4, (2, 1): 5, (3, 1): 6, (4, 1): 7}
NORM_READS = {(0, 0): (0,), (2, 0): (1,), (0, 1): (2,), (2, 1): (3,), (4, 1): (4, 5), (6, 1): (6, 7)}


class Plan:

    def __init__(self):
        self.w = self.g = self.q = 0
        self.uses = [0, 0]

    def pair_use(self, pair):
        self.uses[pair] += 1
        return self.uses[pair] - 1

    def chunk(self, kind, idx, pair, n=8, mods=0, extra=None, both=False):
        c = Chunk(kind, self.w, self.w % RING, self.w // RING, n, self.g, pair, self.uses[pair],
                  tuple(range(self.q, self.q + mods)), idx, extra)
        self.w += n
        self.g += 1
        self.q += mods
        self.uses[pair] += 1
        if both:
            self.uses[1 - pair] += 1
        return c


def moved(c, i, w, g, use, q, idx):
    return c._replace(w0=c.w0 + i * w, round0=c.round0 + i * (w // RING), g=c.g + i * g,
                      use=c.use + i * use, mods=tuple(m + i * q for m in c.mods), idx=c.idx + i * idx)


def make_plan():
    p = Plan()
    plan = {}
    plan["even_in"] = [p.chunk("k", 0, 0, both=True), p.chunk("v", 0, 0, mods=2, both=True),
                       p.chunk("q", 0, 0, mods=1), p.chunk("q", 1, 1, mods=1),
                       p.chunk("q", 2, 0, mods=1), p.chunk("u", 0, 1, mods=2)]
    plan["pool_use"] = (p.pair_use(0), p.uses[1])
    plan["rest_mods"] = (p.q, p.q + 1, p.q + 2)
    p.q += 3
    plan["even_out"] = [p.chunk("res", n, n % 2, mods=int(n < 3), extra="stats gate") for n in range(ND)]
    h = 0
    for layer in range(2):
        splits = []
        for sp, nch in enumerate(SPLITS):
            mods = 1 if layer == 0 or sp == 0 else 0
            gu = []
            for i in range(nch):
                gu.append((p.chunk("gate", i, 0, mods=0 if sp == i == 0 else mods),
                           p.chunk("up", i, 1, extra=h)))
                h += 1
            ex = ("gate" if sp == 0 else "") + (" stats" if sp == len(SPLITS) - 1 else "")
            down = [p.chunk("res", n, n % 2, n=2 * nch, mods=int(layer == 0 and n % 2 == 0), extra=ex)
                    for n in range(ND)]
            splits.append((gu, down))
        plan[f"ffn{layer}"] = splits
        if layer == 0:
            odd = [("f", 0), ("f", 1), ("cg", 0), ("xin", 0), ("bg", 0), ("cg", 1), ("xin", 1), ("bg", 1)]
            plan["odd_in"] = [p.chunk(k, i, n % 2, mods=int(n not in (0, 6))) for n, (k, i) in enumerate(odd)]
            plan["odd_out"] = [p.chunk("res", n, n % 2, mods=int(n < 2), extra="stats gate") for n in range(ND)]
    gates = [c for layer in range(2) for gu, _ in plan[f"ffn{layer}"] for c, _ in gu]
    plan["after_gate"] = {c.mods[0] + 1 for c in gates if c.mods}
    assert p.q == 2 * MOD_CHUNKS - START_CHUNKS, p.q
    return plan


def build(nc, x_d, c_d, ctx_d, c_ctx_d, norm_g_d, w_mod_d, b_mod_d, w_in_e_d, w_out_e_d, q_g_d, k_g_d,
          w_pool_d, pool_scale_d, w_in_o_d, w_out_o_d, conv_w_d, w_gate_d, w_up_d, w_down_d, final_g_d,
          rope_cos_d, rope_sin_d, pool_mat_d, dft_d, out_d):
    f32, f32r, i32 = mybir.dt.float32, mybir.dt.float32r, mybir.dt.int32
    ALU, ACT, AX = mybir.AluOpType, mybir.ActivationFunctionType, mybir.AxisListType
    plan = make_plan()

    def slabs(w):
        return w.rearrange("(s j p) (n c) -> n s p j c", p=P, j=SLAB_K, c=NC)

    wv_in_e, wv_out_e = slabs(w_in_e_d[0]), slabs(w_out_e_d[0])
    wv_in_o, wv_out_o = slabs(w_in_o_d[0]), slabs(w_out_o_d[0])
    wv_gate = [slabs(w_gate_d[l]) for l in range(2)]
    wv_up = [slabs(w_up_d[l]) for l in range(2)]
    wv_down = [slabs(w_down_d[l]) for l in range(2)]
    wv_mod = [slabs(w_mod_d[l]) for l in range(2)]
    even_col = {"q": 0, "k": 3, "v": 4, "u": 5}
    odd_col = {"f": 0, "bg": 2, "cg": 4, "xin": 6}

    with ExitStack() as stack:
        def sb(name, shape, dt=f32):
            return stack.enter_context(nc.sbuf_tensor(name, shape, dt))

        def sem(name):
            return stack.enter_context(nc.semaphore(name))

        x_tok = sb("x_tok", [P, NT, D])
        h_hi, h_lo = sb("h_hi", [P, KT, T], f32r), sb("h_lo", [P, KT, T], f32r)
        m_hi, m_lo = sb("m_hi", [P, KT, T], f32r), sb("m_lo", [P, KT, T], f32r)
        raw = sb("raw", [P, RING, SLAB_K, NC])
        w_hi, w_lo = sb("w_hi", [P, RING, SLAB_K, NC], f32r), sb("w_lo", [P, RING, SLAB_K, NC], f32r)
        mod_raw = sb("mod_raw", [P, RING, SLAB_K, NC])
        acc = sb("acc", [P, 2, NC])
        gate_bc = sb("gate_bc", [P, D])
        scratch = sb("scratch", [P, 6144])
        tables = sb("tables", [P, 2560])
        junk = sb("junk", [P, NC])
        ident, ones = sb("ident", [P, P]), sb("ones", [P, 1])
        rows = sb("rows", [P, 4, P])
        colsA = sb("colsA", [P, P])
        bias_cols = sb("bias_cols", [P, 2 * MOD_CHUNKS, 4])
        mod_cols = sb("mod_cols", [P, 2 * MOD_CHUNKS, 4])
        ctx_cols = sb("ctx_cols", [P, START_CHUNKS, 4])
        silu_c = sb("silu_c", [P, KT, 2])
        s_col = sb("s_col", [P, 2, KT])
        sumsq = sb("sumsq", [P, 2, NT, ND])
        msq = sb("msq", [P, 2, NT])
        rms = sb("rms", [P, 2, NT])
        head_sq = sb("head_sq", [P, 4, 4])
        head_ms = sb("head_ms", [P, NT, 4])
        head_r = sb("head_r", [P, NT, 4])
        minus_half = sb("minus_half", [P, 1])[:, :]
        guess, newton = sb("guess", [P, 8], mybir.dt.int32), sb("newton", [P, 8])
        neg_max = sb("neg_max", [P, 2])
        row_max = sb("row_max", [P, 2])
        p_sum = sb("p_sum", [P, 2])
        p_inv = sb("p_inv", [P, 2])

        ctx_tok = scratch[:, 0:4096].rearrange("p (t n) -> p t n", t=NT)
        hf = scratch[:, 4096:5120].rearrange("p (b n) -> p b n", b=2)
        x_norm = scratch[:, 5120:6144].rearrange("p (b n) -> p b n", b=2)
        kt_sb = x_tok[:, 0, :].rearrange("p (h k) -> p h k", h=N_KV)
        v_sb = x_tok[:, 1, :].rearrange("p (k n) -> p k n", k=4)
        qt = scratch[:, 0:2048].rearrange("p (c h t) -> p c h t", c=2, h=4)
        k_tmp = scratch[:, 0:2048].rearrange("p (i n) -> p i n", i=4)
        q_tmp = scratch[:, 2048:3072].rearrange("p (t n) -> p t n", t=NT)
        rope_a, rope_b = scratch[:, 3072:3584], scratch[:, 3584:4096]
        probs = scratch[:, 4096:5120].rearrange("p (b k) -> p b k", b=2)
        probs_t = scratch[:, 5120:6144].rearrange("p (b k t) -> p b k t", b=2, k=4)
        u_sb = q_tmp
        pooled = scratch[:, 3072:4096].rearrange("p (g t) -> p g t", g=4)
        fold = gate_bc[:, 0:1024].rearrange("p (a t d) -> p a t d", a=4, t=NT)
        rope_raw = gate_bc[:, 1024:1536].rearrange("p (a t d) -> p a t d", a=2, t=NT)
        head_g = gate_bc[:, 1536:1792].rearrange("p (a d) -> p a d", a=2)
        pool_mat = tables[:, 0:2048].rearrange("p (g k t) -> p g k t", g=4, k=NT)
        w_pool = tables[:, 2048:2560].rearrange("p (g d) -> p g d", g=4)
        dft_cs = tables[:, 0:1024].rearrange("p (k n) -> p k n", k=2)
        dft_ns = tables[:, 1024:1536].rearrange("p (k n) -> p k n", k=2)
        silu_g = scratch[:, 0:1024].rearrange("p (t n) -> p t n", t=NT)
        hid_tok = scratch[:, 1024:2048].rearrange("p (t n) -> p t n", t=NT)
        res_tmp = scratch[:, 2048:3072].rearrange("p (t n) -> p t n", t=NT)
        final_g = scratch[:, 4096:6144]
        f_sb = scratch[:, 0:2048].rearrange("p (t n) -> p t n", t=NT)
        y_conv = scratch[:, 0:1024].rearrange("p (c t) -> p c t", c=4)
        odd_tmp = scratch[:, 3072:4096].rearrange("p (t n) -> p t n", t=NT)
        dft1 = scratch[:, 5120:6144].rearrange("p (q n) -> p q n", q=2)

        start_raw = [mod_raw[:, s, :, :] for s in range(RING)] + \
            [v[:, i * 1024:(i + 1) * 1024].rearrange("p (j n) -> p j n", j=SLAB_K)
             for v in (gate_bc, tables) for i in range(2)]

        part = [acc[:, 1, :], tables[:, 2048:2560]]

        norm_cols = colsA[:, 0:64]
        conv_cols = colsA[:, 64:88]
        pscale_cols = colsA[:, 88:92]

        def mod_vec(layer, v):
            n = layer * MOD_CHUNKS + v * ND
            return mod_cols[:, n:n + ND, :].rearrange("p n j -> p (n j)")

        bank = [stack.enter_context(nc.psum_tensor(f"bank{i}", [P, NC], f32)) for i in range(8)]
        B_COL, B_A, B_B, B_C = 4, 5, 6, 7

        raw_full = [sem(f"raw_full{i}") for i in range(RING)]
        hi_done, lo_done, slab_free = sem("hi_done"), sem("lo_done"), sem("slab_free")
        mod_full = [sem(f"mod_full{i}") for i in range(RING)]
        start_full = mod_full + [sem(f"start_full{i}") for i in range(RING, 8)]
        mod_step = sem("mod_step")
        mod_mm, mod_col_done = sem("mod_mm"), sem("mod_col_done")
        start_free, part_step, row_copied, row_mm, start_col = (
            sem("start_free"), sem("part_step"), sem("row_copied"), sem("row_mm"), sem("start_col"))
        pair_freed = [sem("pair0_freed"), sem("pair1_freed")]
        rows_in, x_in, rope_in, tab_in, wpool_in, x_again, fin_in, out_done = (
            sem("rows_in"), sem("x_in"), sem("rope_in"), sem("tab_in"), sem("wpool_in"),
            sem("x_again"), sem("fin_in"), sem("out_done"))
        c_in, c_t = sem("c_in"), sem("c_t")
        ident_ready, cols_t, cols_ready, silu_ready = (
            sem("ident_ready"), sem("cols_t"), sem("cols_ready"), sem("silu_ready"))
        tile0_done = sem("tile0_done")
        sq_done, rms_ready, norm_x, norm_t, norm_hf, norm_hi, h_ready = (
            sem("sq_done"), sem("rms_ready"), sem("norm_x"), sem("norm_t"), sem("norm_hf"), sem("norm_hi"),
            sem("h_ready"))
        v_self = sem("v_self")
        head_sums, rope_done = sem("head_sums"), sem("rope_done")
        kt_t, kt_in, qt_t, qt_in = sem("kt_t"), sem("kt_in"), sem("qt_t"), sem("qt_in")
        scores_done, max_done, exp_done, probs_done = (
            sem("scores_done"), sem("max_done"), sem("exp_done"), sem("probs_done"))
        pt_t, pt_in, pv_done, mix_hi, mix_lo = (
            sem("pt_t"), sem("pt_in"), sem("pv_done"), sem("mix_hi"), sem("mix_lo"))
        pool_mm = sem("pool_mm")
        gb_mm, gb_in = sem("gb_mm"), sem("gb_in")
        res_step = sem("res_step")
        hid_t, hid_hi, hid_lo = sem("hid_t"), sem("hid_hi"), sem("hid_lo")
        dft_a, dft_a_in, dft_y, u_conv_t, conv_done, bg_t, mixed = (
            sem("dft_a"), sem("dft_a_in"), sem("dft_y"), sem("u_conv_t"), sem("conv_done"), sem("bg_t"),
            sem("mixed"))
        x_final = sem("x_final")

        block = stack.enter_context(nc.Block())

        order = plan["even_out"] + [c for _, d in plan["ffn0"] for c in d] + plan["odd_out"] \
            + [c for _, d in plan["ffn1"] for c in d]
        res_no = {c.g: n + 1 for n, c in enumerate(order)}

        last_chunks = {c.g: n + 1 for n, c in enumerate((
            plan["even_out"][-1], plan["ffn0"][-1][1][-1], plan["odd_out"][-1], plan["ffn1"][-1][1][-1]))}

        EVEN_MIX = 24 + 4
        DFT_MIX = 4
        PART = 4 * START_DVE
        HID_CREDIT = 2

        def loop_chunks(gu, i):
            (gate, up), was = gu[1], gu[0][1]
            return (moved(gate, i, 16, 2, 1, 1, 1),
                    moved(up, i, 16, 2, 1, 0, 1)._replace(extra=up.extra + i),
                    moved(was, i, 16, 2, 1, 0, 1)._replace(extra=was.extra + i))

        def norm_groups(k):
            if k == 0:
                return [Group(n, n % 2, n // 2 * 2, 2, (0, 1)) for n in range(16)]
            blocks = [(0, 0), (0, 1), (1, 0), (1, 1), (0, 2), (1, 2), (0, 3), (1, 3)]
            return [Group(16 + 8 * (k - 1) + n, 0, 4 * g, 4, (t,)) for n, (t, g) in enumerate(blocks)]

        def start_groups(i):
            return norm_groups(0)[4 * i:4 * i + 2], norm_groups(0)[4 * i + 2:4 * i + 4]

        def norm_dest(h, g):
            return h[:, g.f0:g.f0 + g.nf, g.toks[0] * P:(g.toks[-1] + 1) * P]

        def norm_source(which):
            return (x_tok, ctx_tok)[which]

        def start_col_chunk(m):
            return m // 2 + ND * (m % 2)

        def acc_slot(c):
            return 0 if c.kind == "gate" else c.mods[-1] % 2

        @block.sync
        def _(sp):
            sp.wait_ge(cols_ready, 4)
            for src, r in ((c_d.rearrange("b (k p) -> (b k) p", p=P), 0),
                           (c_ctx_d.rearrange("(k p) -> k p", p=P), 16)):
                sp.dma_start(rows[r:r + 16, 3, :], src).then_inc(c_in, 16)
            for src, a, r, n in ((norm_g_d.rearrange("l s (k p) -> (l s k) p", p=P), 0, 0, 64),
                                 (conv_w_d.rearrange("o j (k p) -> (o j k) p", p=P), 0, 64, 24),
                                 (pool_scale_d.rearrange("o (k p) -> (o k) p", p=P), 0, 88, 4),
                                 (b_mod_d[0].rearrange("(k p) -> k p", p=P), 1, 0, 96),
                                 (b_mod_d[1].rearrange("(k p) -> k p", p=P), 2, 0, 96)):
                sp.dma_start(rows[r:r + n, a, :], src).then_inc(rows_in, 16)
            def load(c, view, col, row0=0):
                for s in range(c.n):
                    load_slab(c, s, view[col, row0 + s])

            def load_slab(c, s, src):
                if not isinstance(c.w0, int) or c.w0 + s >= RING:
                    sp.wait_ge(lo_done, c.w0 + (s - RING + 1))
                slot = (c.slot0 + s) % RING
                sp.dma_start(raw[:, slot, :, :], src).then_inc(raw_full[slot], 16)

            keys = plan["even_in"][0]
            for m in range(START_CHUNKS):
                for s in range(RING, 8):
                    if m > 0:
                        sp.wait_ge(start_free, START_PE * (m - 1) + s - START_DVE + 1)
                    sp.dma_start(start_raw[s], wv_mod[0][start_col_chunk(m), s]).then_inc(start_full[s], 16)
                if m == 0:
                    sp.dma_start(x_tok[:, :, :], x_d[0].rearrange("(t p) n -> p t n", p=P)).then_inc(x_in, 16)
                    sp.dma_start(ctx_tok, ctx_d[0].rearrange("(t p) n -> p t n", p=P)).then_inc(x_in, 16)
                else:
                    load_slab(keys, m - 1, wv_in_e[even_col["k"], m - 1])
            load_slab(keys, 7, wv_in_e[even_col["k"], 7])

            def ffn(layer):
                first = 0
                for gu, down in plan[f"ffn{layer}"]:
                    with sp.Fori(0, len(gu)) as i:
                        for c, view in zip(gu[0], (wv_gate, wv_up)):
                            load(moved(c, i, 16, 2, 1, 0, 1), view[layer], first + i)
                    for c in down:
                        load(c, wv_down[layer], c.idx, 2 * first)
                    first += len(gu)

            for c in plan["even_in"][1:]:
                load(c, wv_in_e, even_col[c.kind] + c.idx)
            for c in plan["even_out"]:
                load(c, wv_out_e, c.idx)
                if c.idx == 0:
                    sp.wait_ge(pv_done, 24)
                    sp.dma_start(x_tok[:, :, :], x_d[0].rearrange("(t p) n -> p t n", p=P)) \
                      .then_inc(x_again, 16)
            ffn(0)
            for c in plan["odd_in"]:
                load(c, wv_in_o, odd_col[c.kind] + c.idx)
            for c in plan["odd_out"]:
                load(c, wv_out_o, c.idx)
            ffn(1)
            for t in range(NT):
                for half in range(2):
                    cols = slice(half * D // 2, (half + 1) * D // 2)
                    sp.wait_ge(x_final, 2 * t + half + 1)
                    sp.dma_start(out_d[0, t * P:(t + 1) * P, cols], x_tok[:, t, cols]).then_inc(out_done, 16)
            sp.wait_ge(out_done, 16 * 2 * NT)

        @block.gpsimd
        def _(pool):
            def load_mod(view, n, s, slot):
                pool.dma_start(mod_raw[:, slot, :, :], view[n, s]).then_inc(mod_full[slot], 16)

            pool.memset(ident[:, :], 0.0).then_inc(ident_ready, 1)
            pool.wait_ge(ident_ready, 1)
            pool.affine_select(out=ident[:, :], in_=ident[:, :], compare_op=ALU.not_equal, fill=1.0,
                               base=0, pattern=[[-1, P]], channel_multiplier=1).then_inc(ident_ready, 1)
            for s in range(RING):
                load_mod(wv_mod[0], 0, s, s)

            def load_start(i, b, n):
                for s in range(START_DVE):
                    pool.wait_ge(part_step, i * (2 * PART) + (PART * b + 4 * (s + 1)))
                    load_mod(wv_mod[0], n, s, s)
                for s in range(START_DVE, RING):
                    pool.wait_ge(start_free, i * (2 * START_PE) + (START_PE * b + s - START_DVE + 1))
                    load_mod(wv_mod[0], n, s, s)

            with pool.Fori(0, ND - 1) as i:
                load_start(i, 0, i + ND)
                load_start(i, 1, i + 1)
            load_start(ND - 1, 0, START_CHUNKS - 1)
            load_start(ND - 1, 1, START_CHUNKS)

            def stream(layer, n0, count, q0):
                with pool.Fori(0, count) as i:
                    for s in range(8):
                        pool.wait_ge(mod_step, (i + q0) * 16 + 2 * (s - RING + 1))
                        load_mod(wv_mod[layer], i + n0, s, s % RING)

            n_rest = MOD_CHUNKS - START_CHUNKS
            for s in range(RING, 8):
                pool.wait_ge(mod_step, 2 * (s - RING + 1))
                load_mod(wv_mod[0], START_CHUNKS, s, s % RING)

            def norm_los(k):
                for g in norm_groups(k):
                    pool.wait_ge(norm_hi, g.n + 1)
                    pool.tensor_tensor(norm_dest(h_lo, g),
                                       hf[:, g.n % 2, :].rearrange("p (j q) -> p j q", j=g.nf),
                                       norm_dest(h_hi, g).bitcast(f32), ALU.subtract).then_inc(h_ready, 1)

            before = [next(c.mods[0] for c in chunks if c.mods) for chunks in
                      ([c for c, _ in plan["ffn0"][0][0]], plan["odd_in"], [c for c, _ in plan["ffn1"][0][0]])]
            stream(0, START_CHUNKS + 1, before[0] - 1, 1)
            norm_los(1)
            stream(0, START_CHUNKS + before[0], n_rest - before[0], before[0])
            stream(1, 0, before[1] - n_rest, n_rest)
            norm_los(2)
            stream(1, before[1] - n_rest, before[2] - before[1], before[1])
            norm_los(3)
            stream(1, before[2] - n_rest, n_rest + MOD_CHUNKS - before[2], before[2])

        @block.tensor
        def _(pe):
            drained = {}

            def take(b, reader, value):
                if b in drained:
                    pe.wait_ge(*drained[b])
                drained[b] = (reader, value)

            pe.wait_ge(ident_ready, 2)
            pe.wait_ge(cols_ready, 4)
            pe.wait_ge(c_in, 32)
            pe.transpose(bank[B_B][:, 0:P], rows[:, 3, :], ident[:, :]).then_inc(c_t, 1)
            pe.wait_ge(rows_in, 16 * 5)
            for a in range(3):
                op = pe.transpose(bank[B_A][:, a * P:(a + 1) * P], rows[:, a, :], ident[:, :])
            op.then_inc(cols_t, 1)
            pe.wait_ge(silu_ready, 2)
            def matvec(m):
                if m > 0:
                    pe.wait_ge(row_copied, m)
                for s in range(START_DVE, 8):
                    pe.wait_ge(start_full[s], (m + 1) * 16)
                    for j in range(SLAB_K):
                        k = SLAB_K * s + j
                        op = pe.matmul(bank[B_C][0:2, :], silu_c[:, k, :], start_raw[s][:, j, :],
                                       start=(k == SLAB_K * START_DVE), stop=(k == KT - 1))
                    op.then_inc(start_free, 1)

            def row_to_cols(m):
                pe.wait_ge(row_copied, m + 1)
                pe.wait_ge(part_step, PART * (m + 1))
                if m > 0:
                    pe.wait_ge(start_col, m)
                for j in range(4):
                    pe.matmul(bank[B_COL][:, 2 * j:2 * j + 2], acc[0:2, 0, j * P:(j + 1) * P],
                              ident[0:2, 0:2], start=True, stop=False)
                    for v in range(2):
                        op = pe.matmul(bank[B_COL][:, 2 * j + v:2 * j + v + 1],
                                       part[v][:, j * P:(j + 1) * P], ones[:, :], start=False, stop=(v == 1))
                op.then_inc(row_mm, 1)

            def norm_turn(groups):
                for g in groups:
                    b = B_A + g.n % 2
                    pe.wait_ge(norm_x, g.n + 1)
                    take(b, norm_hf, g.n + 1)
                    for j in range(g.nf):
                        for a in range(len(g.toks)):
                            to, at = (j * len(g.toks) + a) * P, (a * g.nf + j) * P
                            op = pe.transpose(bank[b][:, to:to + P], x_norm[:, g.n % 2, at:at + P],
                                              ident[:, :])
                    op.then_inc(norm_t, 1)

            def mod_columns(q, slot):
                take(B_COL, mod_col_done, q + 1)
                pe.wait_ge(mod_step, (q + 1) * 16)
                for j in range(4):
                    op = pe.matmul(bank[B_COL][:, j:j + 1], acc[:, slot, j * P:(j + 1) * P], ones[:, :],
                                   start=True, stop=True)
                op.then_inc(mod_mm, 1)

            def gemm_slab(c, s, groups, tiles=(0, 1)):
                pe.wait_ge(lo_done, c.w0 + s + 1)
                slot = (c.slot0 + s) % RING
                for j in range(SLAB_K):
                    k = SLAB_K * s + j
                    for a_hi, a_lo, pair in groups:
                        for t in tiles:
                            ps = bank[2 * pair + t][:, :]
                            ah, al = a_hi[:, k, t * P:(t + 1) * P], a_lo[:, k, t * P:(t + 1) * P]
                            last = s == c.n - 1 and j == SLAB_K - 1
                            pe.matmul(ps, ah, w_hi[:, slot, j, :], start=(k == 0), stop=False)
                            pe.matmul(ps, ah, w_lo[:, slot, j, :], start=False, stop=False)
                            op = pe.matmul(ps, al, w_hi[:, slot, j, :], start=False, stop=last)
                if 1 in tiles:
                    op.then_inc(slab_free, 1)
                elif s == c.n - 1:
                    op.then_inc(tile0_done, 1)

            def gemm(c, hi, lo, side, ready=None, both=None, norm=None, last=None):
                groups = [(hi, lo, c.pair)]
                if both:
                    groups.append((*both, 1 - c.pair))
                for _, _, pair in groups:
                    if not isinstance(c.use, int) or c.use > 0:
                        pe.wait_ge(pair_freed[pair], c.use)
                by_tile = range(0, RING) if norm else range(c.n - RING, c.n) if last else ()
                steps = [(s, (0, 1)) for s in range(c.n) if s not in by_tile]
                halves = [(s, (t,)) for t in range(NT) for s in by_tile]
                steps = halves + steps if norm else steps + halves
                if norm:
                    every = norm_groups(norm)
                    norm_turn(every[:2])
                for s, tiles in steps:
                    if ready and s in ready:
                        for w in ready[s]:
                            pe.wait_ge(*w)
                    if norm:
                        for e in NORM_READS.get((s, tiles[-1]), ()):
                            pe.wait_ge(h_ready, every[e].n + 1)
                    gemm_slab(c, s, groups, tiles)
                    if norm and (s, tiles[-1]) in NORM_TURNS:
                        norm_turn([every[NORM_TURNS[s, tiles[-1]]]])
                    if 1 in tiles:
                        side(s)
                    if last and s == c.n - RING and tiles == (1,):
                        last()

            def mods_at(c, prev, s):
                if s == 0 and prev is not None and prev.mods:
                    mod_columns(prev.mods[-1], acc_slot(prev))
                if s == 4 and c is not None and len(c.mods) == 2:
                    mod_columns(c.mods[0], c.mods[0] % 2)

            def gate_columns(layer, v, n, value):
                take(B_C, gb_in, value)
                g = mod_vec(layer, v)
                if n == 0:
                    pe.wait_ge(mod_col_done, layer * MOD_CHUNKS + (v + 1) * ND - START_CHUNKS)
                for j in range(4):
                    ft = 4 * n + j
                    op = pe.matmul(bank[B_C][:, j * P:(j + 1) * P], g[:, ft:ft + 1].broadcast_to([P, P]),
                                   ident[:, :], start=True, stop=True)
                op.then_inc(gb_mm, 1)

            def transposes(bk, src, count, sem_):
                for j in range(count):
                    op = pe.transpose(bank[bk][:, j * P:(j + 1) * P], src(j), ident[:, :])
                op.then_inc(sem_, 1)

            def key_slab(s):
                pe.wait_ge(h_ready, 2 * s + 2)
                gemm_slab(plan["even_in"][0], s, [(h_hi, h_lo, 0), (m_hi, m_lo, 1)])

            drained[B_A] = (cols_ready, 5)
            for i in range(ND):
                matvec(2 * i)
                if i > 0:
                    norm_turn(start_groups(i - 1)[1])
                    key_slab(2 * i - 2)
                row_to_cols(2 * i)
                matvec(2 * i + 1)
                if 0 < i < ND - 1:
                    key_slab(2 * i - 1)
                row_to_cols(2 * i + 1)
                norm_turn(start_groups(i)[0])
            key_slab(5)
            norm_turn(start_groups(ND - 1)[1])
            drained[B_COL] = (start_col, START_CHUNKS)
            drained[B_C] = (row_copied, START_CHUNKS)
            for s in range(6, 8):
                key_slab(s)

            def unit(i):
                if 0 <= i - 3 < 24:
                    u = i - 3
                    pe.wait_ge(pt_in, u + 1)
                    take(B_C, mix_lo, u + 1)
                    kv = (4 * (u // 8) + u % 4) // 3
                    for k in range(4):
                        op = pe.matmul(bank[B_C][:, 0:P], v_sb[:, k, kv * P:(kv + 1) * P],
                                       probs_t[:, u % 2, k, :], start=(k == 0), stop=(k == 3))
                    op.then_inc(pv_done, 1)
                if 0 <= i - 2 < 24:
                    u = i - 2
                    pe.wait_ge(probs_done, u + 1)
                    take(B_B, pt_in, u + 1)
                    transposes(B_B, lambda j: probs[:, u % 2, j * P:(j + 1) * P], 4, pt_t)
                if 0 <= i < 24:
                    c, t, h = i // 8, (i // 4) % 2, i % 4
                    if i == 0:
                        pe.wait_ge(kt_in, 4)
                    pe.wait_ge(qt_in, 2 * c + t + 1)
                    take(B_A, exp_done, i + 1)
                    pe.matmul(bank[B_A][:, :], qt[:, c % 2, h, t * P:(t + 1) * P],
                              kt_sb[:, (4 * c + h) // 3, :], start=True, stop=True).then_inc(scores_done, 1)

            def q_turn(c, t):
                pe.wait_ge(rope_done, 4 + 2 * c + t + 1)
                take(B_COL, qt_in, 2 * c + t + 1)
                transposes(B_COL, lambda j: q_tmp[:, t, j * P:(j + 1) * P], 4, qt_t)

            prev = plan["even_in"][0]
            for n, c in enumerate(plan["even_in"][1:], 1):
                def side(s, c=c, n=n, prev=prev):
                    mods_at(c, prev, s)
                    if n == 2 and s < 4:
                        pe.wait_ge(rope_done, s + 1)
                        take(B_B, kt_in, s + 1)
                        transposes(B_B, lambda j: k_tmp[:, s, j * P:(j + 1) * P], 4, kt_t)
                    if n >= 3 and s in (5, 7):
                        q_turn(n - 3, (s - 5) // 2)
                    if n >= 4:
                        unit(8 * (n - 4) + s)
                gemm(c, h_hi, h_lo, side, both=(m_hi, m_lo) if n < 2 else None)
                prev = c
            pool_use, rest = plan["pool_use"], plan["rest_mods"]
            for i in range(16, 28):
                mods_at(None, prev, i - 16)
                if i in (23, 27):
                    q = rest[(i - 23) // 4]
                    mod_columns(q, q % 2)
                if i == 24:
                    pe.wait_ge(pair_freed[prev.pair], prev.use + 1)
                    pe.wait_ge(tab_in, 16)
                    pe.wait_ge(pair_freed[0], pool_use[0])
                    for g in range(4):
                        for k in range(NT):
                            op = pe.matmul(bank[g // 2][:, (g % 2) * T:(g % 2 + 1) * T],
                                           u_sb[:, k, g * P:(g + 1) * P], pool_mat[:, g, k, :],
                                           start=(k == 0), stop=(k == NT - 1))
                    op.then_inc(pool_mm, 1)
                unit(i)
            pe.wait_ge(pair_freed[0], pool_use[0] + 1)
            pe.wait_ge(wpool_in, 16)
            pe.wait_ge(pair_freed[1], pool_use[1])
            for g in range(4):
                op = pe.matmul(bank[2 + g // 2][:, (g % 2) * T:(g % 2 + 1) * T], w_pool[:, g, :],
                               pooled[:, g, :], start=True, stop=True)
            op.then_inc(pool_mm, 1)

            gates_made = 0

            def res_side(c, prev, layer, v, s):
                nonlocal gates_made
                mods_at(c, prev, s)
                if "gate" in c.extra and s == 4:
                    gate_columns(layer, v, c.idx, gates_made + 1)
                    gates_made += 1

            prev = plan["even_out"][0]._replace(mods=rest[2:])
            for c in plan["even_out"]:
                gemm(c, m_hi, m_lo, lambda s: res_side(c, prev, 0, 2, s),
                     {0: [(mix_lo, 24)], 6: [(mix_lo, EVEN_MIX)]} if c.idx == 0 else None,
                     last=(lambda: mods_at(None, c, 0)) if c.idx == ND - 1 else None)
                prev = c

            def hid_turn(up):
                h = up.extra
                pe.wait_ge(pair_freed[1], up.use + 1)
                for t in range(NT):
                    take(B_A + t, hid_lo, HID_CREDIT + 2 * h + t + 1)
                    transposes(B_A + t, lambda j: hid_tok[:, t, j * P:(j + 1) * P], 4, hid_t)

            def ffn(layer, k):
                for sp_n, (gu, down) in enumerate(plan[f"ffn{layer}"]):
                    def gate_up(gate, up, was, norm=None):
                        def side(s):
                            if was and s == 1:
                                hid_turn(was)
                        gemm(gate, h_hi, h_lo, side, norm=norm)
                        gemm(up, h_hi, h_lo, lambda s: mods_at(None, gate, s))

                    gate_up(*gu[0], None, k if sp_n == 0 else None)
                    with pe.Fori(0, len(gu) - 1) as i:
                        gate, up, was = loop_chunks(gu, i)
                        for t in range(NT):
                            drained[B_A + t] = (hid_lo, HID_CREDIT + 2 * was.extra + t - 1)
                        if gate.mods:
                            drained[B_COL] = (mod_col_done, gate.mods[0])
                        gate_up(gate, up, was)
                    gate, up = gu[-1]
                    h = up.extra
                    for t in range(NT):
                        drained[B_A + t] = (hid_lo, HID_CREDIT + 2 * h + t - 1)
                    if gate.mods:
                        drained[B_COL] = (mod_col_done, gate.mods[0] + 1)
                    prev = None
                    for c in down:
                        def side(s):
                            if c.idx == 0 and s == 1:
                                hid_turn(up)
                            res_side(c, prev, layer, 5, s)
                        ready = {0: [(hid_lo, HID_CREDIT + 2 * h)],
                                 2 * (len(gu) - 1): [(hid_lo, HID_CREDIT + 2 * h + 2)]} \
                            if c.idx == 0 else None
                        gemm(c, m_hi, m_lo, side, ready,
                             last=(lambda: None) if sp_n == len(SPLITS) - 1 and c.idx == ND - 1 else None)
                        prev = c

            ffn(0, 1)

            def dft_side(i):
                g, r = divmod(i, 4)
                if g >= 4:
                    return
                if r == 0:
                    f = plan["odd_in"][g // 2]
                    pe.wait_ge(pair_freed[f.pair], f.use + 1)
                    if g == 0:
                        pe.wait_ge(tab_in, 48)
                    for q in range(2):
                        take(B_A + q, dft_a_in, 2 * g + q + 1)
                        for k in range(NT):
                            ch = g * 256 + q * P
                            op = pe.matmul(bank[B_A + q][:, :], f_sb[:, k, ch:ch + P], dft_cs[:, k, :],
                                           start=(k == 0), stop=(k == NT - 1))
                        op.then_inc(dft_a, 1)
                if r == 2:
                    pe.wait_ge(dft_a_in, 2 * g + 2)
                    take(B_C, mix_lo, EVEN_MIX + g + 1)
                    for o in range(2):
                        for q in range(2):
                            pe.matmul(bank[B_C][:, o * T:(o + 1) * T], dft_cs[:, q, o * P:(o + 1) * P],
                                      dft1[:, q, 0:T], start=(q == 0), stop=False)
                            op = pe.matmul(bank[B_C][:, o * T:(o + 1) * T], dft_ns[:, q, o * P:(o + 1) * P],
                                           dft1[:, q, T:2 * T], start=False, stop=(q == 1))
                    op.then_inc(dft_y, 1)

            def conv_turn(src, t_sem, reader, value):
                pe.wait_ge(pair_freed[src.pair], src.use + 1)
                for b in range(2):
                    take(B_A + b, reader, value(b))
                    for j in range(2):
                        for t in range(NT):
                            ct = 2 * b + j
                            op = pe.transpose(bank[B_A + b][:, j * T + t * P:j * T + (t + 1) * P],
                                              odd_tmp[:, t, ct * P:(ct + 1) * P], ident[:, :])
                    op.then_inc(t_sem, 1)

            prev = None
            for n, c in enumerate(plan["odd_in"]):
                def side(s, c=c, n=n, prev=prev):
                    mods_at(c, prev, s)
                    if n >= 2:
                        dft_side(8 * (n - 2) + s)
                    if c.kind == "bg" and s == 2:
                        conv_turn(prev, u_conv_t, conv_done, lambda b: 4 * c.idx + 2 * b + 2)
                    if c.kind == "cg" and c.idx == 1 and s == 1:
                        conv_turn(prev, bg_t, mixed, lambda b: b + 1)
                gemm(c, h_hi, h_lo, side, norm=2 if n == 0 else None)
                prev = c
            for c in plan["odd_out"]:
                def side(s, c=c, prev=prev):
                    if c.idx == 0 and s == 1:
                        conv_turn(prev, bg_t, mixed, lambda b: 2 + b + 1)
                    res_side(c, prev, 1, 2, s)
                gemm(c, m_hi, m_lo, side,
                     {0: [(mix_lo, EVEN_MIX + DFT_MIX + 4)], 6: [(mix_lo, EVEN_MIX + DFT_MIX + 8)]}
                     if c.idx == 0 else None,
                     last=(lambda: mods_at(None, c, 0)) if c.idx == ND - 1 else None)
                prev = c
            ffn(1, 3)

        @block.scalar
        def _(act):
            act.wait_ge(c_t, 1)
            for v in range(2):
                act.activation(silu_c[:, :, v], bank[B_B][:, 16 * v:16 * v + 16], ACT.Silu) \
                   .then_inc(silu_ready, 1)

            def hi(c, s):
                slot = (c.slot0 + s) % RING
                if not isinstance(c.w0, int) or c.w0 + s >= RING:
                    act.wait_ge(slab_free, c.w0 + (s - RING + 1))
                act.wait_ge(raw_full[slot], (c.round0 + (c.slot0 + s) // RING + 1) * 16)
                act.activation(w_hi[:, slot, :, :], raw[:, slot, :, :], ACT.Copy).then_inc(hi_done, 1)

            squared = summed = 0

            def square(which, t, n):
                nonlocal squared
                if squared:
                    act.wait_ge(sq_done, squared)
                squared += 1
                act.activation(junk[:, :], norm_source(which)[:, t, n * NC:(n + 1) * NC], ACT.Square,
                               accum_out=sumsq[:, which, t, n:n + 1]).then_inc(sq_done, 1)

            def chunk(c, at, start=0):
                if start:
                    hi(c, start)
                for s in range(start, c.n):
                    if not start:
                        hi(c, s)
                    elif s + 1 < c.n:
                        hi(c, s + 1)
                    at(s)

            def norm_scaled(k, g):
                act.wait_ge(rms_ready, 2 * g.which + 2 if k == 0 else 4 + 2 * (k - 1) + g.toks[0] + 1)
                if g.n >= 2:
                    act.wait_ge(norm_t, g.n - 1)
                for a, t in enumerate(g.toks):
                    op = act.activation(x_norm[:, g.n % 2, a * g.nf * P:(a + 1) * g.nf * P],
                                        norm_source(g.which)[:, t, g.f0 * P:(g.f0 + g.nf) * P],
                                        ACT.Copy, scale=rms[:, g.which, t:t + 1])
                op.then_inc(norm_x, 1)

            def norm_hi_half(g):
                act.wait_ge(norm_hf, g.n + 1)
                act.activation(norm_dest((h_hi, m_hi)[g.which], g),
                               hf[:, g.n % 2, :].rearrange("p (j q) -> p j q", j=g.nf), ACT.Copy) \
                   .then_inc(norm_hi, 1)

            def norm_his(k, groups):
                every = norm_groups(k)
                for g in groups:
                    norm_hi_half(g)
                    ahead = g.n - every[0].n + 2
                    if ahead < len(every):
                        norm_scaled(k, every[ahead])

            def head_sum(src, i):
                nonlocal summed
                if summed:
                    act.wait_ge(head_sums, summed)
                summed += 1
                for h in range(4):
                    op = act.activation(junk[:, h * P:(h + 1) * P], src[:, h * P:(h + 1) * P], ACT.Square,
                                        accum_out=head_sq[:, i, h:h + 1])
                op.then_inc(head_sums, 1)

            def unit(i):
                if 0 <= i - 6 < 24:
                    u = i - 6
                    act.wait_ge(pt_t, u + 1)
                    if u >= 2:
                        act.wait_ge(pv_done, u - 1)
                    act.activation(probs_t[:, u % 2, :, :],
                                   bank[B_B][:, :].rearrange("p (k t) -> p k t", k=4), ACT.Copy) \
                       .then_inc(pt_in, 1)
                if 0 <= i - 7 < 24:
                    u = i - 7
                    act.wait_ge(pv_done, u + 1)
                    h, t = 4 * (u // 8) + u % 4, (u // 4) % 2
                    act.activation(m_hi[:, h, t * P:(t + 1) * P], bank[B_C][:, 0:P], ACT.Copy) \
                       .then_inc(mix_hi, 1)
                if 0 <= i - 4 < 24:
                    u = i - 4
                    act.wait_ge(max_done, u + 1)
                    if u >= 2:
                        act.wait_ge(pt_t, u - 1)
                    act.activation(probs[:, u % 2, :], bank[B_A][:, :], ACT.Exp, scale=SCALE,
                                   bias=neg_max[:, u % 2:u % 2 + 1],
                                   accum_out=p_sum[:, u % 2:u % 2 + 1]).then_inc(exp_done, 1)

            def even_at(n, prev, s):
                if n == 1:
                    if s == 0:
                        act.wait_ge(slab_free, prev.w0 + prev.n)
                        for t in range(NT):
                            op = act.activation(k_tmp[:, t, :], bank[t][:, :], ACT.Copy)
                        op.then_inc(pair_freed[0], 1)
                    if s in (4, 6):
                        act.wait_ge(pair_freed[(s - 4) // 2], 1)
                        for i in (s - 4, s - 3):
                            head_sum(k_tmp[:, i, :], i)
                if n == 2:
                    if s == 0:
                        act.wait_ge(slab_free, prev.w0 + prev.n)
                        for t in range(NT):
                            op = act.activation(v_sb[:, 2 + t, :], bank[t][:, :], ACT.Copy)
                        op.then_inc(pair_freed[0], 1)
                    if 4 <= s:
                        i = s - 4
                        act.wait_ge(kt_t, i + 1)
                        at = 2 * P + i * P if i < 2 else (i - 2) * P
                        act.activation(kt_sb[:, :, at:at + P],
                                       bank[B_B][:, :].rearrange("p (h k) -> p h k", h=4), ACT.Copy) \
                           .then_inc(kt_in, 1)
                if n >= 3 and s == 3:
                    c = n - 3
                    act.wait_ge(slab_free, prev.w0 + prev.n)
                    if c > 0:
                        act.wait_ge(qt_t, 2 * c)
                    for t in range(NT):
                        op = act.activation(q_tmp[:, t, :], bank[2 * prev.pair + t][:, :], ACT.Copy)
                    op.then_inc(pair_freed[prev.pair], 1)
                    act.wait_ge(pair_freed[prev.pair], prev.use + 1)
                    for t in range(NT):
                        head_sum(q_tmp[:, t, :], t)
                if n >= 4 and s in (1, 3):
                    c, t = n - 4, (s - 1) // 2
                    act.wait_ge(qt_t, 2 * c + t + 1)
                    act.activation(qt[:, c % 2, :, t * P:(t + 1) * P],
                                   bank[B_COL][:, :].rearrange("p (h k) -> p h k", h=4), ACT.Copy) \
                       .then_inc(qt_in, 1)
                if n >= 4:
                    unit(8 * (n - 4) + s)

            even_in, even_out = plan["even_in"], plan["even_out"]

            def start_row(m):
                act.wait_ge(start_free, (m + 1) * START_PE)
                if m > 0:
                    act.wait_ge(row_mm, m)
                act.activation(acc[0:2, 0, :], bank[B_C][0:2, :], ACT.Copy).then_inc(row_copied, 1)

            for i in range(ND):
                start_row(2 * i)
                if i > 0:
                    norm_his(0, start_groups(i - 1)[1])
                if i == 0:
                    for which in range(2):
                        act.wait_ge(x_in, 32)
                        for t in range(NT):
                            for n in range(ND):
                                square(which, t, n)
                else:
                    hi(even_in[0], 2 * i)
                start_row(2 * i + 1)
                if i == 0:
                    for group in norm_groups(0)[:2]:
                        norm_scaled(0, group)
                norm_his(0, start_groups(i)[0])
                if i == 0:
                    hi(even_in[0], 0)
                hi(even_in[0], 2 * i + 1)
            norm_his(0, start_groups(ND - 1)[1])
            act.wait_ge(row_mm, START_CHUNKS)
            act.dma_start(head_g[:, 0, :], q_g_d[0:1, :].broadcast_to([P, HD])).then_inc(rope_in, 16)
            act.dma_start(head_g[:, 1, :], k_g_d[0:1, :].broadcast_to([P, HD])).then_inc(rope_in, 16)
            act.dma_start(rope_raw[:, 0, :, :], rope_cos_d.rearrange("(t p) d -> p t d", p=P)) \
               .then_inc(rope_in, 16)
            act.dma_start(rope_raw[:, 1, :, :], rope_sin_d.rearrange("(t p) d -> p t d", p=P)) \
               .then_inc(rope_in, 16)
            act.dma_start(pool_mat, pool_mat_d.rearrange("g (k p) t -> p g k t", p=P)).then_inc(tab_in, 16)
            act.dma_start(w_pool, w_pool_d[0].rearrange("g c d -> c g d")).then_inc(wpool_in, 16)

            prev = even_in[0]
            for n, c in enumerate(even_in[1:], 1):
                chunk(c, lambda s: even_at(n, prev, s))
                prev = c
            for i in range(16, 32):
                if i < 16 + RING:
                    hi(even_out[0], i - 16)
                if i in (17, 19):
                    c, t = 2, (i - 17) // 2
                    act.wait_ge(qt_t, 2 * c + t + 1)
                    act.activation(qt[:, 0, :, t * P:(t + 1) * P],
                                   bank[B_COL][:, :].rearrange("p (h k) -> p h k", h=4), ACT.Copy) \
                       .then_inc(qt_in, 1)
                if i == 19:
                    act.wait_ge(slab_free, prev.w0 + prev.n)
                    for t in range(NT):
                        op = act.activation(u_sb[:, t, :], bank[2 * prev.pair + t][:, :], ACT.Copy)
                    op.then_inc(pair_freed[prev.pair], 1)
                unit(i)
                if i == 28:
                    act.wait_ge(pool_mm, 1)
                    for b in range(2):
                        op = act.activation(pooled[:, 2 * b:2 * b + 2, :],
                                            bank[b][:, :].rearrange("p (g t) -> p g t", g=2), ACT.Copy)
                    op.then_inc(pair_freed[0], 1)
            act.wait_ge(pool_mm, 2)
            for g in range(4):
                act.activation(m_hi[:, N_HEADS + g, :], bank[2 + g // 2][:, (g % 2) * T:(g % 2 + 1) * T],
                               ACT.Copy, scale=pscale_cols[:, g:g + 1]).then_inc(mix_hi, 1)

            gates_made = 0

            def gate_copy(n):
                nonlocal gates_made
                gates_made += 1
                act.wait_ge(gb_mm, gates_made)
                act.activation(gate_bc[:, n * NC:(n + 1) * NC], bank[B_C][:, :], ACT.Copy) \
                   .then_inc(gb_in, 1)

            def res_at(prev, s):
                if prev is None:
                    return
                if s == 0 and "gate" in prev.extra:
                    gate_copy(prev.idx)
                if s == 4 and "stats" in prev.extra:
                    for t in range(NT):
                        res_square(prev, t)

            def res_square(prev, t):
                act.wait_ge(res_step, 2 * (res_no[prev.g] - 1) + t + 1)
                square(0, t, prev.idx)

            def res_phase(chunks, first_at, start):
                prev = None
                for c in chunks:
                    chunk(c, (lambda s: res_at(prev, s)) if prev else first_at, start if prev is None else 0)
                    prev = c
                if "gate" in prev.extra:
                    gate_copy(prev.idx)
                return prev._replace(extra=prev.extra.replace("gate", ""))

            def turn_over(prev, nxt, k):
                e = norm_groups(k)
                res_square(prev, 0)
                hi(nxt, 0)
                norm_scaled(k, e[0])
                norm_scaled(k, e[1])
                hi(nxt, 1)
                norm_hi_half(e[0])
                norm_hi_half(e[1])
                res_square(prev, 1)
                hi(nxt, 2)
                hi(nxt, 3)
                norm_scaled(k, e[2])
                norm_scaled(k, e[3])
                norm_his(k, e[2:4])

            prev = res_phase(even_out, lambda s: None, RING)

            def hid_copy(h, i):
                for t in range(NT):
                    act.wait_ge(hid_t, 2 * h + t + 1)
                    dst = m_hi[:, :, t * P:(t + 1) * P].rearrange("p (c k) q -> p c k q", k=4)
                    act.activation(dst[:, i, :, :], bank[B_A + t][:, :].rearrange("p (k q) -> p k q", k=4),
                                   ACT.Copy).then_inc(hid_hi, 1)

            def ffn(layer, k):
                prev, start = None, RING
                for gu, down in plan[f"ffn{layer}"]:
                    def gate_up(gate, up, was, start=0):
                        def gate_at(s):
                            if start and s >= 4:
                                norm_his(k, [norm_groups(k)[s]])
                            if was is not None and was.kind == "res":
                                res_at(was, s)
                            elif was is not None and s == 5:
                                hid_copy(was.extra, was.idx)

                        def up_at(s):
                            if s == 3:
                                act.wait_ge(slab_free, gate.w0 + gate.n)
                                act.wait_ge(pair_freed[1], up.use)
                                for t in range(NT):
                                    op = act.activation(silu_g[:, t, :], bank[t][:, :], ACT.Silu)
                                op.then_inc(pair_freed[0], 1)

                        chunk(gate, gate_at, start)
                        chunk(up, up_at)

                    gate_up(*gu[0], prev, start)
                    if start and layer == 1:
                        act.wait_ge(h_ready, norm_groups(3)[-1].n + 1)
                        act.dma_start(final_g, final_g_d.rearrange("(a n) -> a n", a=1)
                                      .broadcast_to([P, D])).then_inc(fin_in, 16)
                    start = 0
                    with act.Fori(0, len(gu) - 1) as i:
                        gate_up(*loop_chunks(gu, i))
                    up = gu[-1][1]
                    prev = res_phase(down, lambda s: hid_copy(up.extra, up.idx) if s == 5 else None, 0)
                return prev

            turn_over(prev, plan["ffn0"][0][0][0][0], 1)
            act.dma_start(dft_cs, dft_d[:, 0:512].rearrange("(k p) n -> p k n", p=P)).then_inc(tab_in, 16)
            act.dma_start(dft_ns, dft_d[:, 512:768].rearrange("(k p) n -> p k n", p=P)).then_inc(tab_in, 16)
            prev = ffn(0, 1)
            odd_in, odd_out = plan["odd_in"], plan["odd_out"]
            turn_over(prev, odd_in[0], 2)

            def odd_at(n, prev, s):
                if n == 0 and s >= 4:
                    norm_his(2, [norm_groups(2)[s]])
                i = 8 * (n - 2) + s
                if i >= 4 and i % 4 == 0 and i // 4 - 1 < 4:
                    g = i // 4 - 1
                    act.wait_ge(dft_a, 2 * g + 1)
                    if g > 0:
                        act.wait_ge(dft_y, g)
                    act.activation(dft1[:, 0, :], bank[B_A][:, :], ACT.Copy).then_inc(dft_a_in, 1)
                if i >= 6 and (i - 6) % 4 == 0 and (i - 6) // 4 < 4:
                    g = (i - 6) // 4
                    act.wait_ge(dft_y, g + 1)
                    act.activation(m_hi[:, 2 * g:2 * g + 2, :],
                                   bank[B_C][:, :].rearrange("p (o t) -> p o t", o=2), ACT.Copy) \
                       .then_inc(mix_hi, 1)
                if prev is not None and s == 3:
                    half = prev.idx
                    banks = [bank[2 * prev.pair + t][:, :] for t in range(NT)]
                    if prev.kind in ("f", "cg", "bg"):
                        act.wait_ge(slab_free, prev.w0 + prev.n)
                        if prev.kind == "cg" and half == 1:
                            act.wait_ge(bg_t, 2)
                        if prev.kind == "bg":
                            act.wait_ge(u_conv_t, 2 * half + 2)
                        for t in range(NT):
                            dst = f_sb[:, t, half * NC:(half + 1) * NC] if prev.kind == "f" else odd_tmp[:, t, :]
                            op = act.activation(dst, banks[t], ACT.Copy)
                        op.then_inc(pair_freed[prev.pair], 1)
                if prev is not None and prev.kind == "bg" and s == 6:
                    mixed_hi(prev.idx)

            def mixed_hi(half):
                for b in range(2):
                    act.wait_ge(mixed, 2 * half + b + 1)
                    for j in range(2):
                        ct = 2 * b + j
                        act.activation(m_hi[:, 8 + 4 * half + ct, :], y_conv[:, ct, :], ACT.Copy) \
                           .then_inc(mix_hi, 1)

            prev = None
            for n, c in enumerate(odd_in):
                chunk(c, lambda s: odd_at(n, prev, s), RING if n == 0 else 0)
                prev = c
            prev = res_phase(odd_out, lambda s: odd_at(8, odd_in[-1], s), 0)
            turn_over(prev, plan["ffn1"][0][0][0][0], 3)
            prev = ffn(1, 3)
            for t in range(NT):
                res_square(prev, t)

        @block.vector
        def _(dve):
            steps = 0

            def own(op):
                nonlocal steps
                op.then_inc(v_self, 1)
                steps += 1

            def own_wait():
                dve.wait_ge(v_self, steps)

            def lo(c, s):
                slot = (c.slot0 + s) % RING
                dve.wait_ge(hi_done, c.w0 + s + 1)
                dve.tensor_tensor(w_lo[:, slot, :, :], raw[:, slot, :, :], w_hi[:, slot, :, :].bitcast(f32),
                                  ALU.subtract).then_inc(lo_done, 1)

            dve.memset(ones[:, :], 1.0).then_inc(hid_lo, HID_CREDIT)
            for a in (3, 0, 1, 2):
                dve.memset(rows[:, a, :], 0.0).then_inc(cols_ready, 1)
            dve.wait_ge(cols_t, 1)
            dve.tensor_copy(colsA[:, :], bank[B_A][:, 0:P])
            for l in range(2):
                op = dve.tensor_copy(bias_cols[:, l * MOD_CHUNKS:(l + 1) * MOD_CHUNKS, :].rearrange(
                    "p n j -> p (n j)"), bank[B_A][:, (1 + l) * P:(1 + l) * P + 96])
            op.then_inc(cols_ready, 1)

            def guess_rsqrt(y, x, n):
                own(dve.tensor_scalar(guess[:, 0:n], x.bitcast(i32), 1, None, ALU.logical_shift_right))
                own_wait()
                own(dve.tensor_scalar(y.bitcast(i32), guess[:, 0:n], -1.0, float(0x5F3759DF), ALU.mult,
                                      ALU.add))
                own_wait()

            def rsqrt(y, x, n):
                guess_rsqrt(y, x, n)
                for _ in range(3):
                    own(dve.tensor_tensor(newton[:, 0:n], y, y, ALU.mult))
                    own_wait()
                    own(dve.scalar_tensor_tensor(out=newton[:, 0:n], in0=newton[:, 0:n], scalar=-0.5, in1=x,
                                                 op0=ALU.mult, op1=ALU.mult))
                    own_wait()
                    own(dve.scalar_tensor_tensor(out=y, in0=newton[:, 0:n], scalar=1.5, in1=y,
                                                 op0=ALU.add, op1=ALU.mult))
                    own_wait()

            def stream_rms(which, t, sq_count):
                dve.wait_ge(sq_done, sq_count)
                ms, y = msq[:, which, t:t + 1], rms[:, which, t:t + 1]
                own(dve.tensor_reduce(ms, sumsq[:, which, t, :], AX.X, ALU.add))
                own_wait()
                own(dve.tensor_scalar(ms, ms, 1.0 / D, EPS, ALU.mult, ALU.add))
                own_wait()
                own(dve.tensor_scalar(minus_half, ms, -0.5, None, ALU.mult))
                guess_rsqrt(y, ms, 1)
                for n in range(3):
                    own(dve.scalar_tensor_tensor(out=newton[:, 0:1], in0=y, scalar=y, in1=minus_half,
                                                 op0=ALU.mult, op1=ALU.mult))
                    own_wait()
                    op = dve.scalar_tensor_tensor(out=y, in0=newton[:, 0:1], scalar=1.5, in1=y,
                                                  op0=ALU.add, op1=ALU.mult)
                    if n < 2:
                        own(op)
                        own_wait()
                    else:
                        op.then_inc(rms_ready, 1)

            def scale_col(which, norm_w, scale, tiles=slice(0, KT)):
                own(dve.scalar_tensor_tensor(out=s_col[:, which, tiles], in0=scale[:, tiles], scalar=1.0,
                                             in1=norm_w[:, tiles], op0=ALU.add, op1=ALU.mult))
                own_wait()

            def norm_modulated(g, shift):
                if g.n >= 2:
                    dve.wait_ge(h_ready, g.n - 1)
                dve.wait_ge(norm_t, g.n + 1)
                width = len(g.toks) * P
                for j in range(g.nf):
                    cols, ft = slice(j * width, (j + 1) * width), g.f0 + j
                    op = dve.tensor_scalar(hf[:, g.n % 2, cols], bank[B_A + g.n % 2][:, cols],
                                           s_col[:, g.which, ft:ft + 1], shift[:, ft:ft + 1],
                                           ALU.mult, ALU.add)
                op.then_inc(norm_hf, 1)

            def norm_lo_half(g):
                dve.wait_ge(norm_hi, g.n + 1)
                dve.tensor_tensor(norm_dest((h_lo, m_lo)[g.which], g),
                                  hf[:, g.n % 2, :].rearrange("p (j q) -> p j q", j=g.nf),
                                  norm_dest((h_hi, m_hi)[g.which], g).bitcast(f32), ALU.subtract) \
                   .then_inc(h_ready, 1)

            def norm_step(groups, shifts):
                for g in groups:
                    norm_modulated(g, shifts[g.which])
                for g in groups:
                    if g.n < 16:
                        norm_lo_half(g)

            def norm_w(layer, sub):
                o = (2 * layer + sub) * KT
                return norm_cols[:, o:o + KT]

            def mod_slab(q, sl, slot, strict):
                dve.wait_ge(mod_full[sl % RING], (q * 2 + (START_CHUNKS + sl // RING + 1)) * 16)
                if sl == 0:
                    if strict:
                        dve.wait_ge(mod_mm, q)
                    elif q >= 2:
                        dve.wait_ge(mod_mm, q - 1)
                    else:
                        dve.wait_ge(row_mm, START_CHUNKS)
                for j in range(SLAB_K):
                    k = SLAB_K * sl + j
                    w = mod_raw[:, sl % RING, j, :]
                    if k == 0:
                        dve.tensor_scalar(acc[:, slot, :], w, silu_c[:, 0, 0:1], None, ALU.mult) \
                           .then_inc(mod_step, 1)
                    else:
                        dve.wait_ge(mod_step, q * 16 + k)
                        dve.scalar_tensor_tensor(out=acc[:, slot, :], in0=w, scalar=silu_c[:, k, 0:1],
                                                 in1=acc[:, slot, :], op0=ALU.mult, op1=ALU.add) \
                           .then_inc(mod_step, 1)

            def chunk(c, at, start=0):
                total, done = 8 * len(c.mods), 0
                strict = c.kind == "gate" or (c.mods and c.mods[0] in plan["after_gate"])
                for s in range(start, c.n):
                    lo(c, s)
                    at(s)
                    until = total * (s - start + 1) // (c.n - start)
                    for m in range(done, until):
                        q = c.mods[m // 8]
                        mod_slab(q, m % 8, 0 if c.kind == "gate" else q % 2, strict)
                    done = until

            def mod_out(q):
                dve.wait_ge(mod_mm, q + 1)
                dve.tensor_tensor(mod_cols[:, q + START_CHUNKS, :], bank[B_COL][:, 0:4],
                                  bias_cols[:, q + START_CHUNKS, :], ALU.add).then_inc(mod_col_done, 1)

            def mods_at(c, prev, s):
                if s == 4 and prev is not None and prev.mods:
                    mod_out(prev.mods[-1])
                if s == 7 and c is not None and len(c.mods) == 2:
                    mod_out(c.mods[0])

            even_in, even_out = plan["even_in"], plan["even_out"]
            ctx_scale = ctx_cols[:, ND:2 * ND, :].rearrange("p n j -> p (n j)")
            ctx_shift = ctx_cols[:, 0:ND, :].rearrange("p n j -> p (n j)")
            start_shifts = (mod_vec(0, 0), ctx_shift)

            def start_cols(m):
                n = start_col_chunk(m)
                both = bank[B_COL][:, 0:8].rearrange("p (j v) -> p j v", v=2)
                dve.wait_ge(row_mm, m + 1)
                dve.tensor_tensor(mod_cols[:, n, :], both[:, :, 0], bias_cols[:, n, :], ALU.add)
                dve.tensor_tensor(ctx_cols[:, n, :], both[:, :, 1], bias_cols[:, n, :], ALU.add) \
                   .then_inc(start_col, 1)

            def start_part(m):
                if m == 0:
                    dve.wait_ge(silu_ready, 2)
                for s in range(START_DVE):
                    dve.wait_ge(start_full[s], (m + 1) * 16)
                    for j in range(SLAB_K):
                        for v in range(2):
                            k = SLAB_K * s + j
                            w, c_k = start_raw[s][:, j, :], silu_c[:, k, v:v + 1]
                            if k == 0:
                                dve.tensor_scalar(part[v], w, c_k, None, ALU.mult).then_inc(part_step, 1)
                            else:
                                dve.wait_ge(part_step, PART * m + 2 * k + v - 1)
                                dve.scalar_tensor_tensor(out=part[v], in0=w, scalar=c_k, in1=part[v],
                                                         op0=ALU.mult, op1=ALU.add).then_inc(part_step, 1)

            dve.wait_ge(cols_ready, 5)
            start_part(0)
            for i in range(ND):
                start_cols(2 * i)
                start_part(2 * i + 1)
                if i == 0:
                    for which in range(2):
                        for t in range(NT):
                            stream_rms(which, t, 8 * which + 4 * (t + 1))
                else:
                    lo(even_in[0], 2 * i)
                start_cols(2 * i + 1)
                dve.wait_ge(start_col, 2 * i + 2)
                for which, scale in ((0, mod_vec(0, 1)), (1, ctx_scale)):
                    scale_col(which, norm_w(0, 0), scale, slice(4 * i, 4 * i + 4))
                norm_step(start_groups(i)[0], start_shifts)
                if i == 0:
                    lo(even_in[0], 0)
                lo(even_in[0], 2 * i + 1)
                if i < ND - 1:
                    start_part(2 * i + 2)
                norm_step(start_groups(i)[1], start_shifts)

            def halves(ap):
                return ap.rearrange("p (b h q) -> p b h q", b=2, h=2)

            def heads(ap):
                return ap.rearrange("p (h d) -> p h d", h=4)

            def fold_tables():
                dve.wait_ge(rope_in, 64)
                for a in range(2):
                    g = head_g[:, a, :]
                    for t in range(NT):
                        dve.tensor_tensor(fold[:, 2 * a, t, :], rope_raw[:, 0, t, :], g, ALU.mult)
                        for h in range(2):
                            op = dve.tensor_tensor(halves(fold[:, 2 * a + 1, t, :])[:, :, h, :],
                                                   halves(rope_raw[:, 1, t, :])[:, :, h, :],
                                                   halves(g)[:, :, 1 - h, :], ALU.mult)
                own(op)

            def head_rms(i):
                own(dve.tensor_scalar(head_ms[:, :, :], head_sq[:, i:i + 2, :], 1.0 / HD, EPS, ALU.mult,
                                      ALU.add))
                own_wait()
                rsqrt(head_r[:, :, :].rearrange("p t h -> p (t h)"),
                      head_ms[:, :, :].rearrange("p t h -> p (t h)"), 2 * 4)

            def head_norm(src, t):
                own(dve.tensor_tensor(heads(src), heads(src),
                                      head_r[:, t, :].unsqueeze(2).broadcast_to([P, 4, HD]), ALU.mult))
                own_wait()

            roped = 0

            def rope(src, t, a):
                nonlocal roped
                if roped:
                    dve.wait_ge(rope_done, roped)
                roped += 1
                cos = fold[:, 2 * a, t, :].unsqueeze(1).broadcast_to([P, 4, HD])
                own(dve.tensor_tensor(heads(rope_a), heads(src), cos, ALU.mult))
                quarters = "p (h b s q) -> p h b s q"
                sv = src.rearrange(quarters, h=4, b=2, s=2)
                bv = rope_b.rearrange(quarters, h=4, b=2, s=2)
                for s in range(2):
                    sin = halves(fold[:, 2 * a + 1, t, :])[:, :, s, :].unsqueeze(1).broadcast_to([P, 4, 2, 32])
                    own(dve.tensor_tensor(bv[:, :, :, s, :], sv[:, :, :, 1 - s, :], sin, ALU.mult))
                own_wait()
                return dve.tensor_tensor(src, rope_a, rope_b, ALU.add)

            def unit(i):
                if 0 <= i - 4 < 24:
                    u = i - 4
                    b = u % 2
                    dve.wait_ge(scores_done, u + 1)
                    own(dve.tensor_reduce(row_max[:, b:b + 1], bank[B_A][:, :], AX.X, ALU.max))
                    own_wait()
                    dve.tensor_scalar(neg_max[:, b:b + 1], row_max[:, b:b + 1], -SCALE, None, ALU.mult) \
                       .then_inc(max_done, 1)
                if 0 <= i - 7 < 24:
                    u = i - 7
                    dve.wait_ge(mix_hi, u + 1)
                    h, t = 4 * (u // 8) + u % 4, (u // 4) % 2
                    dve.tensor_tensor(m_lo[:, h, t * P:(t + 1) * P], bank[B_C][:, 0:P],
                                      m_hi[:, h, t * P:(t + 1) * P].bitcast(f32), ALU.subtract) \
                       .then_inc(mix_lo, 1)
                if 0 <= i - 4 < 24:
                    dve.wait_ge(exp_done, (i - 4) + 1)
                    b = (i - 4) % 2
                    own(dve.reciprocal(p_inv[:, b:b + 1], p_sum[:, b:b + 1]))
                    own_wait()
                    dve.tensor_scalar(probs[:, b, :], probs[:, b, :], p_inv[:, b:b + 1], None, ALU.mult) \
                       .then_inc(probs_done, 1)

            def even_at(n, prev, s):
                nonlocal roped
                if n == 1 and s == 0:
                    fold_tables()
                mods_at(plan["even_in"][n], prev, s)
                if n == 1:
                    if s == 0:
                        dve.wait_ge(slab_free, prev.w0 + prev.n)
                        dve.tensor_copy(k_tmp[:, 2, :], bank[2][:, :])
                        dve.tensor_copy(k_tmp[:, 3, :], bank[3][:, :]).then_inc(pair_freed[1], 1)
                    if s >= 4:
                        i = s - 4
                        if i % 2 == 0:
                            dve.wait_ge(head_sums, i + 2)
                            head_rms(i)
                        head_norm(k_tmp[:, i, :], i % 2)
                        if i < NT:
                            rope(k_tmp[:, i, :], i, 1).then_inc(rope_done, 1)
                        else:
                            g = head_g[:, 1, :].unsqueeze(1).broadcast_to([P, 4, HD])
                            dve.tensor_tensor(heads(k_tmp[:, i, :]), heads(k_tmp[:, i, :]), g, ALU.mult) \
                               .then_inc(rope_done, 1)
                            roped = i + 1
                if n == 2 and s == 3:
                    dve.wait_ge(slab_free, prev.w0 + prev.n)
                    dve.tensor_copy(v_sb[:, 0, :], bank[2][:, :])
                    dve.tensor_copy(v_sb[:, 1, :], bank[3][:, :]).then_inc(pair_freed[1], 1)
                if n >= 3 and s in (4, 6):
                    c, t = n - 3, (s - 4) // 2
                    if t == 0:
                        dve.wait_ge(head_sums, 4 + 2 * c + 2)
                        head_rms(0)
                    head_norm(q_tmp[:, t, :], t)
                    rope(q_tmp[:, t, :], t, 0).then_inc(rope_done, 1)
                if n >= 4:
                    unit(8 * (n - 4) + s)

            prev = even_in[0]
            for n, c in enumerate(even_in[1:], 1):
                chunk(c, lambda s: even_at(n, prev, s))
                prev = c
            rest = plan["rest_mods"]
            for i in range(16, 32):
                if i < 16 + RING:
                    lo(even_out[0], i - 16)
                mods_at(None, prev, i - 16)
                unit(i)
                if i in (27, 31):
                    mod_out(rest[(i - 27) // 4])
                for m in range(24 * (i - 16) // 16, 24 * (i - 15) // 16):
                    mod_slab(rest[m // 8], m % 8, rest[m // 8] % 2, False)
            for g in range(4):
                dve.wait_ge(mix_hi, 24 + 2 * (g // 2) + 2)
                dve.scalar_tensor_tensor(out=m_lo[:, N_HEADS + g, :],
                                         in0=bank[2 + g // 2][:, (g % 2) * T:(g % 2 + 1) * T],
                                         scalar=pscale_cols[:, g:g + 1],
                                         in1=m_hi[:, N_HEADS + g, :].bitcast(f32),
                                         op0=ALU.mult, op1=ALU.subtract).then_inc(mix_lo, 1)
            gates_used = 0

            def residual(prev, tiles=(0, 1)):
                nonlocal gates_used
                if res_no[prev.g] > 1:
                    dve.wait_ge(res_step, 2 * (res_no[prev.g] - 1))
                cols = slice(prev.idx * NC, (prev.idx + 1) * NC)
                if tiles == (0,):
                    dve.wait_ge(tile0_done, last_chunks[prev.g])
                else:
                    dve.wait_ge(slab_free, prev.w0 + prev.n)
                if "gate" in prev.extra and 0 in tiles:
                    gates_used += 1
                    dve.wait_ge(gb_in, gates_used)
                for t in tiles:
                    op = dve.tensor_tensor(res_tmp[:, t, :], bank[2 * prev.pair + t][:, :], gate_bc[:, cols],
                                           ALU.mult)
                if tiles == (0,):
                    own(op)
                    own_wait()
                else:
                    op.then_inc(pair_freed[prev.pair], 1)
                    dve.wait_ge(pair_freed[prev.pair], prev.use + 1)
                for t in tiles:
                    dve.tensor_tensor(x_tok[:, t, cols], x_tok[:, t, cols], res_tmp[:, t, :], ALU.add) \
                       .then_inc(res_step, 1)

            def res_phase(chunks, first_at, start):
                prev = None
                for c in chunks:
                    def at(s, prev=prev):
                        if prev is None:
                            first_at(s)
                        else:
                            mods_at(c, prev, s)
                            if s == 3:
                                residual(prev)
                    chunk(c, at, start if prev is None else 0)
                    prev = c
                return prev

            def turn_over(prev, nxt, k, norm_weight, scale, shift):
                e = norm_groups(k)
                residual(prev, (0,))
                mods_at(None, prev, 4)
                if prev.mods:
                    dve.wait_ge(mod_col_done, prev.mods[-1] + 1)
                scale_col(0, norm_weight, scale)
                stream_rms(0, 0, 16 + 8 * (k - 1) + 7)
                lo(nxt, 0)
                norm_modulated(e[0], shift)
                norm_modulated(e[1], shift)
                residual(prev, (1,))
                lo(nxt, 1)
                lo(nxt, 2)
                stream_rms(0, 1, 16 + 8 * k)
                lo(nxt, 3)
                norm_step(e[2:4], (shift,))

            def first_out(s):
                if s == 4:
                    mod_out(rest[2])
                if s == 7:
                    dve.wait_ge(x_again, 16)

            prev = res_phase(even_out, first_out, RING)
            turn_over(prev, plan["ffn0"][0][0][0][0], 1, norm_w(0, 1), mod_vec(0, 4), mod_vec(0, 3))

            def hid_lo_half(h, i):
                for t in range(NT):
                    dve.wait_ge(hid_hi, 2 * h + t + 1)
                    rng = (slice(None), slice(None), slice(t * P, (t + 1) * P))
                    hi_ = m_hi[rng].rearrange("p (c k) q -> p c k q", k=4)[:, i, :, :].bitcast(f32)
                    lo_ = m_lo[rng].rearrange("p (c k) q -> p c k q", k=4)[:, i, :, :]
                    dve.tensor_tensor(lo_, bank[B_A + t][:, :].rearrange("p (k q) -> p k q", k=4), hi_,
                                      ALU.subtract).then_inc(hid_lo, 1)

            def ffn(layer, k):
                shifts = (mod_vec(layer, 3),)
                prev, start = None, RING
                for gu, down in plan[f"ffn{layer}"]:
                    def hidden(prev, gate_use, s):
                        if s == 3:
                            dve.wait_ge(slab_free, prev.w0 + prev.n)
                            dve.wait_ge(pair_freed[0], gate_use + 1)
                            for t in range(NT):
                                op = dve.tensor_tensor(hid_tok[:, t, :], silu_g[:, t, :],
                                                       bank[2 + t][:, :], ALU.mult)
                            op.then_inc(pair_freed[1], 1)
                        if s == 5:
                            hid_lo_half(prev.extra, prev.idx)

                    def gate_up(gate, up, was, start=0):
                        def gate_at(s):
                            if start and s >= 4:
                                norm_step([norm_groups(k)[s]], shifts)
                            if was is None:
                                return
                            if was.kind == "up":
                                hidden(was, gate.use - 1, s)
                            elif s == 3:
                                residual(was)
                        chunk(gate, gate_at, start)
                        chunk(up, lambda s: mods_at(None, gate, s))

                    gate_up(gu[0][0], gu[0][1], prev, start)
                    start = 0
                    with dve.Fori(0, len(gu) - 1) as i:
                        gate_up(*loop_chunks(gu, i))
                    last_gate, last_up = gu[-1]
                    prev = res_phase(down, lambda s: hidden(last_up, last_gate.use, s), 0)
                return prev

            prev = ffn(0, 1)
            turn_over(prev, plan["odd_in"][0], 2, norm_w(1, 0), mod_vec(1, 1), mod_vec(1, 0))

            def odd_at(n, prev, s):
                mods_at(plan["odd_in"][n] if n < 8 else None, prev, s)
                if n == 0 and s >= 4:
                    norm_step([norm_groups(2)[s]], (mod_vec(1, 0),))
                i = 8 * (n - 2) + s
                if i >= 4 and i % 4 == 0 and i // 4 - 1 < 4:
                    g = i // 4 - 1
                    dve.wait_ge(dft_a, 2 * g + 2)
                    if g > 0:
                        dve.wait_ge(dft_y, g)
                    dve.wait_ge(dft_a_in, 2 * g + 1)
                    dve.tensor_copy(dft1[:, 1, :], bank[B_B][:, :]).then_inc(dft_a_in, 1)
                if i >= 6 and (i - 6) % 4 == 0 and (i - 6) // 4 < 4:
                    g = (i - 6) // 4
                    dve.wait_ge(mix_hi, EVEN_MIX + g + 1)
                    dve.tensor_tensor(m_lo[:, 2 * g:2 * g + 2, :],
                                      bank[B_C][:, :].rearrange("p (o t) -> p o t", o=2),
                                      m_hi[:, 2 * g:2 * g + 2, :].bitcast(f32), ALU.subtract) \
                       .then_inc(mix_lo, 1)
                if prev is None:
                    return
                half = prev.idx
                if prev.kind == "xin" and s == 3:
                    dve.wait_ge(slab_free, prev.w0 + prev.n)
                    cg = plan["odd_in"][n - 2]
                    dve.wait_ge(pair_freed[cg.pair], cg.use + 1)
                    for t in range(NT):
                        op = dve.tensor_tensor(odd_tmp[:, t, :], odd_tmp[:, t, :],
                                               bank[2 * prev.pair + t][:, :], ALU.mult)
                    op.then_inc(pair_freed[prev.pair], 1)
                if n < 8 and plan["odd_in"][n].kind == "bg" and s == 6:
                    conv(plan["odd_in"][n].idx)
                if prev.kind == "bg" and s == 5:
                    for b in range(2):
                        dve.wait_ge(bg_t, 2 * half + b + 1)
                        op = dve.tensor_tensor(y_conv[:, 2 * b:2 * b + 2, :], y_conv[:, 2 * b:2 * b + 2, :],
                                               bank[B_A + b][:, :].rearrange("p (j t) -> p j t", j=2),
                                               ALU.mult)
                        op.then_inc(mixed, 1)
                if prev.kind == "bg" and s == 6:
                    for ct in range(4):
                        dve.wait_ge(mix_hi, EVEN_MIX + DFT_MIX + 4 * half + ct + 1)
                        m = 8 + 4 * half + ct
                        dve.tensor_tensor(m_lo[:, m, :], y_conv[:, ct, :], m_hi[:, m, :].bitcast(f32),
                                          ALU.subtract).then_inc(mix_lo, 1)

            def conv(half):
                for ct in range(4):
                    if ct % 2 == 0:
                        dve.wait_ge(u_conv_t, 2 * half + ct // 2 + 1)
                    u = bank[B_A + ct // 2][:, (ct % 2) * T:(ct % 2 + 1) * T]
                    y = y_conv[:, ct, :]
                    k = 4 * half + ct
                    w = [conv_cols[:, 8 * j + k:8 * j + k + 1] for j in range(3)]
                    own(dve.tensor_scalar(y, u, w[1], None, ALU.mult))
                    own_wait()
                    own(dve.scalar_tensor_tensor(out=y[:, 1:T], in0=u[:, 0:T - 1], scalar=w[0],
                                                 in1=y[:, 1:T], op0=ALU.mult, op1=ALU.add))
                    own_wait()
                    dve.scalar_tensor_tensor(out=y[:, 0:T - 1], in0=u[:, 1:T], scalar=w[2],
                                             in1=y[:, 0:T - 1], op0=ALU.mult, op1=ALU.add) \
                       .then_inc(conv_done, 1)
                dve.wait_ge(conv_done, 4 * half + 4)

            prev = None
            for n, c in enumerate(plan["odd_in"]):
                chunk(c, lambda s: odd_at(n, prev, s), RING if n == 0 else 0)
                prev = c
            prev = res_phase(plan["odd_out"], lambda s: odd_at(8, plan["odd_in"][-1], s), 0)
            turn_over(prev, plan["ffn1"][0][0][0][0], 3, norm_w(1, 1), mod_vec(1, 4), mod_vec(1, 3))
            prev = ffn(1, 3)
            for t in range(NT):
                residual(prev, (t,))
                stream_rms(0, t, 16 + 8 * 3 + 7 + t)
                dve.wait_ge(fin_in, 16)
                dve.wait_ge(rms_ready, 4 + 2 * 3 + t + 1)
                for half in range(2):
                    cols = slice(half * D // 2, (half + 1) * D // 2)
                    dve.scalar_tensor_tensor(out=x_tok[:, t, cols], in0=x_tok[:, t, cols],
                                             scalar=rms[:, 0, t:t + 1], in1=final_g[:, cols],
                                             op0=ALU.mult, op1=ALU.mult).then_inc(x_final, 1)


def tables():
    f = np.float32
    quarter = HD // 4
    grid_w = 64
    freqs = f(10000.0) ** (-np.arange(quarter, dtype=f) / f(quarter))
    pos = np.arange(T)
    ang = np.stack([(pos // grid_w).astype(f)[:, None] * freqs, (pos % grid_w).astype(f)[:, None] * freqs], 1)
    cos, sin = np.cos(ang).astype(f), np.sin(ang).astype(f)
    rope_cos = np.stack([cos, cos], 2).reshape(T, HD)
    rope_sin = np.stack([-sin, sin], 2).reshape(T, HD)
    pool = np.zeros((4, T, T), f)
    for g, w in enumerate((2, 4, 8, 16)):
        for t in range(T):
            lo, hi = max(t - w // 2, 0), min(t - w // 2 + w, T)
            pool[g, lo:hi, t] = f(1) / f(hi - lo)
            pool[g, t, t] -= f(1)
    a = 2 * np.pi * ((np.arange(T)[:, None] * np.arange(T)[None, :]) % T) / T
    c, s = np.cos(a) / 16, np.sin(a) / 16
    dft = np.concatenate([c, s, -s], 1).astype(f)
    return {"rope_cos": rope_cos, "rope_sin": rope_sin, "pool_mat": pool, "dft": dft}


_INS = ["x", "c", "ctx", "c_ctx", "norm_g", "w_mod", "b_mod", "w_in_even", "w_out_even", "q_norm_g",
        "k_norm_g", "w_pool", "pool_scale", "w_in_odd", "w_out_odd", "conv_w", "w_ffn_gate", "w_ffn_up",
        "w_ffn_down", "final_g"]


def kernel(**inputs):
    import concourse.bacc as bacc
    from concourse.bass_utils import run_bass_kernel_spmd

    nc = bacc.Bacc("TRN2", target_bir_lowering=False, num_devices=1)
    given = {n: np.ascontiguousarray(inputs[n]) for n in _INS}
    given.update(tables())
    arrays, args = {}, []
    for name, a in given.items():
        arrays[f"in_{name}"] = a
        args.append(nc.dram_tensor(f"in_{name}", a.shape, mybir.dt.from_np(a.dtype), kind="ExternalInput").ap())
    args.append(nc.dram_tensor("out_0", (1, T, D), mybir.dt.float32, kind="ExternalOutput").ap())
    build(nc, *args)
    r = run_bass_kernel_spmd(nc, [arrays], core_ids=[0])
    return r.results[0]["out_0"]
```
